# Optimizing a Trainium2 kernel written in Bass

```python
import math
import jax, jax.numpy as jnp
from jax import lax
import numpy as np

D_MODEL = 1024
BATCH = 1
SEQ = 256
DEPTH = 1

CHUNK = 64
Q_BLOCK = 128
MEM_LEN = 256
EPS = 1e-6

DA_HEADS = 4
DA_QK_DIM = D_MODEL // 16
DA_V_DIM = 2 * DA_QK_DIM
DA_QK_COLS = DA_HEADS * 2 * DA_QK_DIM
DA_WIDTH = DA_HEADS * DA_V_DIM

GLA_HEADS = 4
GLA_K_DIM = D_MODEL // 16
GLA_V_DIM = D_MODEL // 8
GLA_QK_COLS = GLA_HEADS * GLA_K_DIM
GLA_WIDTH = GLA_HEADS * GLA_V_DIM
GLA_GATE_RANK = 16
GLA_TAU = 16.0

MIX_WIDTH = DA_WIDTH + GLA_WIDTH
IN_WIDTH = 2 * DA_QK_COLS + DA_WIDTH + 2 * GLA_QK_COLS + 2 * GLA_WIDTH + GLA_GATE_RANK

CROSS_HEADS = 4
CROSS_DIM = D_MODEL // CROSS_HEADS

N_GROUPS = 4
EXPERTS_PER_GROUP = 8
N_EXPERTS = N_GROUPS * EXPERTS_PER_GROUP
TOP_K = 2
D_EXPERT = D_MODEL // 2
EXPERT_BLOCK = 128


def _rmsnorm(t, g):
    tf = t.astype(jnp.float32)
    tf = tf * lax.rsqrt(jnp.mean(tf * tf, axis=-1, keepdims=True) + EPS)
    return (tf * g.astype(jnp.float32)).astype(t.dtype)

def _split_heads(t, n):
    b, s, _ = t.shape
    return t.reshape(b, s, n, -1).transpose(0, 2, 1, 3)

def _merge_heads(t):
    b, h, s, d = t.shape
    return t.transpose(0, 2, 1, 3).reshape(b, s, h * d)

def _diff_attention(q1, q2, k1, k2, v, lam):
    b, h, s, d = q1.shape
    n_blocks = s // Q_BLOCK
    scale = d ** -0.5
    key_chunk = jnp.arange(s) // CHUNK

    def to_blocks(t):
        return t.reshape(b, h, n_blocks, Q_BLOCK, d).transpose(2, 0, 1, 3, 4)

    def one_block(args):
        qb1, qb2, bi = args
        q_chunk = (bi * Q_BLOCK + jnp.arange(Q_BLOCK)) // CHUNK
        mask = key_chunk[None, :] <= q_chunk[:, None]

        def probs(qb, kk):
            sc = jnp.einsum('bhqd,bhkd->bhqk', qb, kk).astype(jnp.float32) * scale
            return jax.nn.softmax(jnp.where(mask, sc, -jnp.inf), axis=-1)

        p = probs(qb1, k1) - lam * probs(qb2, k2)
        return jnp.einsum('bhqk,bhkv->bhqv', p.astype(v.dtype), v)

    o = lax.map(one_block, (to_blocks(q1), to_blocks(q2), jnp.arange(n_blocks)))
    return o.transpose(1, 2, 0, 3, 4).reshape(b, h, s, v.shape[-1])

def _gla_chunked(q, k, v, log_a):
    b, h, s, dk = q.shape
    dv = v.shape[-1]
    nc = s // CHUNK
    q = q.reshape(b, h, nc, CHUNK, dk)
    k = k.reshape(b, h, nc, CHUNK, dk)
    v = v.reshape(b, h, nc, CHUNK, dv)
    L = jnp.cumsum(log_a.reshape(b, h, nc, CHUNK, dk), axis=3)
    L_end = L[:, :, :, -1, :]
    Lc = L - L[:, :, :, CHUNK // 2 - 1:CHUNK // 2, :]
    e_pos, e_neg = jnp.exp(Lc), jnp.exp(-Lc)
    a_past = jnp.einsum('bhnid,bhnjd->bhnij', q * e_pos, k * e_neg)
    a_fut = jnp.einsum('bhnid,bhnjd->bhnij', q * e_neg, k * e_pos)
    lower = jnp.tril(jnp.ones((CHUNK, CHUNK), dtype=bool))
    a = jnp.where(lower, a_past, a_fut)
    o_intra = jnp.einsum('bhnij,bhnjv->bhniv', a, v)
    u = jnp.einsum('bhnjd,bhnjv->bhndv', k * jnp.exp(L_end[:, :, :, None, :] - L), v)
    decay = jnp.exp(L_end)

    def step(state, inp):
        d_c, u_c = inp
        return state * d_c[..., None] + u_c, state

    _, s_prev = lax.scan(step, jnp.zeros((b, h, dk, dv), jnp.float32),
                         (jnp.moveaxis(decay, 2, 0), jnp.moveaxis(u, 2, 0)))
    s_prev = jnp.moveaxis(s_prev, 0, 2)
    o_inter = jnp.einsum('bhnid,bhndv->bhniv', q * jnp.exp(L), s_prev)
    return (o_intra + o_inter).reshape(b, h, s, dv)

def _mixer(h, norm_g, w_in, da_qn, da_kn, lq1, lk1, lq2, lk2, da_on, gate_w, gate_b, gla_on, w_o, lam_init):
    b, s, _ = h.shape
    f32 = jnp.float32
    u = _rmsnorm(h, norm_g)
    p = u @ w_in
    widths = (DA_QK_COLS, DA_QK_COLS, DA_WIDTH, GLA_QK_COLS, GLA_QK_COLS, GLA_WIDTH, GLA_WIDTH, GLA_GATE_RANK)
    parts = []
    off = 0
    for w in widths:
        parts.append(p[..., off:off + w])
        off += w
    dq, dk, dv, gq, gk, gv, gg, gr = parts

    dq = dq.reshape(b, s, DA_HEADS, 2, DA_QK_DIM).transpose(0, 2, 3, 1, 4)
    dk = dk.reshape(b, s, DA_HEADS, 2, DA_QK_DIM).transpose(0, 2, 3, 1, 4)
    dq = _rmsnorm(dq, da_qn)
    dk = _rmsnorm(dk, da_kn)
    dvh = _split_heads(dv, DA_HEADS)
    lam = (jnp.exp(jnp.sum(lq1.astype(f32) * lk1.astype(f32)))
           - jnp.exp(jnp.sum(lq2.astype(f32) * lk2.astype(f32))) + lam_init)
    da = _diff_attention(dq[:, :, 0], dq[:, :, 1], dk[:, :, 0], dk[:, :, 1], dvh, lam)
    da = _rmsnorm(da, da_on) * (1.0 - lam_init)
    da_out = _merge_heads(da)

    qg = _split_heads(gq, GLA_HEADS).astype(f32) * (GLA_K_DIM ** -0.5)
    kg = _split_heads(gk, GLA_HEADS).astype(f32)
    vg = _split_heads(gv, GLA_HEADS).astype(f32)
    z = gr.astype(f32) @ gate_w.astype(f32) + gate_b.astype(f32)
    log_a = _split_heads(jax.nn.log_sigmoid(z) / GLA_TAU, GLA_HEADS)
    og = _gla_chunked(qg, kg, vg, log_a)
    og = _rmsnorm(og, gla_on)
    gla_out = (_merge_heads(og) * jax.nn.silu(gg.astype(f32))).astype(h.dtype)

    return jnp.concatenate([da_out.astype(h.dtype), gla_out], axis=-1) @ w_o

def _cross_attention(h, mem, norm_g, norm_m, w_q, w_kv, qn, kn, w_out):
    b, s, d = h.shape
    m = mem.shape[1]
    u = _rmsnorm(h, norm_g)
    mn = _rmsnorm(mem, norm_m)
    q = _rmsnorm((u @ w_q).reshape(b, s, CROSS_HEADS, CROSS_DIM), qn)
    kv = mn @ w_kv
    k = _rmsnorm(kv[..., :d].reshape(b, m, CROSS_HEADS, CROSS_DIM), kn)
    v = kv[..., d:].reshape(b, m, CROSS_HEADS, CROSS_DIM)
    sc = jnp.einsum('bshd,bmhd->bhsm', q, k).astype(jnp.float32) * (CROSS_DIM ** -0.5)
    pr = jax.nn.softmax(sc, axis=-1).astype(v.dtype)
    o = jnp.einsum('bhsm,bmhd->bshd', pr, v).reshape(b, s, d)
    return o @ w_out

def _hier_moe(h, norm_g, w_group, b_group, w_expert, b_expert, w_gate, w_up, w_down):
    b, s, d = h.shape
    t = b * s
    f32 = jnp.float32
    xf = _rmsnorm(h, norm_g).reshape(t, d)
    xr = xf.astype(f32)
    p_group = jax.nn.softmax(xr @ w_group.astype(f32) + b_group.astype(f32), axis=-1)
    g_sel = jnp.argmax(p_group, axis=-1)
    p_g = jnp.take_along_axis(p_group, g_sel[:, None], axis=-1)
    e_logits = (xr @ w_expert.astype(f32) + b_expert.astype(f32)).reshape(t, N_GROUPS, EXPERTS_PER_GROUP)
    e_logits = jnp.take_along_axis(e_logits, g_sel[:, None, None], axis=1)[:, 0]
    top_p, top_i = lax.top_k(jax.nn.softmax(e_logits, axis=-1), TOP_K)
    gate = p_g * top_p / jnp.sum(top_p, axis=-1, keepdims=True)
    flat_id = (g_sel[:, None] * EXPERTS_PER_GROUP + top_i).reshape(-1).astype(jnp.int32)
    flat_gate = gate.reshape(-1)
    n_assign = t * TOP_K
    order = jnp.argsort(flat_id)
    sorted_id = flat_id[order]
    token_of = order // TOP_K
    sizes = jnp.bincount(flat_id, length=N_EXPERTS)
    padded = (sizes + EXPERT_BLOCK - 1) // EXPERT_BLOCK * EXPERT_BLOCK
    start = jnp.cumsum(sizes) - sizes
    padded_end = jnp.cumsum(padded)
    padded_start = padded_end - padded
    dest = padded_start[sorted_id] + jnp.arange(n_assign) - start[sorted_id]
    n_rows = n_assign + N_EXPERTS * EXPERT_BLOCK
    n_blocks = n_rows // EXPERT_BLOCK
    x_pad = jnp.zeros((n_rows, d), xf.dtype).at[dest].set(xf[token_of])
    block_expert = jnp.minimum(
        jnp.searchsorted(padded_end, jnp.arange(n_blocks) * EXPERT_BLOCK, side='right'), N_EXPERTS - 1)

    def expert_block(args):
        xb, e = args
        hid = jax.nn.silu(xb @ w_gate[e]) * (xb @ w_up[e])
        return hid @ w_down[e]

    out_pad = lax.map(expert_block, (x_pad.reshape(n_blocks, EXPERT_BLOCK, d), block_expert)).reshape(n_rows, d)
    out = out_pad[dest] * flat_gate[order][:, None].astype(out_pad.dtype)
    y = jnp.zeros((t, d), out.dtype).at[token_of].add(out)
    return y.reshape(b, s, d).astype(h.dtype)

def first_inputs(seed: int = 0) -> dict:
    key = jax.random.key(seed)
    ks = iter(jax.random.split(key, 40))
    f32 = jnp.float32
    D = D_MODEL

    def nrm(shape, scale):
        return scale * jax.random.normal(next(ks), shape, f32)

    def gain(n):
        return 1.0 + 0.02 * jax.random.normal(next(ks), (DEPTH, n), f32)

    return {
        'x': nrm((BATCH, SEQ, D), 1.0),
        'mem': nrm((BATCH, MEM_LEN, D), 1.0),
        'norm_mix': gain(D),
        'w_in': nrm((DEPTH, D, IN_WIDTH), D ** -0.5),
        'da_q_norm': gain(DA_QK_DIM),
        'da_k_norm': gain(DA_QK_DIM),
        'lambda_q1': nrm((DEPTH, DA_QK_DIM), 0.1),
        'lambda_k1': nrm((DEPTH, DA_QK_DIM), 0.1),
        'lambda_q2': nrm((DEPTH, DA_QK_DIM), 0.1),
        'lambda_k2': nrm((DEPTH, DA_QK_DIM), 0.1),
        'da_out_norm': gain(DA_V_DIM),
        'gla_gate_w': nrm((DEPTH, GLA_GATE_RANK, GLA_QK_COLS), GLA_GATE_RANK ** -0.5),
        'gla_gate_b': nrm((DEPTH, GLA_QK_COLS), 0.1),
        'gla_out_norm': gain(GLA_V_DIM),
        'w_o': nrm((DEPTH, MIX_WIDTH, D), MIX_WIDTH ** -0.5),
        'norm_cross': gain(D),
        'norm_mem': gain(D),
        'w_cq': nrm((DEPTH, D, D), D ** -0.5),
        'w_ckv': nrm((DEPTH, D, 2 * D), D ** -0.5),
        'cross_q_norm': gain(CROSS_DIM),
        'cross_k_norm': gain(CROSS_DIM),
        'w_co': nrm((DEPTH, D, D), D ** -0.5),
        'norm_ffn': gain(D),
        'w_group': nrm((DEPTH, D, N_GROUPS), D ** -0.5),
        'b_group': nrm((DEPTH, N_GROUPS), 0.01),
        'w_expert': nrm((DEPTH, D, N_EXPERTS), D ** -0.5),
        'b_expert': nrm((DEPTH, N_EXPERTS), 0.01),
        'w_e_gate': nrm((DEPTH, N_EXPERTS, D, D_EXPERT), D ** -0.5),
        'w_e_up': nrm((DEPTH, N_EXPERTS, D, D_EXPERT), D ** -0.5),
        'w_e_down': nrm((DEPTH, N_EXPERTS, D_EXPERT, D), D_EXPERT ** -0.5),
    }

def first_block(x, mem, norm_mix, w_in, da_q_norm, da_k_norm, lambda_q1, lambda_k1, lambda_q2, lambda_k2,
              da_out_norm, gla_gate_w, gla_gate_b, gla_out_norm, w_o, norm_cross, norm_mem, w_cq, w_ckv,
              cross_q_norm, cross_k_norm, w_co, norm_ffn, w_group, b_group, w_expert, b_expert,
              w_e_gate, w_e_up, w_e_down):
    h = x
    for l in range(DEPTH):
        lam_init = 0.8 - 0.6 * math.exp(-0.3 * l)
        h = h + _mixer(h, norm_mix[l], w_in[l], da_q_norm[l], da_k_norm[l], lambda_q1[l], lambda_k1[l],
                       lambda_q2[l], lambda_k2[l], da_out_norm[l], gla_gate_w[l], gla_gate_b[l],
                       gla_out_norm[l], w_o[l], lam_init)
        h = h + _cross_attention(h, mem, norm_cross[l], norm_mem[l], w_cq[l], w_ckv[l],
                                 cross_q_norm[l], cross_k_norm[l], w_co[l])
        h = h + _hier_moe(h, norm_ffn[l], w_group[l], b_group[l], w_expert[l], b_expert[l],
                          w_e_gate[l], w_e_up[l], w_e_down[l])
    return h


HEAD_DIM = 64
MOBA_HEADS = 8
MOBA_BLOCK = 256
MOBA_TOPK = 3
MOBA_Q_CHUNK = 8
DSA_HEADS = 8
DSA_TOPK = 256
DSA_Q_CHUNK = 16
IDX_HEADS = 8
IDX_DIM = 64
X_HEADS = 4
X_HEAD_DIM = 128
ROPE_THETA = 10000.0
RMS_EPS = 1e-6
N_BRANCH = 3
MOBA_W = MOBA_HEADS * HEAD_DIM
DSA_W = DSA_HEADS * HEAD_DIM
X_W = X_HEADS * X_HEAD_DIM
IN_SIZES = (MOBA_W, MOBA_W, MOBA_W, MOBA_W, DSA_W, DSA_W, DSA_W, DSA_W,
            IDX_HEADS * IDX_DIM, IDX_DIM, IDX_HEADS, X_W, X_W, N_BRANCH * D_MODEL)
IN_WIDTH_2 = 4 * MOBA_W + 4 * DSA_W + IDX_HEADS * IDX_DIM + IDX_DIM + IDX_HEADS + 2 * X_W + N_BRANCH * D_MODEL


NEG_INF = -jnp.inf

def rmsnorm(x, g):
    xf = x.astype(jnp.float32)
    y = xf * lax.rsqrt(jnp.mean(xf * xf, axis=-1, keepdims=True) + RMS_EPS)
    return (y * g.astype(jnp.float32)).astype(x.dtype)

def rope(x, pos):
    d = x.shape[-1]
    half = d // 2
    inv = jnp.power(ROPE_THETA, -jnp.arange(half, dtype=jnp.float32) * 2.0 / d)
    ang = pos.astype(jnp.float32)[:, None] * inv[None, :]
    cos = jnp.cos(ang)[None, :, None, :]
    sin = jnp.sin(ang)[None, :, None, :]
    xf = x.astype(jnp.float32)
    x1, x2 = xf[..., :half], xf[..., half:]
    return jnp.concatenate([x1 * cos - x2 * sin, x2 * cos + x1 * sin], axis=-1).astype(x.dtype)

def moba_attention(q, k, v):
    B, S, H, D = q.shape
    nb = -(-S // MOBA_BLOCK)
    sp = nb * MOBA_BLOCK
    padw = ((0, 0), (0, sp - S), (0, 0), (0, 0))
    qp, kp, vp = jnp.pad(q, padw), jnp.pad(k, padw), jnp.pad(v, padw)
    scale = D ** -0.5
    kbh = kp.reshape(B, nb, MOBA_BLOCK, H, D).transpose(0, 3, 1, 2, 4)
    vbh = vp.reshape(B, nb, MOBA_BLOCK, H, D).transpose(0, 3, 1, 2, 4)
    kmean = jnp.mean(kbh.astype(jnp.float32), axis=3)
    gate = jnp.einsum('bshd,bhnd->bshn', qp.astype(jnp.float32), kmean)
    qblk = jnp.arange(sp) // MOBA_BLOCK
    past = jnp.arange(nb)[None, :] < qblk[:, None]
    gate = jnp.where(past[None, :, None, :], gate, NEG_INF)
    n_sel = max(min(MOBA_TOPK, nb - 1), 1)
    top_val, top_idx = lax.top_k(gate, n_sel)
    top_ok = jnp.isfinite(top_val)
    nc = sp // MOBA_Q_CHUNK
    b_ix = jnp.arange(B)[:, None, None, None]
    h_ix = jnp.arange(H)[None, None, :, None]

    def to_chunks(a):
        return a.reshape((B, nc, MOBA_Q_CHUNK) + a.shape[2:]).swapaxes(0, 1)

    def step(args):
        ci, q_c, idx_c, ok_c = args
        t0 = ci * MOBA_Q_CHUNK
        blk_start = (t0 // MOBA_BLOCK) * MOBA_BLOCK
        k_own = lax.dynamic_slice_in_dim(kp, blk_start, MOBA_BLOCK, axis=1)
        v_own = lax.dynamic_slice_in_dim(vp, blk_start, MOBA_BLOCK, axis=1)
        qpos = t0 + jnp.arange(MOBA_Q_CHUNK)
        kpos = blk_start + jnp.arange(MOBA_BLOCK)
        s_own = jnp.einsum('bqhd,bkhd->bhqk', q_c, k_own).astype(jnp.float32) * scale
        s_own = jnp.where((kpos[None, :] <= qpos[:, None])[None, None], s_own, NEG_INF)
        k_sel = kbh[b_ix, h_ix, idx_c]
        v_sel = vbh[b_ix, h_ix, idx_c]
        s_past = jnp.einsum('bqhd,bqhnkd->bhqnk', q_c, k_sel).astype(jnp.float32) * scale
        s_past = jnp.where(ok_c.transpose(0, 2, 1, 3)[..., None], s_past, NEG_INF)
        n_past = n_sel * MOBA_BLOCK
        s_all = jnp.concatenate([s_past.reshape(B, H, MOBA_Q_CHUNK, n_past), s_own], axis=-1)
        p = jax.nn.softmax(s_all, axis=-1).astype(q.dtype)
        p_past = p[..., :n_past].reshape(B, H, MOBA_Q_CHUNK, n_sel, MOBA_BLOCK)
        p_own = p[..., n_past:]
        return (jnp.einsum('bhqnk,bqhnkd->bqhd', p_past, v_sel)
                + jnp.einsum('bhqk,bkhd->bqhd', p_own, v_own))

    outs = lax.map(step, (jnp.arange(nc), to_chunks(qp), to_chunks(top_idx), to_chunks(top_ok)))
    return outs.swapaxes(0, 1).reshape(B, sp, H, D)[:, :S]

def dsa_attention(q, k, v, iq, ik, iw):
    B, S, H, D = q.shape
    k_top = min(DSA_TOPK, S // 4)
    nc = S // DSA_Q_CHUNK
    scale = D ** -0.5
    iscale = IDX_DIM ** -0.5
    wscale = IDX_HEADS ** -0.5
    b_ix = jnp.arange(B)[:, None, None]
    kpos = jnp.arange(S)

    def to_chunks(a):
        return a.reshape((B, nc, DSA_Q_CHUNK) + a.shape[2:]).swapaxes(0, 1)

    def step(args):
        ci, q_c, iq_c, iw_c = args
        qpos = ci * DSA_Q_CHUNK + jnp.arange(DSA_Q_CHUNK)
        logits = jnp.einsum('bqgd,bsd->bqgs', iq_c, ik).astype(jnp.float32) * iscale
        score = jnp.einsum('bqgs,bqg->bqs', jax.nn.relu(logits), iw_c.astype(jnp.float32) * wscale)
        score = jnp.where((kpos[None, :] <= qpos[:, None])[None], score, NEG_INF)
        top_val, top_idx = lax.top_k(score, k_top)
        ok = jnp.isfinite(top_val)
        k_sel = k[b_ix, top_idx]
        v_sel = v[b_ix, top_idx]
        s = jnp.einsum('bqhd,bqkhd->bhqk', q_c, k_sel).astype(jnp.float32) * scale
        s = jnp.where(ok[:, None], s, NEG_INF)
        p = jax.nn.softmax(s, axis=-1).astype(q.dtype)
        return jnp.einsum('bhqk,bqkhd->bqhd', p, v_sel)

    outs = lax.map(step, (jnp.arange(nc), to_chunks(q), to_chunks(iq), to_chunks(iw)))
    return outs.swapaxes(0, 1).reshape(B, S, H, D)

def cross_attention(q, mk, mv):
    scale = q.shape[-1] ** -0.5
    s = jnp.einsum('bshd,bmhd->bhsm', q, mk).astype(jnp.float32) * scale
    p = jax.nn.softmax(s, axis=-1).astype(q.dtype)
    return jnp.einsum('bhsm,bmhd->bshd', p, mv)

def hybrid_layer(x, mem, g_in, w_in, b_merge, g_mem, w_mem_kv, w_up_moba, w_up_dsa, w_up_cross, w_out):
    B, S, _ = x.shape
    pos = jnp.arange(S)
    h = rmsnorm(x, g_in)
    z = h @ w_in
    offs = np.cumsum(IN_SIZES)[:-1].tolist()
    (mq, mk, mv, mg, dq, dk, dv, dg, iq, ik, iw, xq, xg, glog) = jnp.split(z, offs, axis=-1)
    heads = lambda a, n, d: a.reshape(B, S, n, d)
    mq = rope(heads(mq, MOBA_HEADS, HEAD_DIM), pos)
    mk = rope(heads(mk, MOBA_HEADS, HEAD_DIM), pos)
    ya = moba_attention(mq, mk, heads(mv, MOBA_HEADS, HEAD_DIM)).reshape(B, S, MOBA_W)
    ya = (ya * jax.nn.silu(mg)) @ w_up_moba
    dq = rope(heads(dq, DSA_HEADS, HEAD_DIM), pos)
    dk = rope(heads(dk, DSA_HEADS, HEAD_DIM), pos)
    iq = rope(heads(iq, IDX_HEADS, IDX_DIM), pos)
    ik = rope(ik[:, :, None, :], pos)[:, :, 0, :]
    yb = dsa_attention(dq, dk, heads(dv, DSA_HEADS, HEAD_DIM), iq, ik, iw).reshape(B, S, DSA_W)
    yb = (yb * jax.nn.silu(dg)) @ w_up_dsa
    M = mem.shape[1]
    kv = rmsnorm(mem, g_mem) @ w_mem_kv
    xk = kv[..., :X_W].reshape(B, M, X_HEADS, X_HEAD_DIM)
    xv = kv[..., X_W:].reshape(B, M, X_HEADS, X_HEAD_DIM)
    yc = cross_attention(heads(xq, X_HEADS, X_HEAD_DIM), xk, xv).reshape(B, S, X_W)
    yc = (yc * jax.nn.silu(xg)) @ w_up_cross
    gates = jax.nn.sigmoid(glog + b_merge).reshape(B, S, N_BRANCH, D_MODEL)
    u = gates[:, :, 0] * ya + gates[:, :, 1] * yb + gates[:, :, 2] * yc
    return x + u @ w_out

def second_inputs(seed: int = 0) -> dict:
    key = jax.random.key(seed)
    ks = jax.random.split(key, 12)
    f32 = jnp.float32
    nrm = lambda k, shape, s: jax.random.normal(k, shape, f32) * s
    return {
        'x': nrm(ks[0], (BATCH, SEQ, D_MODEL), 1.0),
        'mem': nrm(ks[1], (BATCH, MEM_LEN, D_MODEL), 1.0),
        'g_in': 1.0 + nrm(ks[2], (DEPTH, D_MODEL), 0.02),
        'w_in': nrm(ks[3], (DEPTH, D_MODEL, IN_WIDTH_2), D_MODEL ** -0.5),
        'b_merge': nrm(ks[4], (DEPTH, N_BRANCH * D_MODEL), 0.1),
        'g_mem': 1.0 + nrm(ks[5], (DEPTH, D_MODEL), 0.02),
        'w_mem_kv': nrm(ks[6], (DEPTH, D_MODEL, 2 * X_W), D_MODEL ** -0.5),
        'w_up_moba': nrm(ks[7], (DEPTH, MOBA_W, D_MODEL), MOBA_W ** -0.5),
        'w_up_dsa': nrm(ks[8], (DEPTH, DSA_W, D_MODEL), DSA_W ** -0.5),
        'w_up_cross': nrm(ks[9], (DEPTH, X_W, D_MODEL), X_W ** -0.5),
        'w_out': nrm(ks[10], (DEPTH, D_MODEL, D_MODEL), D_MODEL ** -0.5),
        'g_final': 1.0 + nrm(ks[11], (D_MODEL,), 0.02),
    }

def second_block(x, mem, g_in, w_in, b_merge, g_mem, w_mem_kv, w_up_moba, w_up_dsa, w_up_cross, w_out, g_final):
    for l in range(DEPTH):
        x = hybrid_layer(x, mem, g_in[l], w_in[l], b_merge[l], g_mem[l], w_mem_kv[l],
                         w_up_moba[l], w_up_dsa[l], w_up_cross[l], w_out[l])
    return rmsnorm(x, g_final)


def setup_inputs(seed=0):
    out = dict(first_inputs(seed))
    for name, value in second_inputs(seed + 1).items():
        if name != "x":
            out[name + "_2"] = value
    return out


def reference(
    x, mem, norm_mix, w_in, da_q_norm, da_k_norm, lambda_q1, lambda_k1, lambda_q2, lambda_k2,
    da_out_norm, gla_gate_w, gla_gate_b, gla_out_norm, w_o, norm_cross, norm_mem, w_cq, w_ckv,
    cross_q_norm, cross_k_norm, w_co, norm_ffn, w_group, b_group, w_expert, b_expert, w_e_gate,
    w_e_up, w_e_down, mem_2, g_in_2, w_in_2, b_merge_2, g_mem_2, w_mem_kv_2, w_up_moba_2,
    w_up_dsa_2, w_up_cross_2, w_out_2, g_final_2,
):
    x = first_block(
        x, mem, norm_mix, w_in, da_q_norm, da_k_norm, lambda_q1, lambda_k1, lambda_q2,
        lambda_k2, da_out_norm, gla_gate_w, gla_gate_b, gla_out_norm, w_o, norm_cross, norm_mem,
        w_cq, w_ckv, cross_q_norm, cross_k_norm, w_co, norm_ffn, w_group, b_group, w_expert,
        b_expert, w_e_gate, w_e_up, w_e_down,
    )
    return second_block(
        x, mem_2, g_in_2, w_in_2, b_merge_2, g_mem_2, w_mem_kv_2, w_up_moba_2, w_up_dsa_2,
        w_up_cross_2, w_out_2, g_final_2,
    )


_drawn_inputs = setup_inputs


def setup_inputs(seed=0):
    import zlib

    import numpy as np

    out = dict(_drawn_inputs(seed))
    spreads = {}
    factors = {'da_q_norm': 3.73,
     'lambda_k2': 5.096,
     'da_out_norm': 2.812,
     'gla_gate_b': 3.104,
     'gla_out_norm': 3.799,
     'norm_cross': 8.0,
     'norm_mem': 8.0,
     'cross_q_norm': 8.0,
     'cross_k_norm': 6.621,
     'b_group': 8.0,
     'b_expert': 4.527,
     'g_in_2': 7.54,
     'b_merge_2': 8.0,
     'g_mem_2': 8.0,
     'g_final_2': 2.67}
    for name, (base, spread) in spreads.items():
        noise = np.random.default_rng([zlib.crc32(name.encode()), seed]).standard_normal(out[name].shape)
        drawn = base * np.exp(spread * noise) if base else spread * noise
        out[name] = __import__('jax').numpy.asarray(drawn.astype(out[name].dtype))
    for name, factor in factors.items():
        out[name] = (out[name] * factor).astype(out[name].dtype)
    return out
```

```python
from contextlib import ExitStack

import concourse.bass as bass
from concourse import mybir

F32 = mybir.dt.float32
BF16 = mybir.dt.bfloat16
I32 = mybir.dt.int32
U8 = mybir.dt.uint8
ALU = mybir.AluOpType
ACT = mybir.ActivationFunctionType
X = mybir.AxisListType.X

P = 128
T = 256
TT = T // P
D = 1024
KC = D // P
EPS = 1e-6
NEG = -1e30
BIG = 1e30

BLOCK_COLS = 512
SLOT = KC * BLOCK_COLS
RING = 6
DENSE_RING = 4

H1 = 4
DA_D = 64
DV = 128
GLA_CHUNK = 64
LAM_INIT = 0.2
GLA_TAU = 16.0
CROSS_D = 256

N_EXPERTS = 32
N_GROUPS = 4
PER_GROUP = N_EXPERTS // N_GROUPS
CAP = 64
PAIRS = N_EXPERTS // 2
MORE_ROUNDS = T // CAP - 1
F_EXP = 512
FC = F_EXP // P

H2 = 8
HD = 64
DSA_TOPK = 64
X2_HEADS = 4
X2_D = 128

FIRST_BLOCKS = ["gqk", "gv", "dq", "dk", "ck0", "ck1", "cv0", "cv1", "dv", "gg",
                "wo0", "wo1", "cq0", "cq1", "xk2", "xv2", "co0", "co1"]
SECOND_BLOCKS = ["iq", "dq2", "dk2", "dv2", "mq", "mk", "mv", "mg", "xq", "dg", "xg",
                 "gl0", "gl1", "gl2", "gl3", "gl4", "gl5", "up0", "up1", "up2", "out0", "out1"]

PSUM_PLAN = ["cols"]
PSUM_PLAN += [f"xT{c}" for c in range(4)]
PSUM_PLAN += ["grT", "gqk0", "gqk1", "z", "gv_0", "gv_1", "dq_0", "dq_1", "dk_0", "dk_1"]
PSUM_PLAN += [f"memT{c}" for c in range(4)]
PSUM_PLAN += ["kdT", "past0", "fut0", "past1", "fut1", "u01", "u2"]
PSUM_PLAN += ["ck0_0", "ck0_1", "ck1_0", "ck1_1"]
PSUM_PLAN += ["og0", "og1", "dqT0", "dqT1", "dkT0", "dkT1"]
PSUM_PLAN += ["cv0_0", "cv0_1", "cv1_0", "cv1_1", "ckT0", "ckT1", "ckT2", "ckT3", "dv_0", "dv_1"]
PSUM_PLAN += ["ds0_0", "ds1_0", "ds0_1", "ds1_1", "gg_0", "gg_1", "ds0_2", "ds1_2", "dpT0", "do0",
              "ds0_3", "ds1_3", "dpT1", "do1", "dpT2", "do2", "dpT3", "do3"]
PSUM_PLAN += [f"mixT{c}" for c in range(4)]
PSUM_PLAN += ["wo0_0", "wo0_1", "wo1_0", "wo1_1"]
PSUM_PLAN += [f"h1T{c}" for c in range(4)]
PSUM_PLAN += ["cq0_0", "cq0_1", "cq1_0", "cq1_1"]
PSUM_PLAN += [f"cqT{c}" for c in range(4)]
PSUM_PLAN += [f"mem2T{c}" for c in range(4)]
PSUM_PLAN += ["cs0_0", "cs1_0", "cs0_1", "cs1_1", "xk2_0", "cpT0", "co_0", "cpT1", "co_1", "cpT2", "co_2",
              "cpT3", "co_3"]
PSUM_PLAN += ["co0_0", "co0_1", "co1_0", "co1_1", "xk2_1"]
PSUM_PLAN += [f"h2T{c}" for c in range(4)]
PSUM_PLAN += ["logits", "xv2_0", "rank", "xv2_1"]
FIRST_USES = len(PSUM_PLAN)
PSUM_PLAN += [f"h3T{c}" for c in range(4)]
PSUM_PLAN += ["iq_0", "iq_1", "ikw", "dq2_0", "dq2_1", "dk2_0", "dk2_1", "iqT0", "iqT1", "ikT"]
PSUM_PLAN += ["dv2_0", "dv2_1"]
PSUM_PLAN += ["il0_0", "il0_1", "mq_0", "mq_1", "il1_0", "il1_1", "mk_0", "mk_1", "il1_2", "il1_3"]
PSUM_PLAN += ["mv_0", "mv_1", "dqT2_0", "dqT2_1", "dkT2_0", "dkT2_1", "mqT0", "mqT1", "mkT0", "mkT1"]


def attention_uses(kind):
    uses = [f"{kind}s0_0", f"{kind}s1_0"]
    for pair in range(4):
        if pair < 3:
            uses += [f"{kind}s0_{pair + 1}", f"{kind}s1_{pair + 1}"]
        uses += [f"{kind}pT{2 * pair}", f"{kind}pT{2 * pair + 1}"]
        uses += [f"{kind}o{pair}"]
    return uses


def attention_fillers(kind):
    return {"m": {0: ["mg"], 1: ["xq"], 2: ["dg"], 3: ["xg"]},
            "s": {0: ["gl0"], 1: ["gl1"], 2: ["gl2"], 3: ["gl3"]}}[kind]


def with_fillers(kind):
    uses, fillers = attention_uses(kind), attention_fillers(kind)
    for pair in range(4):
        at = uses.index(f"{kind}pT{2 * pair}")
        uses[at:at] = [f"{b}_{half}" for b in fillers[pair] for half in range(2)]
    return uses


PSUM_PLAN += with_fillers("m")
PSUM_PLAN += with_fillers("s")
PSUM_PLAN += ["xs0_0", "xs1_0", "xs0_1", "xs1_1", "gl4_0", "gl4_1", "xpT0", "xo_0", "xpT1", "xo_1",
              "gl5_0", "gl5_1", "xpT2", "xo_2", "xpT3", "xo_3"]
PSUM_PLAN += [f"up{b}_{c}" for b in range(3) for c in range(4)]
PSUM_PLAN += ["out0_0", "out0_1", "out1_0", "out1_1"]
assert len(set(PSUM_PLAN)) == len(PSUM_PLAN)
USE = {name: (n % 8, n // 8) for n, name in enumerate(PSUM_PLAN)}

LAST_USE = {"gqk": "gqk1", "gv": "gv_1", "dq": "dq_1", "dk": "dk_1", "dv": "dv_1", "gg": "gg_1"}
for b in ("ck0", "ck1", "cv0", "cv1", "wo0", "wo1", "cq0", "cq1", "co0", "co1", "xk2", "xv2", "iq",
          "dq2", "dk2", "dv2", "mq", "mk", "mv", "mg", "xq", "dg", "xg", "gl0", "gl1", "gl2", "gl3",
          "gl4", "gl5", "out0", "out1"):
    LAST_USE[b] = f"{b}_1"
for b in range(3):
    LAST_USE[f"up{b}"] = f"up{b}_3"

NORMS = [("x", 2), ("mem", 2), ("dq", 16), ("dk", 16), ("ck", 8), ("gla", 8), ("da", 8), ("h1", 2),
         ("mem2", 2), ("cq", 8), ("h2", 2), ("h3", 2), ("final", 2)]
NORM_AT = {}
for i, (name, width) in enumerate(NORMS):
    lo = sum(w for _, w in NORMS[:i])
    NORM_AT[name] = (i, lo, lo + width)
NORM_COLS = sum(w for _, w in NORMS)

COLS = {}
for name, rows in (("norm_mix", 8), ("norm_mem", 8), ("norm_cross", 8), ("g_in_2", 8), ("g_mem_2", 8),
                   ("b_merge_2", 24), ("gla_gate_b", 2), ("da_out_norm", 1), ("gla_out_norm", 1),
                   ("cross_q_norm", 2), ("cross_k_norm", 2), ("da_q_norm", 1), ("da_k_norm", 1)):
    COLS[name] = (sum(n for _, n in COLS.values()), rows)
N_COLS = sum(n for _, n in COLS.values())
N_PARAMS = 7


ROW_NORMS = ["x", "mem", "h1", "mem2", "h2", "h3", "final"]
HEAD_SQUARES = ["dq0", "dq1", "dk0", "dk1", "ck0", "ck1", "ck2", "ck3", "og0", "og1",
                "cq0", "cq1", "cq2", "cq3"]
SOFTMAXES = [f"{kind}{n}" for kind in "dcmsx" for n in range(4)]
ROPED = ["iq", "ik", "dq2", "dk2", "mq", "mk"]
RELUS = ["il0_0", "il0_1", "il1_0", "il1_1", "il1_2", "il1_3"]
TANHS = ["gg_0", "gg_1", "mg_0", "mg_1", "dg_0", "dg_1", "xg_0", "xg_1"]


class Carver:

    def __init__(self, tensor, start, limit):
        self.tensor, self.at, self.limit = tensor, start, limit

    def take(self, width):
        lo, self.at = self.at, self.at + width
        assert self.at <= self.limit, (self.at, self.limit)
        return self.tensor[:, lo:lo + width]


class ExpertSems:

    def __init__(self, sem, prefix, first_down):
        self.first_down = first_down
        self.weights = sem(f"{prefix}_weights_landed")
        self.select_ready = sem(f"{prefix}_select_ready")
        self.gates_ready = sem(f"{prefix}_gates_ready")
        self.gathered = sem(f"{prefix}_gathered")
        self.lo_drained = sem(f"{prefix}_gathered_low_drained")
        self.hi_drained = sem(f"{prefix}_gathered_high_drained")
        self.gate_psum = sem(f"{prefix}_gates_transposed")
        self.gate_ready = sem(f"{prefix}_gates_moved")
        self.hidden_psum = sem(f"{prefix}_gate_up_done")
        self.tanh_ready = sem(f"{prefix}_tanh_ready")
        self.half_ready = sem(f"{prefix}_half_ready")
        self.hidden_ready = sem(f"{prefix}_hidden_ready")
        self.hidden_turned = sem(f"{prefix}_hidden_turned")
        self.hidT_ready = sem(f"{prefix}_hidden_turned_moved")
        self.down_done = sem(f"{prefix}_down_done")
        self.y_ready = sem(f"{prefix}_outputs_moved")
        self.scattered = sem(f"{prefix}_scattered")
        self.added = sem(f"{prefix}_added")
        self.ranks_shifted = sem(f"{prefix}_ranks_shifted")


def build(nc, A, out):
    with ExitStack() as ctx:
        def sb(name, shape, dt=F32):
            return ctx.enter_context(nc.sbuf_tensor(name, shape, dt))

        def sem(name):
            return ctx.enter_context(nc.semaphore(name))

        ring = sb("ring", [P, RING * SLOT])
        h = sb("h", [P, TT, D])
        normed = sb("normed", [P, TT, D])
        uT = sb("uT", [P, KC, T])
        ident = sb("ident", [P, P])
        ones = sb("ones", [P, P])
        earlier = sb("earlier", [P, P])
        build_m = sb("build_m", [P, P])
        ident_b = sb("ident_b", [P, P], BF16)
        causal_b = sb("causal_b", [P, P], BF16)
        chunks_b = sb("chunks_b", [P, P], BF16)
        past_m = sb("past_m", [P, P], U8)
        future_m = sb("future_m", [P, P], U8)
        slot_no = sb("slot_no", [P, CAP])
        slot_i = sb("slot_i", [P, CAP], I32)
        rope = sb("rope", [P, TT, 2 * HD])
        rows = sb("rows", [P, P])
        cols = sb("cols", [P, N_COLS])
        half_bias = sb("half_bias", [P, 24])
        qk_gain = sb("qk_gain", [P, 4])
        wide_gain = sb("wide_gain", [P, D])
        lam_s = sb("lam_s", [P, 8])
        neg_lam = sb("neg_lam", [P, 1])
        w_router = sb("w_router", [P, KC, N_GROUPS + N_EXPERTS])
        b_router = sb("b_router", [P, N_GROUPS + N_EXPERTS])
        w_ikw = sb("w_ikw", [P, KC, HD + H2])
        iw = sb("iw", [P, TT, H2])
        mean_sq = sb("mean_sq", [P, NORM_COLS])
        rstd = sb("rstd", [P, NORM_COLS])
        minus_half = sb("minus_half", [P, 16])
        expsum = sb("expsum", [P, 2 * 4])
        act_junk = sb("act_junk", [P, 1])
        most = sb("most", [P, 1])
        marks = sb("marks", [P, 8])
        rt_exp = sb("rt_exp", [P, TT, N_GROUPS + 1])
        assigned = sb("assigned", [P, TT, N_EXPERTS])
        maxes = sb("maxes", [P, 2 * 4])
        bias = sb("bias", [P, 2 * 4])
        inv = sb("inv", [P, 2 * 4])
        coef = sb("coef", [P, 2 * 4])
        q_scale = sb("q_scale", [P, 2, 24])
        decay = sb("decay", [P, 8])
        chunk_start = sb("chunk_start", [P, T])
        rank1 = sb("rank1", [P, TT, N_EXPERTS])
        gates = sb("gates", [P, TT, N_EXPERTS])
        expert_no = sb("expert_no", [P, N_EXPERTS])
        expert_i = sb("expert_i", [P, N_EXPERTS], I32)
        over_flag = sb("over_flag", [P, 1], I32)
        squares = sb("squares", [P, 2 * 512])
        tanh_b = squares
        free = nc.sbuf_bytes_remaining() if callable(nc.sbuf_bytes_remaining) else nc.sbuf_bytes_remaining
        main_cols = min(int(free) // 4 - 64, 16800)
        main = sb("main", [P, main_cols])

        bank = [ctx.enter_context(nc.psum_tensor(f"bank{b}", [P, 512], F32)) for b in range(8)]

        c = Carver(main, 0, main_cols)
        gq, gk = c.take(512), c.take(512)
        la = c.take(512)
        L = c.take(512)
        e_pos = c.take(512)
        q_pos, k_pos, q_neg, k_neg, q_L, k_dec = (c.take(512) for _ in range(6))
        k_decT = c.take(512)
        aT = c.take(1024)
        states = c.take(768)
        gla_end = c.at
        gv = c.take(1024)
        gg = c.take(1024)
        dq_tok, dk_tok, dv = c.take(1024), c.take(1024), c.take(1024)
        dqT, dkT = c.take(1024), c.take(1024)
        d_pT = c.take(384)
        c = Carver(dqT, 0, 1024)
        w_gr = c.take(KC * 16).rearrange("p (k n) -> p k n", k=KC)
        lam_in = c.take(4 * DA_D)
        gate_w, grT = c.take(256)[0:16, :], c.take(T)[0:16, :]
        d_prob = [main[:, 1024:1792], main[:, 1792:2560]]
        c = Carver(main, 0, main_cols)
        cq_tok, cqT, coT = c.take(2048), c.take(2048), c.take(2048)
        c_prob = [c.take(512) for _ in range(4)]
        c_pT = [c.take(512) for _ in range(2)]
        ck_tok = normed[:, :, :].rearrange("p t d -> p (t d)")
        c = Carver(ring, DENSE_RING * SLOT, RING * SLOT)
        mix = c.take(2048)
        mixT = memT = c.take(2048)
        ckT, cv = c.take(2048), c.take(2048)

        c = Carver(main, 0, main_cols)
        xgT = c.take(KC * 2 * CAP)
        select = c.take(2 * 2 * CAP)
        select_g = c.take(2 * 2 * CAP)
        gate_mat = c.take(T)
        tanh_g, half_h, hid = (c.take(F_EXP) for _ in range(3))
        hidT = c.take(FC * 2 * CAP)
        y_slots = c.take(D)
        experts_end = c.at
        rt = main[:, experts_end:experts_end + 512]

        c = Carver(main, 0, main_cols)
        iq_tok, dq2_tok, dk2_tok, mq_tok, mk_tok = (c.take(1024) for _ in range(5))
        iqT, ikT = c.take(1024), c.take(256)
        assert c.at >= experts_end
        dq2T, dk2T = c.take(1024), c.take(1024)
        mqT, mkT = c.take(1024), c.take(1024)
        dv2, mv = c.take(1024), c.take(1024)
        mem2_tok = main[:, c.at - 2048:c.at]
        xkT, xv2 = c.take(1024), c.take(1024)
        mem2T = main[:, c.at:c.at + 2048]
        work_lo = c.at
        score = c.take(512)
        work = c.take(256)
        best8 = c.take(8)
        probs = c.take(768)
        sel_b = c.take(192).bitcast(BF16)
        probT = main[:, work_lo:work_lo + 768]
        rope_t = probs[:, 0:512]
        ik_tok = work
        relu = mk_tok
        ya, yb, yc = iq_tok, dq2_tok, dk2_tok
        mgate, dgate = mq_tok, mk_tok
        x_prob = [main[:, c0:c0 + 512] for c0 in range(6400, 8448, 512)]
        x_pT = [mqT[:, 0:512], mqT[:, 512:1024]]
        up_t = mkT[:, 0:512]
        c = Carver(ring, DENSE_RING * SLOT, RING * SLOT)
        xqT, xgate = c.take(1024), c.take(1024)
        branch_gate = c.take(3 * KC * T)

        filled = [sem(f"bank_filled{b}") for b in range(8)]
        drained = [sem(f"bank_drained{b}") for b in range(8)]
        landed = [sem(f"weights_landed{j}") for j in range(RING)]
        x_landed, mem_landed, mem2_landed = sem("x_landed"), sem("mem_landed"), sem("mem2_landed")
        rows_landed, params_landed = sem("rows_landed"), sem("params_landed")
        gates_landed, lambdas_landed = sem("gates_landed"), sem("lambdas_landed")
        final_gain_landed = sem("final_gain_landed")
        consts_made, masks_cast = sem("consts_made"), sem("masks_cast")
        means_ready, rstd_ready = sem("means_ready"), sem("rstd_ready")
        row_squared = sem("row_squared")
        head_squared, head_summed = sem("head_squared"), sem("head_summed")
        normed_ready = sem("normed_ready")
        keys_normed, scales_ready = sem("keys_normed"), sem("scales_ready")
        lam_products, lam_exps = sem("lam_products"), sem("lam_exps")
        gla_vec, gla_act = sem("gla_vec"), sem("gla_act")
        mix_ready = sem("mix_ready")
        bias_ready, probs_ready = sem("bias_ready"), sem("probs_ready")
        roped = sem("roped")
        relu_done, scored = sem("relu_done"), sem("scored")
        selected = sem("selected")
        tanh_done = sem("tanh_done")
        cross_sq = sem("cross_sq")
        router_step = sem("router_step")
        router_exp = sem("router_exp")
        after_experts = sem("after_experts")
        out_ready, out_stored = sem("out_ready"), sem("out_stored")
        dve_step, act_step, pool_step = sem("dve_step"), sem("act_step"), sem("pool_step")
        rows_switched = sem("rows_switched")

        main_s, more_s = ExpertSems(sem, "moe", 0), ExpertSems(sem, "more", 1)

        def in_bank(name):
            return bank[USE[name][0]]

        def wait_filled(eng, name):
            b, k = USE[name]
            eng.wait_ge(filled[b], k + 1)
            return bank[b]

        def wait_drained(eng, name):
            b, k = USE[name]
            eng.wait_ge(drained[b], k + 1)

        def wait_free(name):
            b, k = USE[name]
            if k:
                nc.tensor.wait_ge(drained[b], k)
            return bank[b]

        def done(name, ins):
            ins.then_inc(drained[USE[name][0]], 1)

        def full(name, ins):
            ins.then_inc(filled[USE[name][0]], 1)

        def chain(eng, signal):
            count = [0]

            def link(ins):
                count[0] += 1
                ins.then_inc(signal, 1)
                eng.wait_ge(signal, count[0])
            return link

        def in_order(eng, signal, names, name):
            eng.wait_ge(signal, names.index(name) + 1)

        def column(name, c=0):
            at = COLS[name][0] + c
            return cols[:, at:at + 1]

        def stat(tile, name):
            _, lo, hi = NORM_AT[name]
            return tile[:, lo:hi]

        def wait_rstd(eng, name):
            eng.wait_ge(rstd_ready, NORM_AT[name][0] + 1)

        def slot(j, chunks=KC):
            return ring[:, j * SLOT:(j + 1) * SLOT].rearrange("p (k n) -> p k n", k=chunks)

        dense = [(n, b) for n, b in enumerate(FIRST_BLOCKS)]
        dense += [(n + len(FIRST_BLOCKS), b) for n, b in enumerate(SECOND_BLOCKS)]
        SLOT_OF = {b: n % DENSE_RING for n, b in dense}
        BEFORE = {b: n // DENSE_RING for n, b in dense}
        FIRST_IN_SLOT = [sum(SLOT_OF[b] == j for b in FIRST_BLOCKS) for j in range(RING)]

        def weights(name, chunks=KC):
            j = SLOT_OF[name]
            turns = BEFORE[name] + 1 + (PAIRS if name in SECOND_BLOCKS else 0)
            nc.tensor.wait_ge(landed[j], 16 * turns)
            return slot(j, chunks)

        def block_cols(w, lo, width=BLOCK_COLS):
            return w[0, :, lo:lo + width].rearrange("(k p) n -> p k n", p=P)

        W1, W2 = A["w_in"], A["w_in_2"]
        SOURCE = {"gqk": block_cols(W1, 1536), "gv": block_cols(W1, 2048), "dq": block_cols(W1, 0),
                  "dk": block_cols(W1, 512), "dv": block_cols(W1, 1024), "gg": block_cols(W1, 2560)}
        for j in range(2):
            SOURCE[f"ck{j}"] = block_cols(A["w_ckv"], 512 * j)
            SOURCE[f"cv{j}"] = block_cols(A["w_ckv"], D + 512 * j)
            SOURCE[f"wo{j}"] = block_cols(A["w_o"], 512 * j)
            SOURCE[f"cq{j}"] = block_cols(A["w_cq"], 512 * j)
            SOURCE[f"co{j}"] = block_cols(A["w_co"], 512 * j)
            SOURCE[f"out{j}"] = block_cols(A["w_out_2"], 512 * j)
        for n, b in enumerate(("mq", "mk", "mv", "mg", "dq2", "dk2", "dv2", "dg", "iq")):
            SOURCE[b] = block_cols(W2, 512 * n)
        IKW_AT = 9 * 512
        SOURCE["xq"] = block_cols(W2, IKW_AT + HD + H2)
        SOURCE["xg"] = block_cols(W2, IKW_AT + HD + H2 + 512)
        for n in range(6):
            SOURCE[f"gl{n}"] = block_cols(W2, IKW_AT + HD + H2 + 1024 + 512 * n)
        SOURCE["xk2"] = block_cols(A["w_mem_kv_2"], 0)
        SOURCE["xv2"] = block_cols(A["w_mem_kv_2"], 512)
        for n, w in enumerate(("w_up_moba_2", "w_up_dsa_2", "w_up_cross_2")):
            SOURCE[f"up{n}"] = A[w][0].rearrange("(k p) n -> p k n", p=P)

        def token_major(a):
            return a.rearrange("(t p) d -> p t d", p=P)

        def token_tiles(x):
            return x.rearrange("p (t d) -> p t d", t=TT)

        block = ctx.enter_context(nc.Block())

        @block.sync
        def _(sp):
            def load_dense(name, extra=None):
                n, j = BEFORE[name], SLOT_OF[name]
                names = FIRST_BLOCKS if name in FIRST_BLOCKS else SECOND_BLOCKS
                at = names.index(name)
                if at >= DENSE_RING:
                    wait_filled(sp, LAST_USE[names[at - DENSE_RING]])
                src = SOURCE[name]
                sp.dma_start(slot(j, src.shape[1]), src).then_inc(landed[j], 16)

            for name, (at, n) in COLS.items():
                w = A[name]
                if name in ("da_q_norm", "da_k_norm"):
                    for half in range(2):
                        sp.dma_start(rows[at:at + 1, half * DA_D:(half + 1) * DA_D], w[0:1, :])\
                            .then_inc(rows_landed, 16)
                else:
                    sp.dma_start(rows[at:at + n, :], w[0].rearrange("(c p) -> c p", p=P))\
                        .then_inc(rows_landed, 16)
            sp.wait_ge(x_landed, 16)
            for name in FIRST_BLOCKS[:2]:
                load_dense(name)
            sp.dma_start(token_tiles(mix), token_major(A["mem"][0])).then_inc(mem_landed, 16)
            for name in FIRST_BLOCKS[2:DENSE_RING]:
                load_dense(name)
            params = [(rope[:, :, :], token_major(A["rope"])),
                      (wide_gain[:, :], A["norm_ffn"].broadcast_to([P, D])),
                      (w_router[:, :, 0:N_GROUPS], A["w_group"][0].rearrange("(k p) n -> p k n", p=P)),
                      (w_router[:, :, N_GROUPS:], A["w_expert"][0].rearrange("(k p) n -> p k n", p=P)),
                      (b_router[:, 0:N_GROUPS], A["b_group"].broadcast_to([P, N_GROUPS])),
                      (b_router[:, N_GROUPS:], A["b_expert"].broadcast_to([P, N_EXPERTS])),
                      (w_ikw[:, :, :], block_cols(W2, IKW_AT, HD + H2))]
            assert len(params) == N_PARAMS
            for dst, src in params:
                sp.dma_start(dst, src).then_inc(params_landed, 16)
            for name in FIRST_BLOCKS[DENSE_RING:]:
                load_dense(name)

            gate_w_of = A["w_e_gate"][0].rearrange("e (k p) n -> e p k n", p=P)
            up_w_of = A["w_e_up"][0].rearrange("e (k p) n -> e p k n", p=P)
            down_w_of = A["w_e_down"][0].rearrange("e (k p) n -> e p k n", p=P)

            def load_two(first_slot, pair, w_of, signals):
                for n in range(2):
                    sp.dma_start(slot(first_slot + n), w_of[pair[n], :, :, :]).then_inc(signals[n], 16)

            def load_down(j, e, signal):
                sp.dma_start(slot(j, FC), down_w_of[e, :, :, :]).then_inc(signal, 16)

            for j in range(2):
                wait_filled(sp, LAST_USE[FIRST_BLOCKS[j - 2]])
                sp.dma_start(slot(j), gate_w_of[j, :, :, :]).then_inc(landed[j], 16)
            wait_filled(sp, "co_3")
            for e in range(2):
                sp.dma_start(slot(4 + e), up_w_of[e, :, :, :]).then_inc(landed[4 + e], 16)
            for e in range(2):
                wait_filled(sp, LAST_USE[("xk2", "xv2")[e]])
                load_down(2 + e, e, landed[2 + e])
            with sp.Fori(1, PAIRS) as i:
                e0 = sp.snap(i * 2)
                e1 = sp.snap(i * 2 + 1)
                gates_used = sp.snap(i * 2 - 1)
                all_used = sp.snap(i * 2)
                sp.wait_ge(main_s.hidden_psum, gates_used)
                load_two(0, (e0, e1), gate_w_of, landed[0:2])
                sp.wait_ge(main_s.hidden_psum, all_used)
                load_two(4, (e0, e1), up_w_of, landed[4:6])
                sp.wait_ge(main_s.down_done, all_used)
                load_down(2, e0, landed[2])
                load_down(3, e1, landed[3])
            sp.wait_ge(main_s.down_done, N_EXPERTS)

            sp.wait_ge(router_step, 2)
            over = sp.value_load(over_flag[0:1, 0:1], min_val=0, max_val=1)
            with sp.If(over):
                sp.sem_inc(more_s.down_done, 1)
                with sp.Fori(0, MORE_ROUNDS) as r:
                    with sp.Fori(0, PAIRS) as i:
                        e0 = sp.snap(i * 2)
                        e1 = sp.snap(i * 2 + 1)
                        used = sp.snap(r * N_EXPERTS + i * 2 + 1)
                        sp.wait_ge(more_s.down_done, used)
                        load_two(0, (e0, e1), gate_w_of, [more_s.weights] * 2)
                        load_two(4, (e0, e1), up_w_of, [more_s.weights] * 2)
                        load_down(2, e0, more_s.weights)
                        load_down(3, e1, more_s.weights)
                sp.wait_ge(more_s.down_done, 1 + MORE_ROUNDS * N_EXPERTS)
            for name in SECOND_BLOCKS:
                load_dense(name)

            for t in range(TT):
                sp.wait_ge(out_ready, 1 + t)
                sp.dma_start(token_major(out[0])[:, t, :], normed[:, t, :]).then_inc(out_stored, 16)
            sp.wait_ge(out_stored, 16 * TT)

        @block.gpsimd
        def _(pool):
            g = nc.gpsimd
            link = chain(pool, pool_step)
            link(g.memset(ident[:, :], 0.0))
            g.affine_select(out=ident[:, :], in_=ident[:, :], compare_op=ALU.not_equal, fill=1.0, base=0,
                            pattern=[[-1, P]], channel_multiplier=1).then_inc(consts_made, 1)
            g.memset(minus_half[:, :], -0.5).then_inc(consts_made, 1)
            g.memset(ones[:, :], 1.0).then_inc(consts_made, 1)
            g.iota(slot_i[:, :], pattern=[[1, CAP]], base=1, channel_multiplier=0).then_inc(consts_made, 1)
            g.iota(expert_i[:, :], pattern=[[1, N_EXPERTS]], base=0, channel_multiplier=0)\
                .then_inc(consts_made, 1)
            pool.wait_ge(consts_made, 5)
            g.affine_select(out=earlier[:, :], in_=ones[:, :], compare_op=ALU.is_gt, fill=0.0, base=0,
                            pattern=[[1, P]], channel_multiplier=-1).then_inc(consts_made, 1)

            def rsqrt(name):
                n, lo, hi = NORM_AT[name]
                pool.wait_ge(means_ready, n + 1)
                g.tensor_tensor(out=rstd[:, lo:hi], in0=mean_sq[:, lo:hi], in1=minus_half[:, 0:hi - lo],
                                op=ALU.pow).then_inc(rstd_ready, 1)

            def mask(made, steps):
                if made:
                    pool.wait_ge(masks_cast, made)
                for step in steps[:-1]:
                    link(step())
                steps[-1]().then_inc(consts_made, 1)

            def fill(value, rows_=slice(0, P), cols_=slice(0, P)):
                return lambda: g.memset(build_m[rows_, cols_], value)

            def keep(op, pattern, mult, value):
                return lambda: g.affine_select(out=build_m[:, :], in_=build_m[:, :], compare_op=op,
                                               fill=value, base=0, pattern=[[pattern, P]],
                                               channel_multiplier=mult)

            low, high = slice(0, GLA_CHUNK), slice(GLA_CHUNK, P)
            rsqrt("x")
            mask(0, [fill(1.0), keep(ALU.is_ge, 1, -1, 0.0), fill(0.0, low, high)])
            mask(1, [fill(1.0), keep(ALU.is_gt, -1, 1, 0.0), fill(0.0, high, low)])
            mask(2, [fill(0.0), fill(NEG, low, high)])
            mask(3, [fill(0.0), keep(ALU.is_ge, -1, 1, NEG)])
            for name, _ in NORMS[1:]:
                rsqrt(name)

        @block.scalar
        def _(act):
            a = nc.scalar
            link = chain(act, act_step)
            act.dma_start(h[:, :, :], token_major(A["x"][0])).then_inc(x_landed, 16)
            act.dma_start(w_gr[:, :, :], block_cols(W1, 3072, 16)).then_inc(gates_landed, 16)
            act.dma_start(gate_w[:, :], A["gla_gate_w"][0]).then_inc(gates_landed, 16)
            for n, name in enumerate(("lambda_q1", "lambda_k1", "lambda_q2", "lambda_k2")):
                act.dma_start(lam_in[:, n * DA_D:(n + 1) * DA_D], A[name].broadcast_to([P, DA_D]))\
                    .then_inc(lambdas_landed, 16)

            def copy(name, dst, width=512, rows_=P, scale=1.0):
                src = wait_filled(act, name)[0:rows_, 0:width]
                done(name, a.activation(dst, src, ACT.Copy, scale=scale))

            def square_rows(name, src, junk):
                _, lo, _ = NORM_AT[name]
                for t in range(TT):
                    last = a.activation(junk[:, t, :], src[:, t, :], ACT.Square,
                                        accum_out=mean_sq[:, lo + t:lo + t + 1])
                last.then_inc(row_squared, 1)

            def square_heads(name, bank_name):
                n = HEAD_SQUARES.index(name)
                if n >= 2:
                    act.wait_ge(head_summed, n - 1)
                a.activation(squares[:, n % 2 * 512:n % 2 * 512 + 512], wait_filled(act, bank_name)[:, :],
                             ACT.Square).then_inc(head_squared, 1)

            def gained(name, dst, gains):
                src = wait_filled(act, name)
                for n, gain in enumerate(gains):
                    last = a.activation(dst[:, n * T:(n + 1) * T], src[:, n * T:(n + 1) * T], ACT.Copy,
                                        scale=gain)
                done(name, last)

            def uT_chunks(c2):
                return uT[:, 2 * c2:2 * c2 + 2, :].rearrange("p c t -> p (c t)")

            def norm_T(prefix, dst, gain):
                for c2 in (0, 2):
                    gained(f"{prefix}T{c2}", dst(c2), [column(gain, 2 * c2 + n) for n in range(2)])

            def exps(name, n, parts, probs_free=None):
                place = SOFTMAXES.index(name)
                act.wait_ge(bias_ready, place + 1)
                if probs_free:
                    wait_filled(act, probs_free)
                at = place % 2 * 4
                for i, (src, dst, col, scale, ends) in enumerate(parts):
                    ins = a.activation(dst, src, ACT.Exp, bias=bias[:, at + col:at + col + 1], scale=scale,
                                       accum_out=expsum[:, at + col:at + col + 1])
                    if ends:
                        done(ends, ins)

            def tiles(x):
                return x.rearrange("p (t d) -> p t d", t=TT)

            act.wait_ge(rows_landed, 16 * (len(COLS) + 2))
            copy("cols", cols[:, :], N_COLS)
            act.wait_ge(x_landed, 16)
            square_rows("x", h, normed)
            wait_drained(act, "cols")
            norm_T("x", uT_chunks, "norm_mix")

            copy("grT", grT[:, :], T, 16)
            copy("gqk0", gq, scale=DA_D ** -0.5)
            copy("gqk1", gk)
            act.wait_ge(mem_landed, 16)
            square_rows("mem", mix.rearrange("p (t d) -> p t d", t=TT),
                        memT.rearrange("p (t d) -> p t d", t=TT))
            act.wait_ge(lam_products, 1)
            a.activation(lam_s[:, 2:4], lam_s[:, 0:2], ACT.Exp).then_inc(lam_exps, 1)
            act.wait_ge(gla_vec, 1)
            link(a.activation(k_dec, k_dec, ACT.Exp))
            a.activation(k_dec, k_dec, ACT.Ln, bias=1.0).then_inc(gla_act, 1)
            for t in range(TT):
                copy(f"gv_{t}", gv[:, t * 512:t * 512 + 512])
            for name, dst in (("dq", dq_tok), ("dk", dk_tok)):
                for t in range(TT):
                    square_heads(f"{name}{t}", f"{name}_{t}")
                    copy(f"{name}_{t}", dst[:, t * 512:t * 512 + 512])
            act.wait_ge(gla_vec, 2)
            tau = 1.0 / GLA_TAU
            a.activation(e_pos, la, ACT.Exp, scale=tau)
            a.activation(q_L, L, ACT.Exp, scale=tau)
            a.activation(decay[:, :], L.rearrange("p (c t) -> p c t", t=GLA_CHUNK)[:, :, GLA_CHUNK - 1],
                         ACT.Exp, scale=tau)
            a.activation(k_dec, k_dec, ACT.Exp, scale=tau)
            a.activation(la, la, ACT.Exp, scale=-tau).then_inc(gla_act, 1)
            norm_T("mem", lambda c2: memT[:, c2 * 512:c2 * 512 + 512], "norm_mem")
            copy("kdT", k_decT)
            for j in range(2):
                for t in range(TT):
                    square_heads(f"ck{2 * j + t}", f"ck{j}_{t}")
                    if j + t == 0:
                        wait_filled(act, "xT3")
                    copy(f"ck{j}_{t}", ck_tok[:, t * D + j * 512:t * D + j * 512 + 512])
            for t in range(TT):
                square_heads(f"og{t}", f"og{t}")
                if t == 0:
                    wait_filled(act, "memT3")
                copy(f"og{t}", mix[:, t * D + 512:(t + 1) * D])
            for half in range(2):
                copy(f"dkT{half}", dkT[:, half * 512:half * 512 + 512])
            for c2 in (0, 2):
                copy(f"ckT{c2}", ckT[:, c2 * 512:c2 * 512 + 512])
            for t in range(TT):
                copy(f"dv_{t}", dv[:, t * 512:t * 512 + 512])

            def d_exps(hh):
                s0 = wait_filled(act, f"ds0_{hh}")
                s1 = wait_filled(act, f"ds1_{hh}")
                parts = []
                for t in range(TT):
                    for s in range(2):
                        lo = s * P if t == 0 else s * T
                        src = (s0, s1)[t][:, lo:lo + (t + 1) * P]
                        dst = d_prob[hh % 2][:, s * 384 + t * P:s * 384 + t * P + (t + 1) * P]
                        at = t * 8 + hh * 2 + s
                        ends = f"ds{t}_{hh}" if s else None
                        parts.append((src, dst, t * 2 + s, q_scale[:, 0, at:at + 1], ends))
                exps(f"d{hh}", hh, parts, f"dpT{hh - 2}" if hh >= 2 else None)

            def d_pT_out(hh):
                if hh:
                    wait_filled(act, f"do{hh - 1}")
                copy(f"dpT{hh}", d_pT, 384)

            def d_out(hh):
                src = wait_filled(act, f"do{hh}")
                _, lo, _ = NORM_AT["da"]
                for t in range(TT):
                    junk = squares[:, (t * 4 + hh) * P:(t * 4 + hh + 1) * P]
                    a.activation(junk, src[:, t * P:(t + 1) * P], ACT.Square,
                                 accum_out=mean_sq[:, lo + t * 4 + hh:lo + t * 4 + hh + 1])
                dst = mix.rearrange("p (t d) -> p t d", t=TT)[:, :, hh * P:(hh + 1) * P]
                done(f"do{hh}", a.activation(dst, src[:, 0:2 * P].rearrange("p (t d) -> p t d", t=TT),
                                             ACT.Copy))

            def gate_tanh(name):
                n = TANHS.index(name)
                if n >= 2:
                    wait_drained(act, TANHS[n - 2])
                a.activation(tanh_b[:, n % 2 * 512:n % 2 * 512 + 512], wait_filled(act, name)[:, :],
                             ACT.Tanh, scale=0.5).then_inc(tanh_done, 1)

            d_exps(0)
            d_exps(1)
            act.wait_ge(head_summed, len(HEAD_SQUARES[:10]))
            for t in range(TT):
                gate_tanh(f"gg_{t}")
            d_pT_out(0)
            wait_drained(act, "gg_1")
            d_out(0)
            d_exps(2)
            d_pT_out(1)
            d_out(1)
            d_exps(3)
            for hh in (2, 3):
                d_pT_out(hh)
                d_out(hh)
            wait_filled(act, "do3")
            act.dma_start(tiles(mem2_tok), token_major(A["mem_2"][0])).then_inc(mem2_landed, 16)
            act.wait_ge(mix_ready, 1)
            da_gain, gla_gain = qk_gain[:, 1:2], column("gla_out_norm")
            gained("mixT0", mixT[:, 0:512], [da_gain] * 2)
            gained("mixT2", mixT[:, 1024:1536], [gla_gain] * 2)

            for j in range(2):
                for t in range(TT):
                    wait_drained(act, f"wo{j}_{t}")
            square_rows("h1", h, normed)
            norm_T("h1", uT_chunks, "norm_cross")
            act.wait_ge(mem2_landed, 16)
            square_rows("mem2", tiles(mem2_tok), tiles(mem2T))
            for j in range(2):
                for t in range(TT):
                    square_heads(f"cq{2 * j + t}", f"cq{j}_{t}")
                    copy(f"cq{j}_{t}", cq_tok[:, t * D + j * 512:t * D + j * 512 + 512])
            for c2 in (0, 2):
                gained(f"cqT{c2}", cqT[:, c2 * 512:c2 * 512 + 512], [qk_gain[:, 2 + n:3 + n] for n in range(2)])

            norm_T("mem2", lambda c2: mem2T[:, c2 * 512:c2 * 512 + 512], "g_mem_2")

            def pair_exps(kind, t, hp, dsts, scale):
                name = f"{kind}s{t}_{hp}"
                src = wait_filled(act, name)
                parts = [(src[:, n * T:(n + 1) * T], dsts[t + 2 * hp][:, n * T:(n + 1) * T], n,
                          scale(t, 2 * hp + n), name if n else None) for n in range(2)]
                exps(f"{kind}{t + 2 * hp}", t + 2 * hp, parts)

            at = NORM_AT["dq"][2] - NORM_AT["dq"][1]
            for hp in range(2):
                for t in range(TT):
                    pair_exps("c", t, hp, c_prob,
                              lambda t, hh: q_scale[:, 0, at + t * 4 + hh:at + t * 4 + hh + 1])
            copy("xk2_0", xkT[:, 0:512])
            for hh in range(4):
                if hh >= 2:
                    wait_filled(act, f"co_{hh - 2}")
                copy(f"cpT{hh}", c_pT[hh % 2])
            for j in range(2):
                for t in range(TT):
                    wait_drained(act, f"co{j}_{t}")
            square_rows("h2", h, normed)
            copy("xk2_1", xkT[:, 512:1024])
            for c2 in (0, 2):
                copy(f"h2T{c2}", uT_chunks(c2))
            act.wait_ge(normed_ready, 10)
            act.dma_start(wide_gain[:, :], A["g_final_2"].broadcast_to([P, D])).then_inc(final_gain_landed, 16)
            act.wait_ge(router_step, 1)
            a.activation(rt_exp[:, :, :], rt_exp[:, :, :], ACT.Exp).then_inc(router_exp, 1)

            def expert_gates(S, n):
                act.wait_ge(S.gate_psum, n + 1)
                a.activation(gate_mat, bank[4][:, 0:T], ACT.Copy).then_inc(S.gate_ready, 1)

            def expert_tanh(S, n):
                act.wait_ge(S.hidden_psum, n * 2 + 1)
                a.activation(tanh_g, bank[2][:, :], ACT.Tanh, scale=0.5).then_inc(S.tanh_ready, 1)

            def turned_hidden(S, n):
                act.wait_ge(S.hidden_turned, n + 1)
                a.activation(hidT, bank[0][:, :], ACT.Copy).then_inc(S.hidT_ready, 1)

            def expert_out(S, n):
                for half in range(2):
                    act.wait_ge(S.down_done, n * 2 + 1 + half + S.first_down)
                    last = a.activation(y_slots[:, half * 512:half * 512 + 512], bank[4 + half][:, :], ACT.Copy)
                last.then_inc(S.y_ready, 1)

            def gathered_low(S, n):
                act.wait_ge(S.gathered, n + 1)
                a.activation(xgT[:, 0:512], bank[0][:, :], ACT.Copy).then_inc(S.lo_drained, 1)

            a.activation(act_junk[:, :], bias[:, 0:1], ACT.Copy).then_inc(main_s.y_ready, 1)
            gathered_low(main_s, 0)
            with act.Fori(0, PAIRS - 1) as i:
                expert_gates(main_s, i)
                expert_tanh(main_s, i)
                turned_hidden(main_s, i)
                expert_out(main_s, i)
                gathered_low(main_s, i + 1)
            expert_gates(main_s, PAIRS - 1)
            expert_tanh(main_s, PAIRS - 1)
            turned_hidden(main_s, PAIRS - 1)
            expert_out(main_s, PAIRS - 1)
            act.wait_ge(router_step, 2)
            over = act.value_load(over_flag[0:1, 0:1], min_val=0, max_val=1)
            with act.If(over):
                a.activation(act_junk[:, :], bias[:, 0:1], ACT.Copy).then_inc(more_s.y_ready, 1)
                with act.Fori(0, MORE_ROUNDS * PAIRS) as n:
                    gathered_low(more_s, n)
                    expert_gates(more_s, n)
                    expert_tanh(more_s, n)
                    turned_hidden(more_s, n)
                    expert_out(more_s, n)

            act.wait_ge(after_experts, 1)
            square_rows("h3", h, normed)
            norm_T("h3", uT_chunks, "g_in_2")
            for half in range(2):
                copy(f"iqT{half}", iqT[:, half * 512:half * 512 + 512])
            copy("ikT", ikT, T)
            for t in range(TT):
                copy(f"dv2_{t}", dv2[:, t * 512:t * 512 + 512])

            def relu_bank(name):
                n = RELUS.index(name)
                if n >= 2:
                    act.wait_ge(scored, n - 1)
                done(name, a.activation(relu[:, n % 2 * 512:n % 2 * 512 + 512], wait_filled(act, name)[:, :],
                                        ACT.Relu, scale=HD ** -0.5))

            for name in RELUS:
                relu_bank(name)
            for t in range(TT):
                copy(f"mv_{t}", mv[:, t * 512:t * 512 + 512])
            for name, dst in (("dqT2", dq2T), ("dkT2", dk2T)):
                for half in range(2):
                    copy(f"{name}_{half}", dst[:, half * 512:half * 512 + 512])
            for name, dst in (("mqT", mqT), ("mkT", mkT)):
                for half in range(2):
                    copy(f"{name}{half}", dst[:, half * 512:half * 512 + 512])

            def branch_tanh(n, half):
                name = f"gl{n}_{half}"
                src = wait_filled(act, name)
                for c in range(2):
                    chunk = 4 * n + 2 * half + c
                    last = a.activation(branch_gate[:, chunk * T:(chunk + 1) * T], src[:, c * T:(c + 1) * T],
                                        ACT.Tanh, scale=0.5, bias=half_bias[:, chunk:chunk + 1])
                done(name, last)

            def filler(b):
                for half in range(2):
                    if b == "xq":
                        copy(f"xq_{half}", xqT[:, half * 512:half * 512 + 512])
                    elif b.startswith("gl"):
                        branch_tanh(int(b[2:]), half)
                    else:
                        gate_tanh(f"{b}_{half}")

            def pair8_exps(kind, pair):
                s0 = wait_filled(act, f"{kind}s0_{pair}")
                s1 = wait_filled(act, f"{kind}s1_{pair}")
                parts = []
                for t in range(TT):
                    for n in range(2):
                        lo = n * P if t == 0 else n * T
                        src = (s0, s1)[t][:, lo:lo + (t + 1) * P]
                        dst = probs[:, n * 384 + t * P:n * 384 + t * P + (t + 1) * P]
                        ends = f"{kind}s{t}_{pair}" if n else None
                        parts.append((src, dst, t * 2 + n, HD ** -0.5, ends))
                exps(f"{kind}{pair}", pair, parts, f"{kind}pT{2 * pair - 1}" if pair else None)

            def pair8(kind, pair):
                if kind == "m" and pair == 0:
                    pair8_exps(kind, 0)
                for b in attention_fillers(kind)[pair]:
                    filler(b)
                for n in range(2):
                    if kind + str(pair) == "m0" and n == 0:
                        act.wait_ge(selected, 2)
                    copy(f"{kind}pT{2 * pair + n}", probT[:, n * 384:n * 384 + 384], 384)
                if pair < 3:
                    pair8_exps(kind, pair + 1)
                elif kind == "m":
                    pair8_exps("s", 0)

            for kind in "ms":
                for pair in range(4):
                    pair8(kind, pair)
            for hp in range(2):
                for t in range(TT):
                    pair_exps("x", t, hp, x_prob, lambda t, hh: X2_D ** -0.5)
            filler("gl4")
            for hh in range(4):
                if hh == 2:
                    filler("gl5")
                if hh >= 2:
                    wait_filled(act, f"xo_{hh - 2}")
                copy(f"xpT{hh}", x_pT[hh % 2])
            for j in range(2):
                for t in range(TT):
                    wait_drained(act, f"out{j}_{t}")
            square_rows("final", h, normed)

        @block.vector
        def _(dve):
            v = nc.vector
            link = chain(dve, dve_step)

            def mean(name, width):
                st = stat(mean_sq, name)
                v.tensor_scalar(st, st, 1.0 / width, EPS, ALU.mult, ALU.add).then_inc(means_ready, 1)

            def scale_rows(name, src, dst):
                in_order(dve, row_squared, ROW_NORMS, name)
                mean(name, D)
                wait_rstd(dve, name)
                _, lo, _ = NORM_AT[name]
                for t in range(TT):
                    v.tensor_scalar(dst[:, t, :], src[:, t, :], rstd[:, lo + t:lo + t + 1], None, ALU.mult)\
                        .then_inc(normed_ready, 1)

            def head_sums(name, dst, heads):
                n = HEAD_SQUARES.index(name)
                dve.wait_ge(head_squared, n + 1)
                src = squares[:, n % 2 * 512:n % 2 * 512 + 512].rearrange("p (h d) -> p h d", h=heads)
                v.tensor_reduce(dst, src, axis=X, op=ALU.add).then_inc(head_summed, 1)

            def copy(name, dst, width=512):
                done(name, v.tensor_copy(dst, wait_filled(dve, name)[:, 0:width]))

            def gained(name, dst, gains):
                src = wait_filled(dve, name)
                for n, gain in enumerate(gains):
                    last = v.tensor_scalar(dst[:, n * T:(n + 1) * T], src[:, n * T:(n + 1) * T], gain, None,
                                           ALU.mult)
                done(name, last)

            def uT_chunks(c2):
                return uT[:, 2 * c2:2 * c2 + 2, :].rearrange("p c t -> p (c t)")

            def norm_T(prefix, dst, gain):
                for c2 in (1, 3):
                    gained(f"{prefix}T{c2}", dst(c2), [column(gain, 2 * c2 + n) for n in range(2)])

            def tiles(x):
                return x.rearrange("p (t d) -> p t d", t=TT)

            marks_made = [0]

            def mark(signal, by):
                n = marks_made[0]
                marks_made[0] += 1
                v.tensor_copy(marks[:, n:n + 1], ones[:, 0:1]).then_inc(signal, by)

            v.memset(aT, 0.0)
            link(v.memset(chunk_start[:, :], 1.0))
            link(v.memset(chunk_start[:, :].rearrange("p (c t) -> p c t", t=GLA_CHUNK)[:, :, 0:1], 0.0))
            scale_rows("x", h, normed)
            wait_drained(dve, "cols")
            v.tensor_scalar(half_bias[:, :], cols[:, COLS["b_merge_2"][0]:COLS["b_merge_2"][0] + 24], 0.5,
                            None, ALU.mult)
            v.tensor_tensor(qk_gain[:, 0:1], column("da_q_norm"), column("da_k_norm"), ALU.mult)
            v.tensor_scalar(qk_gain[:, 1:2], column("da_out_norm"), 1.0 - LAM_INIT, None, ALU.mult)
            q0, k0 = COLS["cross_q_norm"][0], COLS["cross_k_norm"][0]
            link(v.tensor_tensor(qk_gain[:, 2:4], cols[:, q0:q0 + 2], cols[:, k0:k0 + 2], ALU.mult))
            norm_T("x", uT_chunks, "norm_mix")
            dve.wait_ge(consts_made, 6)
            v.tensor_copy(ident_b[:, :], ident[:, :])
            v.tensor_copy(slot_no[:, :], slot_i[:, :])
            v.tensor_copy(expert_no[:, :], expert_i[:, :])
            for n, dst in enumerate((past_m, future_m, chunks_b, causal_b)):
                dve.wait_ge(consts_made, 7 + n)
                v.tensor_copy(dst[:, :], build_m[:, :]).then_inc(masks_cast, 1)
            dve.wait_ge(lambdas_landed, 16 * 4)
            pr = lam_in[:, :].rearrange("p (q k d) -> p q k d", q=2, k=2)
            link(v.tensor_tensor(pr[:, :, 0, :], pr[:, :, 0, :], pr[:, :, 1, :], ALU.mult))
            v.tensor_reduce(lam_s[:, 0:2], pr[:, :, 0, :], axis=X, op=ALU.add).then_inc(lam_products, 1)

            z = wait_filled(dve, "z")
            for pair in range(2):
                last = v.tensor_scalar(la[:, pair * T:(pair + 1) * T], z[:, pair * T:(pair + 1) * T],
                                       column("gla_gate_b", pair), None, ALU.add)
            done("z", last)
            wait_drained(dve, "z")
            v.scalar_tensor_tensor(k_dec, la, -1.0, la, ALU.mult, ALU.min).then_inc(gla_vec, 1)
            link(v.tensor_scalar(la, la, 0.0, None, ALU.min))
            dve.wait_ge(lam_exps, 1)
            link(v.tensor_tensor(neg_lam[:, :], lam_s[:, 3:4], lam_s[:, 2:3], ALU.subtract))
            link(v.tensor_scalar(neg_lam[:, :], neg_lam[:, :], -LAM_INIT, None, ALU.add))
            dve.wait_ge(gla_act, 1)
            link(v.tensor_tensor(la, la, k_dec, ALU.subtract))
            for pair in range(2):
                at = slice(pair * T, (pair + 1) * T)
                scan = v.tensor_tensor_scan(L[:, at], chunk_start[:, :], la[:, at], 0.0, ALU.mult, ALU.add)
            link(scan)
            Lr = L.rearrange("p (c t) -> p c t", t=GLA_CHUNK)

            def from_L(dst, at, first_is_L):
                ref = Lr[:, :, at:at + 1].broadcast_to([P, 2 * T // GLA_CHUNK, GLA_CHUNK])
                d = dst.rearrange("p (c t) -> p c t", t=GLA_CHUNK)
                pair = (Lr, ref) if first_is_L else (ref, Lr)
                return v.tensor_tensor(d, pair[0], pair[1], ALU.subtract)

            from_L(la, GLA_CHUNK // 2 - 1, True)
            from_L(k_dec, GLA_CHUNK - 1, False).then_inc(gla_vec, 1)
            scale_rows("mem", tiles(mix), tiles(mix))
            for name, at in (("dq", NORM_AT["dq"][1]), ("dk", NORM_AT["dk"][1])):
                for t in range(TT):
                    head_sums(f"{name}{t}", mean_sq[:, at + 8 * t:at + 8 * t + 8], 8)
                dve.wait_ge(head_summed, 2 if name == "dq" else 4)
                mean(name, DA_D)
            dve.wait_ge(gla_act, 2)
            wait_drained(dve, "gqk1")
            v.tensor_tensor(q_pos, gq, e_pos, ALU.mult)
            v.tensor_tensor(k_neg, gk, la, ALU.mult)
            v.tensor_tensor(q_neg, gq, la, ALU.mult)
            v.tensor_tensor(k_pos, gk, e_pos, ALU.mult)
            v.tensor_tensor(k_dec, gk, k_dec, ALU.mult).then_inc(gla_vec, 1)
            v.tensor_tensor(q_L, gq, q_L, ALU.mult).then_inc(gla_vec, 1)
            norm_T("mem", lambda c2: memT[:, c2 * 512:c2 * 512 + 512], "norm_mem")
            wait_rstd(dve, "dk")
            _, lo, hi = NORM_AT["dk"]
            kk = dk_tok.rearrange("p (j d) -> p j d", d=DA_D)
            wait_drained(dve, "dk_1")
            v.tensor_tensor(kk, kk, rstd[:, lo:hi].rearrange("p (j o) -> p j o", o=1)
                            .broadcast_to([P, 16, DA_D]), ALU.mult).then_inc(keys_normed, 1)

            def q_scales(name, at, scale):
                st = stat(rstd, name)
                n = st.shape[1]
                v.tensor_scalar(q_scale[:, 0, at:at + n], st, scale, None, ALU.mult)
                v.tensor_scalar(q_scale[:, 1, at:at + n], st, -scale, None, ALU.mult)\
                    .then_inc(scales_ready, 1)

            q_scales("dq", 0, DA_D ** -0.5)
            dve.wait_ge(scales_ready, 1)
            for t in range(TT):
                for name, m in (("past", past_m), ("fut", future_m)):
                    src = wait_filled(dve, f"{name}{t}")
                    dst = aT[:, t * 512:t * 512 + 512].rearrange("p (h i) -> p h i", h=H1)
                    mask3 = m[:, :].rearrange("p (o i) -> p o i", o=1).broadcast_to([P, H1, P])
                    done(f"{name}{t}", v.copy_predicated(dst, mask3, src[:, :].rearrange("p (h i) -> p h i", h=H1)))
                    wait_drained(dve, f"{name}{t}")
            u01 = wait_filled(dve, "u01")
            u2 = wait_filled(dve, "u2")
            link(v.tensor_copy(states[:, 0:256], u01[:, 0:256]))
            for ch in (1, 2):
                src = (u01[:, 256:512], u2[:, 0:256])[ch - 1]
                for pair in range(2):
                    lo = pair * P
                    last = v.scalar_tensor_tensor(states[:, ch * 256 + lo:ch * 256 + lo + P],
                                                  states[:, (ch - 1) * 256 + lo:(ch - 1) * 256 + lo + P],
                                                  decay[:, pair * 4 + ch:pair * 4 + ch + 1],
                                                  src[:, lo:lo + P], ALU.mult, ALU.add)
                done(("u01", "u2")[ch - 1], last)
                wait_drained(dve, ("u01", "u2")[ch - 1])
            _, lo, hi = NORM_AT["ck"]
            for j in range(2):
                for t in range(TT):
                    head_sums(f"ck{2 * j + t}", mean_sq[:, lo + 4 * t + 2 * j:lo + 4 * t + 2 * j + 2], 2)
            dve.wait_ge(head_summed, 8)
            mean("ck", CROSS_D)
            _, glo, _ = NORM_AT["gla"]
            for t in range(TT):
                head_sums(f"og{t}", mean_sq[:, glo + 4 * t:glo + 4 * t + 4], H1)
            dve.wait_ge(head_summed, 10)
            mean("gla", DV)
            wait_rstd(dve, "ck")
            wait_drained(dve, "ck1_1")
            kk = ck_tok.rearrange("p (j d) -> p j d", d=CROSS_D)
            v.tensor_tensor(kk, kk, rstd[:, lo:hi].rearrange("p (j o) -> p j o", o=1)
                            .broadcast_to([P, 8, CROSS_D]), ALU.mult).then_inc(keys_normed, 1)
            for half in range(2):
                gained(f"dqT{half}", dqT[:, half * 512:half * 512 + 512], [qk_gain[:, 0:1]] * 2)
            for j in range(2):
                for t in range(TT):
                    copy(f"cv{j}_{t}", cv[:, t * D + j * 512:t * D + j * 512 + 512])
            for c2 in (1, 3):
                copy(f"ckT{c2}", ckT[:, c2 * 512:c2 * 512 + 512])

            def soft_bias(name, parts, out_view, scale_view):
                place = SOFTMAXES.index(name)
                at = place % 2 * 4
                for src, lo, n in parts:
                    last = v.tensor_reduce(maxes[:, at + lo:at + lo + n], src, axis=X, op=ALU.max)
                link(last)
                b, m = out_view(bias[:, at:at + 4]), out_view(maxes[:, at:at + 4])
                if isinstance(scale_view, float):
                    v.tensor_scalar(b, m, scale_view, None, ALU.mult).then_inc(bias_ready, 1)
                else:
                    v.tensor_tensor(b, m, scale_view, ALU.mult).then_inc(bias_ready, 1)

            def soft_inverse(name, n, last_bank):
                at = SOFTMAXES.index(name) % 2 * 4
                wait_drained(dve, last_bank)
                link(v.reciprocal(inv[:, at:at + n], expsum[:, at:at + n]))
                return at

            def d_bias(hh):
                s0 = wait_filled(dve, f"ds0_{hh}")[:, 0:2 * P]
                s1 = wait_filled(dve, f"ds1_{hh}")
                neg = q_scale[:, 1, 0:16].rearrange("p (t j) -> p t j", t=TT)[:, :, 2 * hh:2 * hh + 2]
                soft_bias(f"d{hh}", [(s0.rearrange("p (s k) -> p s k", s=2), 0, 2),
                                     (s1[:, :].rearrange("p (s k) -> p s k", s=2), 2, 2)],
                          lambda x: x.rearrange("p (t s) -> p t s", t=2), neg)

            def d_weights(hh):
                at = soft_inverse(f"d{hh}", 4, f"ds1_{hh}")
                iv = inv[:, at:at + 4].rearrange("p (t s) -> p t s", t=2)
                cf = coef[:, at:at + 4].rearrange("p (t s) -> p t s", t=2)
                link(v.tensor_scalar(cf[:, :, 1], iv[:, :, 1], neg_lam[:, 0:1], None, ALU.mult))
                pr = d_prob[hh % 2]
                for t in range(TT):
                    lo, w = t * P, (t + 1) * P
                    last = v.tensor_scalar(pr[:, lo:lo + w], pr[:, lo:lo + w],
                                           inv[:, at + 2 * t:at + 2 * t + 1], None, ALU.mult)
                link(last)
                for t in range(TT):
                    lo, w = t * P, (t + 1) * P
                    last = v.scalar_tensor_tensor(pr[:, lo:lo + w], pr[:, 384 + lo:384 + lo + w],
                                                  coef[:, at + 2 * t + 1:at + 2 * t + 2], pr[:, lo:lo + w],
                                                  ALU.mult, ALU.add)
                last.then_inc(probs_ready, 1)

            def silu_gate(name, dst):
                n = TANHS.index(name)
                dve.wait_ge(tanh_done, n + 1)
                src = wait_filled(dve, name)
                done(name, v.scalar_tensor_tensor(dst, tanh_b[:, n % 2 * 512:n % 2 * 512 + 512], 1.0,
                                                  src[:, :], ALU.add, ALU.mult))

            d_bias(0)
            d_bias(1)
            for t in range(TT):
                silu_gate(f"gg_{t}", gg[:, t * 512:t * 512 + 512])
            wait_drained(dve, "gg_1")
            wait_rstd(dve, "gla")
            wait_drained(dve, "og1")
            mg3 = tiles(mix)[:, :, 512:1024]
            for t in range(TT):
                m4 = mix[:, t * D + 512:(t + 1) * D].rearrange("p (h d) -> p h d", h=H1)
                st = rstd[:, glo + 4 * t:glo + 4 * t + 4].rearrange("p (h o) -> p h o", o=1)
                last = v.tensor_tensor(m4, m4, st.broadcast_to([P, H1, DV]), ALU.mult)
            link(last)
            v.scalar_tensor_tensor(mg3, mg3, 0.5, gg.rearrange("p (t d) -> p t d", t=TT), ALU.mult, ALU.mult)\
                .then_inc(mix_ready, 1)
            d_weights(0)
            d_bias(2)
            d_weights(1)
            d_bias(3)
            d_weights(2)
            d_weights(3)
            wait_drained(dve, "do3")
            mean("da", DV)
            wait_rstd(dve, "da")
            _, lo, _ = NORM_AT["da"]
            for t in range(TT):
                m4 = mix[:, t * D:t * D + 512].rearrange("p (h d) -> p h d", h=H1)
                st = rstd[:, lo + 4 * t:lo + 4 * t + 4].rearrange("p (h o) -> p h o", o=1)
                last = v.tensor_tensor(m4, m4, st.broadcast_to([P, H1, DV]), ALU.mult)
            last.then_inc(mix_ready, 1)
            gained("mixT1", mixT[:, 512:1024], [qk_gain[:, 1:2]] * 2)
            gained("mixT3", mixT[:, 1536:2048], [column("gla_out_norm")] * 2)

            def add_to_h(prefix, scale=None):
                for j in range(2):
                    for t in range(TT):
                        name = f"{prefix}{j}_{t}"
                        src = wait_filled(dve, name)
                        hs = h[:, t, j * 512:(j + 1) * 512]
                        if scale:
                            done(name, v.scalar_tensor_tensor(hs, src[:, :], scale, hs, ALU.mult, ALU.add))
                        else:
                            done(name, v.tensor_tensor(hs, src[:, :], hs, ALU.add))
                for j in range(2):
                    for t in range(TT):
                        wait_drained(dve, f"{prefix}{j}_{t}")

            add_to_h("wo")
            scale_rows("h1", h, normed)
            norm_T("h1", uT_chunks, "norm_cross")
            scale_rows("mem2", tiles(mem2_tok), tiles(mem2_tok))
            _, lo, _ = NORM_AT["cq"]
            for j in range(2):
                for t in range(TT):
                    head_sums(f"cq{2 * j + t}", mean_sq[:, lo + 4 * t + 2 * j:lo + 4 * t + 2 * j + 2], 2)
            dve.wait_ge(head_summed, 14)
            mean("cq", CROSS_D)
            wait_rstd(dve, "cq")
            q_scales("cq", 16, CROSS_D ** -0.5)
            dve.wait_ge(scales_ready, 2)
            for c2 in (1, 3):
                gained(f"cqT{c2}", cqT[:, c2 * 512:c2 * 512 + 512], [qk_gain[:, 2 + n:3 + n] for n in range(2)])

            norm_T("mem2", lambda c2: mem2T[:, c2 * 512:c2 * 512 + 512], "g_mem_2")

            def pair_bias(kind, n, scale_view):
                t, hp = n % 2, n // 2
                src = wait_filled(dve, f"{kind}s{t}_{hp}")
                soft_bias(f"{kind}{n}", [(src[:, :].rearrange("p (h k) -> p h k", h=2), 0, 2)],
                          lambda x: x[:, 0:2], scale_view)

            def pair_weights(kind, n, buffers):
                at = soft_inverse(f"{kind}{n}", 2, f"{kind}s{n % 2}_{n // 2}")
                for i in range(2):
                    pr = buffers[n][:, i * T:(i + 1) * T]
                    last = v.tensor_scalar(pr, pr, inv[:, at + i:at + i + 1], None, ALU.mult)
                last.then_inc(probs_ready, 1)

            def four(bias_, weights_):
                bias_(0)
                bias_(1)
                weights_(0)
                bias_(2)
                weights_(1)
                bias_(3)
                weights_(2)
                weights_(3)

            def c_neg(n):
                at = 16 + n % 2 * 4 + n // 2 * 2
                return q_scale[:, 1, at:at + 2]

            four(lambda n: pair_bias("c", n, c_neg(n)), lambda n: pair_weights("c", n, c_prob))
            for hh in range(4):
                copy(f"co_{hh}", coT[:, hh * 512:hh * 512 + 512])
            add_to_h("co")

            dve.wait_ge(params_landed, 16 * N_PARAMS)
            in_order(dve, row_squared, ROW_NORMS, "h2")
            mean("h2", D)
            wait_rstd(dve, "h2")
            _, lo, _ = NORM_AT["h2"]
            for t in range(TT):
                v.scalar_tensor_tensor(normed[:, t, :], h[:, t, :], rstd[:, lo + t:lo + t + 1],
                                       wide_gain[:, :], ALU.mult, ALU.mult).then_inc(normed_ready, 1)
            for c2 in (1, 3):
                copy(f"h2T{c2}", uT_chunks(c2))

            NG, NE = N_GROUPS, N_EXPERTS
            lg_b = wait_filled(dve, "logits")[:, 0:TT * (NG + NE)].rearrange("p (t e) -> p t e", t=TT)
            rc = Carver(rt, 0, 512)

            def small(w):
                return rc.take(TT * w).rearrange("p (t e) -> p t e", t=TT)

            def wide(x, w):
                return x.broadcast_to([P, TT, w])

            def all_tiles(x):
                return x.rearrange("p (o e) -> p o e", o=1).broadcast_to([P, TT, x.shape[1]])

            lg = small(NG + NE)
            done("logits", v.tensor_tensor(lg, lg_b, all_tiles(b_router[:, :]), ALU.add))
            wait_drained(dve, "logits")

            def one_hot_max(values, numbers, w, out_max, out_hot, tmp):
                link(v.tensor_reduce(out_max, values, axis=X, op=ALU.max))
                link(v.tensor_tensor(tmp, values, wide(out_max, w), ALU.is_lt))
                link(v.scalar_tensor_tensor(tmp, tmp, 1000.0, all_tiles(numbers), ALU.mult, ALU.add))
                link(v.tensor_reduce(first, tmp, axis=X, op=ALU.min))
                link(v.tensor_tensor(out_hot, all_tiles(numbers), wide(first, w), ALU.is_equal))

            first = small(1)
            g_max, g_hot, g_tmp = small(1), small(NG), small(NG)
            one_hot_max(lg[:, :, 0:NG], expert_no[:, 0:NG], NG, g_max, g_hot, g_tmp)
            e_val, e_tmp = small(NE), small(NE)
            hot1, hot2 = small(NE), small(NE)
            for t in range(TT):
                gh = g_hot[:, t, :].rearrange("p (g o) -> p g o", o=1).broadcast_to([P, NG, PER_GROUP])
                ev = e_val[:, t, :].rearrange("p (g e) -> p g e", g=NG)
                et = e_tmp[:, t, :].rearrange("p (g e) -> p g e", g=NG)
                v.tensor_scalar(et, gh, BIG, -BIG, ALU.mult, ALU.add)
                last = v.tensor_tensor(ev, lg[:, t, NG:].rearrange("p (g e) -> p g e", g=NG), gh, ALU.mult)
            link(last)
            link(v.tensor_tensor(e_val, e_val, e_tmp, ALU.add))
            m1, m2 = small(1), small(1)
            one_hot_max(e_val, expert_no[:, :], NE, m1, hot1, e_tmp)
            link(v.scalar_tensor_tensor(e_val, hot1, -3.0 * BIG, e_val, ALU.mult, ALU.add))
            one_hot_max(e_val, expert_no[:, :], NE, m2, hot2, e_tmp)
            v.tensor_tensor(rt_exp[:, :, 0:NG], lg[:, :, 0:NG], wide(g_max, NG), ALU.subtract)
            link(v.tensor_tensor(rt_exp[:, :, NG:NG + 1], m2, m1, ALU.subtract))
            v.tensor_tensor(assigned[:, :, :], hot1, hot2, ALU.add).then_inc(router_step, 1)
            copy("xv2_0", xv2[:, 0:512])
            dve.wait_ge(router_exp, 1)
            g_sum, w_sum = small(1), small(1)
            v.tensor_reduce(g_sum, rt_exp[:, :, 0:NG], axis=X, op=ALU.add)
            link(v.tensor_scalar(w_sum, rt_exp[:, :, NG:NG + 1], 1.0, None, ALU.add))
            link(v.tensor_tensor(g_sum, g_sum, w_sum, ALU.mult))
            link(v.reciprocal(g_sum, g_sum))
            link(v.tensor_tensor(w_sum, g_sum, rt_exp[:, :, NG:NG + 1], ALU.mult))
            v.tensor_tensor(hot1, hot1, wide(g_sum, NE), ALU.mult)
            link(v.tensor_tensor(hot2, hot2, wide(w_sum, NE), ALU.mult))
            link(v.tensor_tensor(gates[:, :, :], hot1, hot2, ALU.add))
            rk = wait_filled(dve, "rank")
            link(v.scalar_tensor_tensor(rank1[:, :, :], rk[:, 0:TT * NE].rearrange("p (t e) -> p t e", t=TT),
                                        1.0, assigned[:, :, :], ALU.add, ALU.mult))
            link(v.tensor_reduce(most[:, :], rk[:, TT * NE:(TT + 1) * NE], axis=X, op=ALU.max))
            done("rank", v.tensor_scalar(over_flag[:, :], most[:, :], float(CAP), None, ALU.is_gt))
            wait_drained(dve, "rank")
            mark(router_step, 1)

            rank_flat = rank1[:, :, :].rearrange("p t e -> p (t e)")
            gate_flat = gates[:, :, :].rearrange("p t e -> p (t e)")

            def select_slots(S, i):
                for t in range(TT):
                    for e in range(2):
                        lo = (2 * t + e) * CAP
                        col = bass.ds(i * 2 + (t * N_EXPERTS + e), 1)
                        last = v.tensor_scalar(select[:, lo:lo + CAP], slot_no[:, :], rank_flat[:, col], None,
                                               ALU.is_equal)
                last.then_inc(S.select_ready, 1)

            def select_gates(S, i):
                for t in range(TT):
                    for e in range(2):
                        lo = (2 * t + e) * CAP
                        col = bass.ds(i * 2 + (t * N_EXPERTS + e), 1)
                        last = v.tensor_scalar(select_g[:, lo:lo + CAP], slot_no[:, :], rank_flat[:, col],
                                               gate_flat[:, col], ALU.is_equal, ALU.mult)
                last.then_inc(S.gates_ready, 1)

            def hidden(S, n):
                dve.wait_ge(S.tanh_ready, n + 1)
                v.scalar_tensor_tensor(half_h, tanh_g, 1.0, bank[2][:, :], ALU.add, ALU.mult)\
                    .then_inc(S.half_ready, 1)
                dve.wait_ge(S.half_ready, n + 1)
                dve.wait_ge(S.hidden_psum, n * 2 + 2)
                v.scalar_tensor_tensor(hid, half_h, 0.5, bank[3][:, :], ALU.mult, ALU.mult)\
                    .then_inc(S.hidden_ready, 1)

            def gathered_high(S, n):
                dve.wait_ge(S.gathered, n + 1)
                v.tensor_copy(xgT[:, 512:1024], bank[1][:, :]).then_inc(S.hi_drained, 1)

            def add_outputs(S, n):
                for t in range(TT):
                    for half in range(2):
                        dve.wait_ge(S.scattered, n * 4 + (2 * t + half + 1))
                        b = bank[(6, 2)[t] + half]
                        hs = h[:, t, half * 512:half * 512 + 512]
                        v.tensor_tensor(hs, b[:, :], hs, ALU.add).then_inc(S.added, 1)

            select_slots(main_s, 0)
            copy("xv2_1", xv2[:, 512:1024])
            select_gates(main_s, 0)
            mark(main_s.added, 4)
            gathered_high(main_s, 0)
            with dve.Fori(0, PAIRS - 1) as i:
                dve.wait_ge(main_s.gathered, i + 1)
                select_slots(main_s, i + 1)
                dve.wait_ge(main_s.gate_psum, i + 1)
                select_gates(main_s, i + 1)
                hidden(main_s, i)
                gathered_high(main_s, i + 1)
                add_outputs(main_s, i)
            hidden(main_s, PAIRS - 1)
            add_outputs(main_s, PAIRS - 1)
            over = dve.value_load(over_flag[0:1, 0:1], min_val=0, max_val=1)
            with dve.If(over):
                mark(more_s.added, 4)
                with dve.Fori(0, MORE_ROUNDS) as r:
                    with dve.Fori(0, PAIRS) as i:
                        n = r * PAIRS + i
                        pair_ranks = rank1[:, :, bass.ds(i * 2, 2)]
                        v.tensor_scalar(pair_ranks, pair_ranks, -float(CAP), None, ALU.add)\
                            .then_inc(more_s.ranks_shifted, 1)
                        dve.wait_ge(more_s.ranks_shifted, n + 1)
                        select_slots(more_s, i)
                        select_gates(more_s, i)
                        gathered_high(more_s, n)
                        hidden(more_s, n)
                        add_outputs(more_s, n)
            mark(after_experts, 1)
            dve.wait_ge(main_s.added, 4 * PAIRS + 4)

            scale_rows("h3", h, normed)
            norm_T("h3", uT_chunks, "g_in_2")

            def rope_heads(src, dst, t, heads):
                s3 = src.rearrange("p (h d) -> p h d", d=HD)
                d3 = dst.rearrange("p (h d) -> p h d", d=HD)
                t3 = rope_t[:, 0:heads * HD].rearrange("p (h d) -> p h d", d=HD)
                half = HD // 2

                def table(lo, w):
                    return rope[:, t, lo:lo + w].rearrange("p (o d) -> p o d", o=1)\
                        .broadcast_to([P, heads, w])
                v.tensor_tensor(d3, s3, table(0, HD), ALU.mult)
                v.tensor_tensor(t3[:, :, 0:half], s3[:, :, half:HD], table(HD, half), ALU.mult)
                last = v.tensor_tensor(t3[:, :, half:HD], s3[:, :, 0:half], table(HD + half, half), ALU.mult)
                return last, lambda: v.tensor_tensor(d3, d3, t3, ALU.add)

            def rope_tensor(name, dst):
                for t in range(TT):
                    src = wait_filled(dve, f"{name}_{t}")
                    last, finish = rope_heads(src[:, :], dst[:, t * 512:t * 512 + 512], t, H2)
                    done(f"{name}_{t}", last)
                    wait_drained(dve, f"{name}_{t}")
                    if t == 0:
                        link(finish())
                    else:
                        finish().then_inc(roped, 1)
                        in_order(dve, roped, ROPED, name)

            rope_tensor("iq", iq_tok)
            src = wait_filled(dve, "ikw")
            for t in range(TT):
                lo = t * (HD + H2)
                v.tensor_scalar(iw[:, t, :], src[:, lo + HD:lo + HD + H2], H2 ** -0.5, None, ALU.mult)
                last, finish = rope_heads(src[:, lo:lo + HD], ik_tok[:, t * P:t * P + HD], t, 1)
                if t:
                    done("ikw", last)
                    wait_drained(dve, "ikw")
                else:
                    link(last)
                link(finish())
            ik3 = ik_tok.rearrange("p (t two d) -> p t two d", t=TT, two=2)
            v.tensor_copy(ik3[:, :, 1, :], ik3[:, :, 0, :]).then_inc(roped, 1)
            rope_tensor("dq2", dq2_tok)
            rope_tensor("dk2", dk2_tok)

            def score_bank(name):
                n = RELUS.index(name)
                t, part = int(name[2]), int(name[4])
                w = (t + 1) * P
                heads = 512 // w
                wait_drained(dve, name)
                dst = score[:, t * P:t * P + w]
                for i in range(heads):
                    hh = part * heads + i
                    lo = n % 2 * 512 + i * w
                    wcol = iw[:, t, hh:hh + 1]
                    if hh == 0:
                        link(v.tensor_scalar(dst, relu[:, lo:lo + w], wcol, None, ALU.mult))
                    else:
                        ins = v.scalar_tensor_tensor(dst, relu[:, lo:lo + w], wcol, dst, ALU.mult, ALU.add)
                        if i == heads - 1:
                            ins.then_inc(scored, 1)
                            dve.wait_ge(scored, n + 1)
                        else:
                            link(ins)

            score_bank("il0_0")
            score_bank("il0_1")
            rope_tensor("mq", mq_tok)
            for name in RELUS[2:]:
                score_bank(name)
            rope_tensor("mk", mk_tok)

            def pick_keys(t):
                w = (t + 1) * P
                sc = score[:, t * P:t * P + w]
                wk = work[:, 0:w]
                link(v.tensor_tensor(sc[:, t * P:w], sc[:, t * P:w], causal_b[:, :], ALU.add))
                for step in range(DSA_TOPK // 8):
                    src = wk if step else sc
                    link(v.max(out=best8, in_=src))
                    link(v.match_replace(out=wk, in_to_replace=best8, in_values=src, imm_value=-3e38))
                link(v.tensor_tensor(wk, wk, sc, ALU.is_equal))
                dst = sel_b[:, t * P:t * P + w]
                if t:
                    v.tensor_scalar(dst[:, 0:P], wk[:, 0:P], NEG, None, ALU.mult)
                v.scalar_tensor_tensor(dst[:, t * P:w], wk[:, t * P:w], NEG, causal_b[:, :], ALU.mult,
                                       ALU.add).then_inc(selected, 1)
                dve.wait_ge(selected, t + 1)

            def head_bias(kind, pair):
                s0 = wait_filled(dve, f"{kind}s0_{pair}")[:, 0:2 * P]
                s1 = wait_filled(dve, f"{kind}s1_{pair}")
                soft_bias(f"{kind}{pair}", [(s0.rearrange("p (h k) -> p h k", h=2), 0, 2),
                                            (s1[:, :].rearrange("p (h k) -> p h k", h=2), 2, 2)],
                          lambda x: x, -(HD ** -0.5))

            def head_weights(kind, pair):
                at = soft_inverse(f"{kind}{pair}", 4, f"{kind}s1_{pair}")
                for n in range(2):
                    for t in range(TT):
                        lo, w = n * 384 + t * P, (t + 1) * P
                        pr = probs[:, lo:lo + w]
                        last = v.tensor_scalar(pr, pr, inv[:, at + 2 * t + n:at + 2 * t + n + 1], None,
                                               ALU.mult)
                last.then_inc(probs_ready, 1)

            def gated_out(name, dst, gate):
                src = wait_filled(dve, name)
                done(name, v.scalar_tensor_tensor(dst, src[:, 0:T], 0.5, gate, ALU.mult, ALU.mult))

            for t in range(TT):
                pick_keys(t)
            gate_of = {"mg": mgate, "dg": dgate, "xg": xgate}
            heads_of = {"m": (ya, mgate), "s": (yb, dgate)}

            def finish_pair(kind, pair):
                y, gate = heads_of[kind]
                at = slice(pair * T, (pair + 1) * T)
                gated_out(f"{kind}o{pair}", y[:, at], gate[:, at])

            for kind in "ms":
                head_bias(kind, 0)
                for pair in range(4):
                    head_weights(kind, pair)
                    for b in attention_fillers(kind)[pair]:
                        if b in gate_of:
                            for half in range(2):
                                silu_gate(f"{b}_{half}", gate_of[b][:, half * 512:half * 512 + 512])
                            wait_drained(dve, f"{b}_1")
                    if pair < 3:
                        head_bias(kind, pair + 1)
                    finish_pair(kind, pair)
            four(lambda n: pair_bias("x", n, -(X2_D ** -0.5)), lambda n: pair_weights("x", n, x_prob))
            for hh in range(4):
                at = slice(hh * T, (hh + 1) * T)
                gated_out(f"xo_{hh}", yc[:, at], xgate[:, at])

            for b in range(3):
                for c in range(4):
                    name = f"up{b}_{c}"
                    src = wait_filled(dve, name)
                    chunk = b * KC + 2 * c
                    gate = branch_gate[:, chunk * T:(chunk + 2) * T]
                    if b == 0:
                        if c == 0:
                            wait_drained(dve, "gl5_1")
                        done(name, v.scalar_tensor_tensor(uT_chunks(c), gate, 1.0, src[:, :], ALU.add,
                                                          ALU.mult))
                    else:
                        done(name, v.scalar_tensor_tensor(up_t, gate, 1.0, src[:, :], ALU.add, ALU.mult))
                        wait_drained(dve, name)
                        link(v.tensor_tensor(uT_chunks(c), uT_chunks(c), up_t, ALU.add))
            mark(after_experts, 1)
            add_to_h("out", 0.5)
            in_order(dve, row_squared, ROW_NORMS, "final")
            mean("final", D)
            wait_rstd(dve, "final")
            dve.wait_ge(final_gain_landed, 16)
            _, lo, _ = NORM_AT["final"]
            for t in range(TT):
                v.scalar_tensor_tensor(normed[:, t, :], h[:, t, :], rstd[:, lo + t:lo + t + 1],
                                       wide_gain[:, :], ALU.mult, ALU.mult).then_inc(out_ready, 1)

        @block.tensor
        def _(pe):
            mm = nc.tensor.matmul
            then_upper = chain(pe, rows_switched)
            pe.wait_ge(consts_made, 6)
            pe.wait_ge(rows_landed, 16 * (len(COLS) + 2))

            def transpose(dst, src):
                k = src.shape[0]
                return nc.tensor.transpose(dst, src, ident[0:k, 0:k])

            def as_chunks(x):
                return x.rearrange("p (c t) -> p c t", t=T)

            def as_tiles(x):
                return x.rearrange("p (t d) -> p t d", t=TT)

            def turn(names, src, needs=()):
                for c2, name in enumerate(names):
                    b = wait_free(name)
                    for c in range(2):
                        for t in range(TT):
                            last = transpose(b[:, c * T + t * P:c * T + t * P + P],
                                             src[:, t, (2 * c2 + c) * P:(2 * c2 + c + 1) * P])
                    full(name, last)

            def turn_normed(prefix, src):
                pe.wait_ge(normed_ready, 2 * ROW_NORMS.index(prefix) + 2)
                turn([f"{prefix}T{c}" for c in range(4)], src)

            def wait_turned(prefix, n=4):
                for c in range(n):
                    wait_drained(pe, f"{prefix}{c}")

            def moving(name, xT, tiles=range(TT)):
                w = weights(name)
                for t in tiles:
                    b = wait_free(f"{name}_{t}")
                    for k in range(KC):
                        last = mm(b[:, :], xT[:, k, t * P:(t + 1) * P], w[:, k, :], start=k == 0,
                                  stop=k == KC - 1)
                    full(f"{name}_{t}", last)

            def standing(name, xT, uses=None, halves=range(2)):
                w = weights(name)
                for half in halves:
                    use = uses[half] if uses else f"{name}_{half}"
                    b = wait_free(use)
                    for c in range(2):
                        chunk = 2 * half + c
                        for k in range(KC):
                            last = mm(b[:, c * T:(c + 1) * T], w[:, k, chunk * P:(chunk + 1) * P],
                                      xT[:, k, :], start=k == 0, stop=k == KC - 1)
                    full(use, last)

            b = wait_free("cols")
            full("cols", transpose(b[:, 0:N_COLS], rows[0:N_COLS, :]))
            turn_normed("x", normed)
            wait_turned("xT")
            pe.wait_ge(gates_landed, 16 * 2)
            b = wait_free("grT")
            for k in range(KC):
                last = mm(b[0:16, 0:T], w_gr[:, k, :], uT[:, k, :], start=k == 0, stop=k == KC - 1)
            full("grT", last)
            standing("gqk", uT, ["gqk0", "gqk1"])
            wait_drained(pe, "grT")
            b = wait_free("z")
            for pair in range(2):
                last = mm(b[:, pair * T:(pair + 1) * T], gate_w[:, pair * P:(pair + 1) * P], grT[:, :],
                          start=True, stop=True)
            full("z", last)
            moving("gv", uT)
            moving("dq", uT)
            moving("dk", uT)
            turn_normed("mem", as_tiles(mix))
            gp, gn = as_chunks(q_pos), as_chunks(q_neg)
            kp, kn = as_chunks(k_pos), as_chunks(k_neg)
            pe.wait_ge(gla_vec, 4)
            b = wait_free("kdT")
            for t in range(TT):
                for pair in range(2):
                    lo = (2 * t + pair) * P
                    last = transpose(b[:, lo:lo + P], as_chunks(k_dec)[:, pair, t * P:(t + 1) * P])
            full("kdT", last)
            for t in range(TT):
                at = slice(t * P, (t + 1) * P)
                for name, k_, q_ in ((f"past{t}", kn, gp), (f"fut{t}", kp, gn)):
                    b = wait_free(name)
                    for hh in (0, 2, 1, 3):
                        on = slice(DA_D * (hh % 2), DA_D * (hh % 2) + DA_D)
                        last = mm(b[:, hh * P:(hh + 1) * P], k_[on, hh // 2, at], q_[on, hh // 2, at],
                                  start=True, stop=True)
                        if hh == 2:
                            then_upper(last)
                    full(name, last)
            wait_drained(pe, "kdT")
            for t in range(TT):
                wait_drained(pe, f"gv_{t}")
            kd4 = k_decT.rearrange("p (t r d) -> p t r d", t=TT, r=2)
            gv3 = as_tiles(gv)
            for name, chunks in (("u01", (0, 1)), ("u2", (2,))):
                b = wait_free(name)
                for ch in chunks:
                    on = slice(GLA_CHUNK * (ch % 2), GLA_CHUNK * (ch % 2) + GLA_CHUNK)
                    for hh in range(H1):
                        o = DA_D * (hh % 2)
                        lo = (ch % 2) * 256 * (name == "u01") + hh // 2 * P
                        last = mm(b[o:o + DA_D, lo:lo + P], kd4[on, ch // 2, hh // 2, o:o + DA_D],
                                  gv3[on, ch // 2, hh * DV:(hh + 1) * DV], start=True, stop=True)
                    if ch == 0:
                        then_upper(last)
                full(name, last)
            wait_turned("memT")
            memT3 = as_chunks(memT)
            moving("ck0", memT3)
            moving("ck1", memT3)
            for t in range(TT):
                wait_drained(pe, f"fut{t}")
            wait_drained(pe, "u2")
            st4 = states.rearrange("p (c r d) -> p c r d", c=3, r=2)
            qL = as_chunks(q_L)
            for t in range(TT):
                b = wait_free(f"og{t}")
                for hh in range(H1):
                    out_at = slice(hh * DV, (hh + 1) * DV)
                    mm(b[:, out_at], aT[:, t * 512 + hh * P:t * 512 + hh * P + P], gv3[:, t, out_at],
                       start=hh == 0, stop=True, skip_group_check=True)
                for hh in (0, 2, 1, 3):
                    out_at = slice(hh * DV, (hh + 1) * DV)
                    on = slice(DA_D * (hh % 2), DA_D * (hh % 2) + DA_D)
                    for half in range(2):
                        ch = 2 * t + half
                        if ch:
                            o = GLA_CHUNK * half
                            last = mm(b[o:o + GLA_CHUNK, out_at],
                                      qL[on, hh // 2, ch * GLA_CHUNK:(ch + 1) * GLA_CHUNK],
                                      st4[on, ch - 1, hh // 2, :], start=False, stop=True,
                                      skip_group_check=True)
                    if hh == 2:
                        then_upper(last)
                full(f"og{t}", last)
            pe.wait_ge(keys_normed, 1)
            wait_drained(pe, "dq_1")
            turn(["dqT0", "dqT1"], as_tiles(dq_tok))
            turn(["dkT0", "dkT1"], as_tiles(dk_tok))
            moving("cv0", memT3)
            moving("cv1", memT3)
            pe.wait_ge(keys_normed, 2)
            turn([f"ckT{c}" for c in range(4)], as_tiles(ck_tok))
            moving("dv", uT)
            wait_turned("dqT", 2)
            wait_turned("dkT", 2)
            q4, k4 = as_chunks(dqT), as_chunks(dkT)
            dv3 = as_tiles(dv)

            def mask_add(dst, m):
                return mm(dst, ident_b[:, :], m, start=False, stop=True, skip_group_check=True)

            def d_scores0(hh):
                b = wait_free(f"ds0_{hh}")
                for s in range(2):
                    on = slice(DA_D * s, DA_D * s + DA_D)
                    last = mm(b[:, s * P:(s + 1) * P], q4[on, hh, 0:P], k4[on, hh, 0:P], start=s == 0, stop=True,
                              skip_group_check=True)
                    if s == 0:
                        then_upper(last)
                for s in range(2):
                    last = mask_add(b[:, s * P:(s + 1) * P], chunks_b[:, :])
                full(f"ds0_{hh}", last)

            def d_scores1(hh):
                b = wait_free(f"ds1_{hh}")
                for s in range(2):
                    on = slice(DA_D * s, DA_D * s + DA_D)
                    last = mm(b[:, s * T:(s + 1) * T], q4[on, hh, P:T], k4[on, hh, :], start=s == 0, stop=True,
                              skip_group_check=True)
                    if s == 0:
                        then_upper(last)
                for s in range(2):
                    last = mask_add(b[:, s * T + P:(s + 1) * T], chunks_b[:, :])
                full(f"ds1_{hh}", last)

            def three_blocks(name, pr):
                b = wait_free(name)
                for n in range(3):
                    last = transpose(b[:, n * P:(n + 1) * P], pr[:, n * P:(n + 1) * P])
                full(name, last)

            def d_out(hh):
                in_order(pe, probs_ready, SOFTMAXES, f"d{hh}")
                three_blocks(f"dpT{hh}", d_prob[hh % 2])
                wait_drained(pe, f"dpT{hh}")
                b = wait_free(f"do{hh}")
                at = slice(hh * DV, (hh + 1) * DV)
                mm(b[:, 0:P], d_pT[:, 0:P], dv3[:, 0, at], start=True, stop=True)
                mm(b[:, P:2 * P], d_pT[:, P:2 * P], dv3[:, 0, at], start=True, stop=False)
                full(f"do{hh}", mm(b[:, P:2 * P], d_pT[:, 2 * P:3 * P], dv3[:, 1, at], start=False, stop=True))

            pe.wait_ge(masks_cast, 4)
            for hh in (0, 1):
                d_scores0(hh)
                d_scores1(hh)
            moving("gg", uT)
            d_scores0(2)
            d_scores1(2)
            for t in range(TT):
                wait_drained(pe, f"dv_{t}")
            d_out(0)
            d_scores0(3)
            d_scores1(3)
            for hh in (1, 2, 3):
                d_out(hh)
            pe.wait_ge(mix_ready, 2)
            turn([f"mixT{c}" for c in range(4)], as_tiles(mix))
            wait_turned("mixT")
            moving("wo0", as_chunks(mixT))
            moving("wo1", as_chunks(mixT))
            turn_normed("h1", normed)
            wait_turned("h1T")
            moving("cq0", uT)
            moving("cq1", uT)
            wait_drained(pe, "cq0_1")
            wait_drained(pe, "cq1_1")
            turn([f"cqT{c}" for c in range(4)], as_tiles(cq_tok))
            turn_normed("mem2", as_tiles(mem2_tok))
            wait_turned("cqT")
            wait_turned("ckT")
            cq3, ck3, cv3 = as_chunks(cqT), as_chunks(ckT), as_tiles(cv)
            for hp in range(2):
                for t in range(TT):
                    b = wait_free(f"cs{t}_{hp}")
                    for n in range(2):
                        for k in range(2):
                            c = 2 * (2 * hp + n) + k
                            last = mm(b[:, n * T:(n + 1) * T], cq3[:, c, t * P:(t + 1) * P], ck3[:, c, :],
                                      start=k == 0, stop=k == 1)
                    full(f"cs{t}_{hp}", last)
            wait_turned("mem2T")
            standing("xk2", as_chunks(mem2T), halves=[0])

            def four_blocks(name, buffers, hh):
                b = wait_free(name)
                for kt in range(TT):
                    for t in range(TT):
                        lo = hh % 2 * T + kt * P
                        last = transpose(b[:, kt * T + t * P:kt * T + t * P + P],
                                         buffers[t + hh // 2 * 2][:, lo:lo + P])
                full(name, last)

            for hh in range(H1):
                if hh % 2 == 0:
                    in_order(pe, probs_ready, SOFTMAXES, f"c{hh + 1}")
                four_blocks(f"cpT{hh}", c_prob, hh)
                wait_drained(pe, f"cpT{hh}")
                b = wait_free(f"co_{hh}")
                for c in range(2):
                    for kt in range(TT):
                        lo = hh * CROSS_D + c * P
                        last = mm(b[:, c * T:(c + 1) * T], cv3[:, kt, lo:lo + P],
                                  c_pT[hh % 2][:, kt * T:(kt + 1) * T], start=kt == 0, stop=kt == 1)
                full(f"co_{hh}", last)
            for hh in range(H1):
                wait_drained(pe, f"co_{hh}")
            moving("co0", as_chunks(coT))
            moving("co1", as_chunks(coT))
            standing("xk2", as_chunks(mem2T), halves=[1])
            turn_normed("h2", normed)
            wait_turned("h2T")
            pe.wait_ge(params_landed, 16 * N_PARAMS)
            b = wait_free("logits")
            NE = N_EXPERTS
            w = N_GROUPS + NE
            for t in range(TT):
                for k in range(KC):
                    last = mm(b[:, t * w:(t + 1) * w], uT[:, k, t * P:(t + 1) * P], w_router[:, k, :],
                              start=k == 0, stop=k == KC - 1)
            full("logits", last)
            moving("xv2", as_chunks(mem2T), [0])
            pe.wait_ge(router_step, 1)
            b = wait_free("rank")
            mm(b[:, 0:NE], earlier[:, :], assigned[:, 0, :], start=True, stop=True)
            mm(b[:, NE:2 * NE], ones[:, :], assigned[:, 0, :], start=True, stop=False)
            mm(b[:, NE:2 * NE], earlier[:, :], assigned[:, 1, :], start=False, stop=True)
            mm(b[:, 2 * NE:3 * NE], ones[:, :], assigned[:, 0, :], start=True, stop=False)
            full("rank", mm(b[:, 2 * NE:3 * NE], ones[:, :], assigned[:, 1, :], start=False, stop=True))
            moving("xv2", as_chunks(mem2T), [1])
            for name in PSUM_PLAN[FIRST_USES - 8:FIRST_USES]:
                wait_drained(pe, name)

            sel3, selg3 = as_tiles(select), as_tiles(select_g)
            xg3 = xgT.rearrange("p (k s) -> p k s", k=KC)
            hidT3 = hidT.rearrange("p (c s) -> p c s", c=FC)

            def gather(S, n):
                pe.wait_ge(S.select_ready, n + 1)
                for k in range(KC):
                    dst = bank[k // 4][:, k % 4 * P:k % 4 * P + P]
                    for t in range(TT):
                        last = mm(dst, normed[:, t, k * P:(k + 1) * P], sel3[:, t, :], start=t == 0,
                                  stop=t == TT - 1)
                last.then_inc(S.gathered, 1)

            def experts(S, n, expert_landed):
                pe.wait_ge(S.gates_ready, n + 1)
                pe.wait_ge(S.y_ready, n + 1)
                for t in range(TT):
                    last = transpose(bank[4][:, t * P:(t + 1) * P], selg3[:, t, :])
                last.then_inc(S.gate_psum, 1)
                pe.wait_ge(S.lo_drained, n + 1)
                pe.wait_ge(S.hi_drained, n + 1)
                for part in range(2):
                    pe.wait_ge(S.added, n * 4 + (3 + part))
                    expert_landed(4 * part)
                    expert_landed(4 * part + 1)
                    for k in range(KC):
                        for e in range(2):
                            on = slice(e * CAP, (e + 1) * CAP)
                            last = mm(bank[2 + part][on, :], xg3[:, k, on], slot(4 * part + e)[:, k, :],
                                      start=k == 0, stop=k == KC - 1)
                    last.then_inc(S.hidden_psum, 1)
                pe.wait_ge(S.hidden_ready, n + 1)
                for c in range(FC):
                    last = transpose(bank[0][:, c * P:(c + 1) * P], hid[:, c * P:(c + 1) * P])
                last.then_inc(S.hidden_turned, 1)
                pe.wait_ge(S.gate_ready, n + 1)
                pe.wait_ge(S.hidT_ready, n + 1)
                expert_landed(2)
                expert_landed(3)
                for half in range(2):
                    for c in range(FC):
                        for e in range(2):
                            on = slice(e * CAP, (e + 1) * CAP)
                            last = mm(bank[4 + half][on, :], hidT3[:, c, on],
                                      slot(2 + e, FC)[:, c, half * 512:half * 512 + 512],
                                      start=c == 0, stop=c == FC - 1)
                    last.then_inc(S.down_done, 1)

            def scatter(S, n):
                pe.wait_ge(S.y_ready, n + 2)
                for t in range(TT):
                    for half in range(2):
                        mm(bank[(6, 2)[t] + half][:, :], gate_mat[:, t * P:(t + 1) * P],
                           y_slots[:, half * 512:half * 512 + 512], start=True, stop=True)\
                            .then_inc(S.scattered, 1)

            def main_landed(i):
                def wait(j):
                    pe.wait_ge(landed[j], i * 16 + 16 * (FIRST_IN_SLOT[j] + 1))
                return wait

            gather(main_s, 0)
            with pe.Fori(0, PAIRS - 1) as i:
                experts(main_s, i, main_landed(i))
                gather(main_s, i + 1)
                scatter(main_s, i)
            experts(main_s, PAIRS - 1, main_landed(PAIRS - 1))
            scatter(main_s, PAIRS - 1)
            pe.wait_ge(main_s.added, 4 * PAIRS + 4)
            pe.wait_ge(router_step, 2)
            over = pe.value_load(over_flag[0:1, 0:1], min_val=0, max_val=1)
            with pe.If(over):
                with pe.Fori(0, MORE_ROUNDS * PAIRS) as n:
                    gather(more_s, n)
                    experts(more_s, n, lambda j: pe.wait_ge(more_s.weights, n * 96 + 96))
                    scatter(more_s, n)
                pe.wait_ge(more_s.added, 4 * MORE_ROUNDS * PAIRS + 4)

            turn_normed("h3", normed)
            wait_turned("h3T")
            moving("iq", uT)
            b = wait_free("ikw")
            for t in range(TT):
                w = HD + H2
                for k in range(KC):
                    last = mm(b[:, t * w:(t + 1) * w], uT[:, k, t * P:(t + 1) * P], w_ikw[:, k, :],
                              start=k == 0, stop=k == KC - 1)
            full("ikw", last)
            moving("dq2", uT)
            moving("dk2", uT)
            in_order(pe, roped, ROPED, "ik")
            turn(["iqT0", "iqT1"], as_tiles(iq_tok))
            b = wait_free("ikT")
            for t in range(TT):
                last = transpose(b[:, t * P:(t + 1) * P], ik_tok[:, t * P:(t + 1) * P])
            full("ikT", last)
            moving("dv2", uT)
            wait_turned("iqT", 2)
            wait_drained(pe, "ikT")
            iq3 = as_chunks(iqT)

            def index_scores(name):
                t, part = int(name[2]), int(name[4])
                w = (t + 1) * P
                heads = 512 // w
                b = wait_free(name)
                for i in [*range(0, heads, 2), *range(1, heads, 2)]:
                    hh = part * heads + i
                    on = slice(HD * (hh % 2), HD * (hh % 2) + HD)
                    last = mm(b[:, i * w:(i + 1) * w], iq3[on, hh // 2, t * P:(t + 1) * P], ikT[on, 0:w],
                              start=True, stop=True)
                    if i == heads - 2:
                        then_upper(last)
                full(name, last)

            index_scores("il0_0")
            index_scores("il0_1")
            moving("mq", uT)
            index_scores("il1_0")
            index_scores("il1_1")
            moving("mk", uT)
            index_scores("il1_2")
            index_scores("il1_3")
            moving("mv", uT)
            in_order(pe, roped, ROPED, "dk2")
            turn(["dqT2_0", "dqT2_1"], as_tiles(dq2_tok))
            turn(["dkT2_0", "dkT2_1"], as_tiles(dk2_tok))
            in_order(pe, roped, ROPED, "mk")
            turn(["mqT0", "mqT1"], as_tiles(mq_tok))
            turn(["mkT0", "mkT1"], as_tiles(mk_tok))

            def attention(kind, qT, kT, v3):
                q3, k3 = as_chunks(qT), as_chunks(kT)

                def scores0(pair):
                    b = wait_free(f"{kind}s0_{pair}")
                    for n in range(2):
                        on = slice(HD * n, HD * n + HD)
                        last = mm(b[:, n * P:(n + 1) * P], q3[on, pair, 0:P], k3[on, pair, 0:P],
                                  start=n == 0, stop=True, skip_group_check=True)
                        if n == 0:
                            then_upper(last)
                    for n in range(2):
                        last = mask_add(b[:, n * P:(n + 1) * P],
                                        causal_b[:, :] if kind == "m" else sel_b[:, 0:P])
                    full(f"{kind}s0_{pair}", last)

                def scores1(pair):
                    b = wait_free(f"{kind}s1_{pair}")
                    for n in range(2):
                        on = slice(HD * n, HD * n + HD)
                        last = mm(b[:, n * T:(n + 1) * T], q3[on, pair, P:T], k3[on, pair, :],
                                  start=n == 0, stop=True, skip_group_check=True)
                        if n == 0:
                            then_upper(last)
                    for n in range(2):
                        if kind == "m":
                            last = mask_add(b[:, n * T + P:(n + 1) * T], causal_b[:, :])
                        else:
                            last = mask_add(b[:, n * T:(n + 1) * T], sel_b[:, P:P + T])
                    full(f"{kind}s1_{pair}", last)

                scores0(0)
                scores1(0)
                for pair in range(4):
                    if pair < 3:
                        scores0(pair + 1)
                        scores1(pair + 1)
                    for b in attention_fillers(kind)[pair]:
                        standing(b, uT)
                    in_order(pe, probs_ready, SOFTMAXES, f"{kind}{pair}")
                    for n in range(2):
                        three_blocks(f"{kind}pT{2 * pair + n}", probs[:, n * 384:n * 384 + 384])
                    b = wait_free(f"{kind}o{pair}")
                    for n in range(2):
                        wait_drained(pe, f"{kind}pT{2 * pair + n}")
                        o, lo, pT = HD * n, (2 * pair + n) * HD, n * 384
                        mm(b[o:o + HD, 0:T], v3[:, 0, lo:lo + HD], probT[:, pT:pT + T], start=True, stop=False)
                        last = mm(b[o:o + HD, P:T], v3[:, 1, lo:lo + HD], probT[:, pT + T:pT + T + P],
                                  start=False, stop=True)
                    full(f"{kind}o{pair}", last)

            for c in range(2):
                wait_drained(pe, f"mqT{c}")
                wait_drained(pe, f"mkT{c}")
            wait_drained(pe, "mv_1")
            attention("m", mqT, mkT, as_tiles(mv))
            for c in range(2):
                wait_drained(pe, f"dqT2_{c}")
                wait_drained(pe, f"dkT2_{c}")
            wait_drained(pe, "dv2_1")
            pe.wait_ge(selected, 2)
            attention("s", dq2T, dk2T, as_tiles(dv2))

            xq3, xk3, xv3 = as_chunks(xqT), as_chunks(xkT), as_tiles(xv2)
            for c in range(2):
                wait_drained(pe, f"xq_{c}")
                wait_drained(pe, f"xk2_{c}")
                wait_drained(pe, f"xv2_{c}")
            for hp in range(2):
                for t in range(TT):
                    b = wait_free(f"xs{t}_{hp}")
                    for n in range(2):
                        last = mm(b[:, n * T:(n + 1) * T], xq3[:, 2 * hp + n, t * P:(t + 1) * P],
                                  xk3[:, 2 * hp + n, :], start=True, stop=True)
                    full(f"xs{t}_{hp}", last)
            standing("gl4", uT)
            for hh in range(X2_HEADS):
                if hh == 2:
                    standing("gl5", uT)
                if hh % 2 == 0:
                    in_order(pe, probs_ready, SOFTMAXES, f"x{hh + 1}")
                four_blocks(f"xpT{hh}", x_prob, hh)
                wait_drained(pe, f"xpT{hh}")
                b = wait_free(f"xo_{hh}")
                for kt in range(TT):
                    last = mm(b[:, 0:T], xv3[:, kt, hh * P:(hh + 1) * P],
                              x_pT[hh % 2][:, kt * T:(kt + 1) * T], start=kt == 0, stop=kt == 1)
                full(f"xo_{hh}", last)

            for n, (y, last_use) in enumerate(((ya, "mo3"), (yb, "so3"), (yc, "xo_3"))):
                wait_drained(pe, last_use)
                if n == 2:
                    for hh in range(3):
                        wait_drained(pe, f"xo_{hh}")
                w = weights(f"up{n}", 4)
                y3 = as_chunks(y)
                for c2 in range(4):
                    b = wait_free(f"up{n}_{c2}")
                    for c in range(2):
                        at = (2 * c2 + c) * P
                        for k in range(4):
                            last = mm(b[:, c * T:(c + 1) * T], w[:, k, at:at + P], y3[:, k, :],
                                      start=k == 0, stop=k == 3)
                    full(f"up{n}_{c2}", last)
            pe.wait_ge(after_experts, 2)
            moving("out0", uT)
            moving("out1", uT)


NAMES = ["x", "mem", "norm_mix", "w_in", "da_q_norm", "da_k_norm", "lambda_q1", "lambda_k1", "lambda_q2",
         "lambda_k2", "da_out_norm", "gla_gate_w", "gla_gate_b", "gla_out_norm", "w_o", "norm_cross",
         "norm_mem", "w_cq", "w_ckv", "cross_q_norm", "cross_k_norm", "w_co", "norm_ffn", "w_group",
         "b_group", "w_expert", "b_expert", "w_e_gate", "w_e_up", "w_e_down", "mem_2", "g_in_2", "w_in_2",
         "b_merge_2", "g_mem_2", "w_mem_kv_2", "w_up_moba_2", "w_up_dsa_2", "w_up_cross_2", "w_out_2",
         "g_final_2"]


def rope_table():
    import numpy as np

    half = HD // 2
    inv = np.power(np.float32(10000.0), -np.arange(half, dtype=np.float32) * np.float32(2.0) / np.float32(HD))
    angle = np.arange(T, dtype=np.float32)[:, None] * inv[None, :].astype(np.float32)
    cos, sin = np.cos(angle), np.sin(angle)
    return np.concatenate([cos, cos, -sin, sin], axis=1).astype(np.float32)


def kernel(**inputs):
    import numpy as np
    import concourse.bacc as bacc
    from concourse.bass_utils import run_bass_kernel_spmd

    nc = bacc.Bacc("TRN2", target_bir_lowering=False, num_devices=1)
    arrays, aps = {}, {}
    for name in NAMES + ["rope"]:
        a = rope_table() if name == "rope" else np.ascontiguousarray(inputs[name])
        if a.ndim == 1:
            a = a.reshape(1, -1)
        arrays[f"in_{name}"] = a
        aps[name] = nc.dram_tensor(f"in_{name}", a.shape, mybir.dt.from_np(a.dtype), kind="ExternalInput").ap()
    out = nc.dram_tensor("out_x", (1, T, D), F32, kind="ExternalOutput").ap()
    build(nc, aps, out)
    r = run_bass_kernel_spmd(nc, [arrays], core_ids=[0])
    return r.results[0]["out_x"]
```

```python
from contextlib import ExitStack

import concourse.bass as bass
import numpy as np
from concourse import mybir

F32 = mybir.dt.float32
FR = mybir.dt.float32r
BF16 = mybir.dt.bfloat16
I32 = mybir.dt.int32
U8 = mybir.dt.uint8
ALU = mybir.AluOpType
ACT = mybir.ActivationFunctionType
X = mybir.AxisListType.X

P = 128
T = 256
TT = T // P
D = 1024
KC = D // P
EPS = 1e-6
NEG = -1e30
BIG = 1e30

BLOCK_COLS = 512
SLOT = KC * BLOCK_COLS
RING = 6
HALF = SLOT // 2
RAW_HALVES = 4

H1 = 4
DA_D = 64
DV = 128
GLA_CHUNK = 64
LAM_INIT = 0.2
GLA_TAU = 16.0
CROSS_D = 256

N_EXPERTS = 32
N_GROUPS = 4
PER_GROUP = N_EXPERTS // N_GROUPS
CAP = 64
PAIRS = N_EXPERTS // 2
MORE_ROUNDS = T // CAP - 1
F_EXP = 512
FC = F_EXP // P

H2 = 8
HD = 64
DSA_TOPK = 64
X2_D = 128

FIRST_BLOCKS = ["gqk", "gv", "dq", "dk", "ck0", "ck1", "cv0", "cv1", "dv", "gg",
                "wo0", "wo1", "cq0", "cq1", "xk2", "co0", "co1", "xv2"]
SECOND_BLOCKS = ["iq", "dq2", "dk2", "dv2", "mq", "mk", "mv", "mg", "xq", "dg", "xg",
                 "gl0", "gl1", "gl2", "gl3", "gl4", "gl5", "up0", "up1", "up2", "out0", "out1"]

PSUM_PLAN = ["cols"]
PSUM_PLAN += [f"xT{c}" for c in range(4)]
PSUM_PLAN += ["grT", "gqk0", "gqk1", "z", "gv_0", "gv_1", "dq_0", "dq_1", "dk_0", "dk_1"]
PSUM_PLAN += [f"memT{c}" for c in range(4)]
PSUM_PLAN += ["kdT", "past0", "fut0", "past1", "fut1", "u01", "u2"]
PSUM_PLAN += ["ck0_0", "ck0_1", "ck1_0", "ck1_1"]
PSUM_PLAN += ["og0", "og1", "dqT0", "dqT1", "dkT0", "dkT1"]
PSUM_PLAN += ["cv0_0", "cv0_1", "cv1_0", "cv1_1", "ckT0", "ckT1", "ckT2", "ckT3", "dv_0", "dv_1"]
PSUM_PLAN += ["ds0_0", "ds1_0", "ds0_1", "ds1_1", "gg_0", "gg_1", "ds0_2", "ds1_2", "dpT0", "do0",
              "ds0_3", "ds1_3", "dpT1", "do1", "dpT2", "do2", "dpT3", "do3"]
PSUM_PLAN += [f"mixT{c}" for c in range(4)]
PSUM_PLAN += ["wo0_0", "wo0_1", "wo1_0", "wo1_1"]
PSUM_PLAN += [f"h1T{c}" for c in range(4)]
PSUM_PLAN += ["cq0_0", "cq0_1", "cq1_0", "cq1_1"]
PSUM_PLAN += [f"cqT{c}" for c in range(4)]
PSUM_PLAN += [f"mem2T{c}" for c in range(4)]
PSUM_PLAN += ["cs0_0", "cs1_0", "cs0_1", "cs1_1", "xk2_0", "xk2_1"]
PSUM_PLAN += ["cpT0", "cpT1", "co_0", "cpT2", "co_1", "cpT3", "co_2", "co_3"]
PSUM_PLAN += ["co0_0", "co0_1", "co1_0", "co1_1"]
PSUM_PLAN += [f"h2T{c}" for c in range(4)]
PSUM_PLAN += ["logits", "xv2_0", "xv2_1", "rank"]
FIRST_USES = len(PSUM_PLAN)
PSUM_PLAN += [f"h3T{c}" for c in range(4)]
PSUM_PLAN += ["iq_0", "iq_1", "ikw", "dq2_0", "dq2_1", "dk2_0", "dk2_1", "iqT0", "iqT1", "ikT"]
PSUM_PLAN += ["dv2_0", "dv2_1"]
PSUM_PLAN += ["il0_0", "il0_1", "mq_0", "mq_1", "il1_0", "il1_1", "mk_0", "mk_1", "il1_2", "il1_3"]
PSUM_PLAN += ["mv_0", "mv_1", "dqT2_0", "dqT2_1", "dkT2_0", "dkT2_1", "mqT0", "mqT1", "mkT0", "mkT1"]


def attention_uses(kind):
    uses = [f"{kind}s0_0", f"{kind}s1_0"]
    for pair in range(4):
        if pair < 3:
            uses += [f"{kind}s0_{pair + 1}", f"{kind}s1_{pair + 1}"]
        uses += [f"{kind}pT{2 * pair}", f"{kind}pT{2 * pair + 1}"]
        uses += [f"{kind}o{pair}"]
    return uses


def attention_fillers(kind):
    return {"m": {0: ["mg"], 1: ["xq"], 2: ["dg"], 3: ["xg"]},
            "s": {0: ["gl0"], 1: ["gl1"], 2: ["gl2"], 3: ["gl3"]}}[kind]


def with_fillers(kind):
    uses, fillers = attention_uses(kind), attention_fillers(kind)
    for pair in range(4):
        at = uses.index(f"{kind}pT{2 * pair}")
        uses[at:at] = [f"{b}_{half}" for b in fillers[pair] for half in range(2)]
    return uses


PSUM_PLAN += with_fillers("m")
PSUM_PLAN += with_fillers("s")
PSUM_PLAN += ["xs0_0", "xs1_0", "xs0_1", "xs1_1", "gl4_0", "gl4_1", "xpT0", "xpT1", "xo_0", "xo_1",
              "gl5_0", "gl5_1", "xpT2", "xpT3", "xo_2", "xo_3"]
PSUM_PLAN += [f"up{b}_{c}" for b in range(3) for c in range(4)]
PSUM_PLAN += ["out0_0", "out0_1", "out1_0", "out1_1"]
assert len(set(PSUM_PLAN)) == len(PSUM_PLAN)
USE = {name: (n % 8, n // 8) for n, name in enumerate(PSUM_PLAN)}

LAST_USE = {"gqk": "gqk1", "gv": "gv_1", "dq": "dq_1", "dk": "dk_1", "dv": "dv_1", "gg": "gg_1"}
for b in ("ck0", "ck1", "cv0", "cv1", "wo0", "wo1", "cq0", "cq1", "co0", "co1", "xk2", "xv2", "iq",
          "dq2", "dk2", "dv2", "mq", "mk", "mv", "mg", "xq", "dg", "xg", "gl0", "gl1", "gl2", "gl3",
          "gl4", "gl5", "out0", "out1"):
    LAST_USE[b] = f"{b}_1"
for b in range(3):
    LAST_USE[f"up{b}"] = f"up{b}_3"

DENSE_BLOCKS = FIRST_BLOCKS + SECOND_BLOCKS
assert len(FIRST_BLOCKS) % 2 == 0

NORMS = [("x", 2), ("mem", 2), ("dq", 16), ("dk", 16), ("ck", 8), ("gla", 8), ("da", 8), ("h1", 2),
         ("mem2", 2), ("cq", 8), ("h2", 2), ("h3", 2), ("final", 2)]
NORM_AT = {}
for i, (name, width) in enumerate(NORMS):
    lo = sum(w for _, w in NORMS[:i])
    NORM_AT[name] = (i, lo, lo + width)
NORM_COLS = sum(w for _, w in NORMS)

COLS = {}
for name, rows in (("norm_mix", 8), ("norm_mem", 8), ("norm_cross", 8), ("g_in_2", 8), ("g_mem_2", 8),
                   ("b_merge_2", 24), ("gla_gate_b", 2), ("da_out_norm", 1), ("gla_out_norm", 1),
                   ("cross_q_norm", 2), ("cross_k_norm", 2), ("da_q_norm", 1), ("da_k_norm", 1)):
    COLS[name] = (sum(n for _, n in COLS.values()), rows)
N_COLS = sum(n for _, n in COLS.values())
N_PARAMS = 7


ROW_NORMS = ["x", "mem", "h1", "mem2", "h2", "h3", "final"]
HEAD_SQUARES = ["dq0", "dq1", "dk0", "dk1", "ck0", "ck1", "ck2", "ck3", "og0", "og1",
                "cq0", "cq1", "cq2", "cq3"]
SOFTMAXES = [f"{kind}{n}" for kind in "dcmsx" for n in range(4)]
HI_BANKS = [f"{x}T{c}" for x in ("x", "mem", "mix", "h1", "mem2") for c in range(4)]
HI_BANKS += [f"co_{c}" for c in range(4)] + [f"h3T{c}" for c in range(4)]
ROPED = ["iq", "ik", "dq2", "dk2", "mq", "mk"]
RELUS = ["il0_0", "il0_1", "il1_0", "il1_1", "il1_2", "il1_3"]
TANHS = ["gg_0", "gg_1", "mg_0", "mg_1", "dg_0", "dg_1", "xg_0", "xg_1"]


class Carver:

    def __init__(self, tensor, start, limit):
        self.tensor, self.at, self.limit = tensor, start, limit

    def take(self, width):
        lo, self.at = self.at, self.at + width
        assert self.at <= self.limit, (self.at, self.limit)
        return self.tensor[:, lo:lo + width]


class ExpertSems:

    def __init__(self, sem, prefix, first_down):
        self.first_down = first_down
        self.weights = sem(f"{prefix}_weights_landed")
        self.select_ready = sem(f"{prefix}_select_ready")
        self.gates_ready = sem(f"{prefix}_gates_ready")
        self.gathered = sem(f"{prefix}_gathered")
        self.lo_drained = sem(f"{prefix}_gathered_low_drained")
        self.hi_drained = sem(f"{prefix}_gathered_high_drained")
        self.gate_psum = sem(f"{prefix}_gates_transposed")
        self.gate_ready = sem(f"{prefix}_gates_moved")
        self.hidden_psum = sem(f"{prefix}_gate_up_done")
        self.tanh_ready = sem(f"{prefix}_tanh_ready")
        self.half_ready = sem(f"{prefix}_half_ready")
        self.hidden_ready = sem(f"{prefix}_hidden_ready")
        self.hidden_turned = sem(f"{prefix}_hidden_turned")
        self.hidT_ready = sem(f"{prefix}_hidden_turned_moved")
        self.down_done = sem(f"{prefix}_down_done")
        self.y_ready = sem(f"{prefix}_outputs_moved")
        self.scattered = sem(f"{prefix}_scattered")
        self.added = sem(f"{prefix}_added")
        self.ranks_shifted = sem(f"{prefix}_ranks_shifted")


def build(nc, A, out):
    with ExitStack() as ctx:
        def sb(name, shape, dt=F32):
            return ctx.enter_context(nc.sbuf_tensor(name, shape, dt))

        def sem(name):
            return ctx.enter_context(nc.semaphore(name))

        twins = {}

        def sb_twin(name, shape):
            tensor = sb(name, shape)
            n_bytes = 4 * int(np.prod(shape[1:]))
            twins[name] = nc.alloc_sbuf_tensor_at(f"{name}_rounded", [shape[0], n_bytes // 4], FR,
                                                  offset=nc.sbuf_base - n_bytes)
            return tensor

        def rounded(x):
            return bass.AP(tensor=twins[x.tensor.name], offset=x.offset, ap=x.ap)

        def as_f32(x):
            return rounded(x).bitcast(F32)

        ring = sb_twin("ring", [P, RING * SLOT])
        h = sb("h", [P, TT, D])
        normed = sb("normed", [P, TT, D])
        uT = sb_twin("uT", [P, KC, T])
        ident = sb("ident", [P, P])
        ones = sb("ones", [P, P])
        earlier = sb("earlier", [P, P])
        build_m = sb("build_m", [P, P])
        ident_b = sb("ident_b", [P, P], BF16)
        causal_b = sb("causal_b", [P, P], BF16)
        chunks_b = sb("chunks_b", [P, P], BF16)
        past_m = sb("past_m", [P, P], U8)
        future_m = sb("future_m", [P, P], U8)
        slot_no = sb("slot_no", [P, CAP])
        slot_i = sb("slot_i", [P, CAP], I32)
        rope = sb("rope", [P, TT, 2 * HD])
        rows = sb("rows", [P, P])
        cols = sb("cols", [P, N_COLS])
        half_bias = sb("half_bias", [P, 24])
        qk_gain = sb("qk_gain", [P, 4])
        wide_gain = sb("wide_gain", [P, D])
        lam_s = sb("lam_s", [P, 8])
        neg_lam = sb("neg_lam", [P, 1])
        w_router = sb("w_router", [P, KC, N_GROUPS + N_EXPERTS])
        b_router = sb("b_router", [P, N_GROUPS + N_EXPERTS])
        w_ikw = sb("w_ikw", [P, KC, HD + H2])
        iw = sb("iw", [P, TT, H2])
        mean_sq = sb("mean_sq", [P, NORM_COLS])
        rstd = sb("rstd", [P, NORM_COLS])
        minus_half = sb("minus_half", [P, 16])
        expsum = sb("expsum", [P, 2 * 4])
        act_junk = sb("act_junk", [P, 1])
        most = sb("most", [P, 1])
        marks = sb("marks", [P, 8])
        rt_exp = sb("rt_exp", [P, TT, N_GROUPS + 1])
        assigned = sb("assigned", [P, TT, N_EXPERTS])
        maxes = sb("maxes", [P, 2 * 4])
        bias = sb("bias", [P, 2 * 4])
        inv = sb("inv", [P, 2 * 4])
        coef = sb("coef", [P, 2 * 4])
        q_scale = sb("q_scale", [P, 2, 24])
        decay = sb("decay", [P, 8])
        chunk_start = sb("chunk_start", [P, T])
        rank1 = sb("rank1", [P, TT, N_EXPERTS])
        gates = sb("gates", [P, TT, N_EXPERTS])
        expert_no = sb("expert_no", [P, N_EXPERTS])
        expert_i = sb("expert_i", [P, N_EXPERTS], I32)
        over_flag = sb("over_flag", [P, 1], I32)
        squares = sb("squares", [P, 2 * 512])
        tanh_b = squares
        free = nc.sbuf_bytes_remaining() if callable(nc.sbuf_bytes_remaining) else nc.sbuf_bytes_remaining
        main_cols = min(int(free) // 4 - 64, 16800)
        main = sb_twin("main", [P, main_cols])

        bank = [ctx.enter_context(nc.psum_tensor(f"bank{b}", [P, 512], F32)) for b in range(8)]

        c = Carver(main, 0, main_cols)
        gq, gk = c.take(512), c.take(512)
        la = c.take(512)
        L = c.take(512)
        e_pos = c.take(512)
        q_pos, k_pos, q_neg, k_neg, q_L, k_dec = (c.take(512) for _ in range(6))
        k_decT = c.take(512)
        aT = c.take(1024)
        states = c.take(768)
        gv = c.take(1024)
        gg = c.take(1024)
        dq_tok, dk_tok, dv = c.take(1024), c.take(1024), c.take(1024)
        dqT, dkT = c.take(1024), c.take(1024)
        d_pT = c.take(384)
        c = Carver(dqT, 0, 1024)
        w_gr = c.take(KC * 16)
        lam_in = c.take(4 * DA_D)
        gate_w, grT = c.take(256)[0:16, :], c.take(T)[0:16, :]
        w_gr_hi = c.take(KC * 16)
        d_prob = [main[:, 1024:1792], main[:, 1792:2560]]
        c = Carver(main, 0, main_cols)
        cq_tok, cqT, coT = c.take(2048), c.take(2048), c.take(2048)
        c_prob = [c.take(512) for _ in range(4)]
        c_pT = [c.take(512) for _ in range(2)]
        ck_tok = normed[:, :, :].rearrange("p t d -> p (t d)")
        c = Carver(ring, 4 * SLOT, RING * SLOT)
        mix = c.take(2048)
        mixT = memT = c.take(2048)
        ckT, cv = c.take(2048), c.take(2048)

        lo_a, lo_b = ring[:, 3 * SLOT:3 * SLOT + 2048], ring[:, 3 * SLOT + 2048:4 * SLOT]

        c = Carver(main, 0, main_cols)
        xgT = c.take(KC * 2 * CAP)
        select = c.take(2 * 2 * CAP)
        select_g = c.take(2 * 2 * CAP)
        gate_mat = c.take(T)
        tanh_g, half_h, hid = (c.take(F_EXP) for _ in range(3))
        hidT = c.take(FC * 2 * CAP)
        y_slots = c.take(D)
        experts_end = c.at
        rt = main[:, experts_end:experts_end + 512]

        c = Carver(main, 0, main_cols)
        iq_tok, dq2_tok, dk2_tok, mq_tok, mk_tok = (c.take(1024) for _ in range(5))
        iqT, ikT = c.take(1024), c.take(256)
        assert c.at >= experts_end
        dq2T, dk2T = c.take(1024), c.take(1024)
        mqT, mkT = c.take(1024), c.take(1024)
        dv2, mv = c.take(1024), c.take(1024)
        mem2_tok = main[:, c.at - 2048:c.at]
        xkT, xv2 = c.take(1024), c.take(1024)
        mem2T = main[:, c.at:c.at + 2048]
        work_lo = c.at
        score = c.take(512)
        work = c.take(256)
        best8 = c.take(8)
        probs = c.take(768)
        sel_b = c.take(192).bitcast(BF16)
        probT = main[:, work_lo:work_lo + 768]
        rope_t = probs[:, 0:512]
        ik_tok = work
        relu = mk_tok
        ya, yb, yc = iq_tok, dq2_tok, dk2_tok
        ya_hi, yb_hi, yc_hi = iqT, mv, dv2
        mgate, dgate = mq_tok, mk_tok
        x_prob = [main[:, c0:c0 + 512] for c0 in range(6400, 8448, 512)]
        x_pT = [mqT[:, 0:512], mqT[:, 512:1024]]
        up_t = mkT[:, 0:512]
        c = Carver(ring, 4 * SLOT, RING * SLOT)
        xqT, xgate = c.take(1024), c.take(1024)
        branch_gate = c.take(3 * KC * T)

        filled = [sem(f"bank_filled{b}") for b in range(8)]
        drained = [sem(f"bank_drained{b}") for b in range(8)]
        landed = [sem(f"expert_weights_landed{j}") for j in range(RING)]
        raw_landed = [sem(f"raw_weights_landed{j}") for j in range(RAW_HALVES)]
        hi_made, split_made = sem("weights_hi_made"), sem("weights_split")
        half_used = sem("first_half_used")
        gates_split = sem("low_rank_weights_split")
        hi_moved, y_split = sem("input_hi_moved"), sem("branch_inputs_split")
        x_landed, mem_landed, mem2_landed = sem("x_landed"), sem("mem_landed"), sem("mem2_landed")
        rows_landed, params_landed = sem("rows_landed"), sem("params_landed")
        gates_landed, lambdas_landed = sem("gates_landed"), sem("lambdas_landed")
        final_gain_landed = sem("final_gain_landed")
        consts_made, masks_cast = sem("consts_made"), sem("masks_cast")
        means_ready, rstd_ready = sem("means_ready"), sem("rstd_ready")
        row_squared = sem("row_squared")
        head_squared, head_summed = sem("head_squared"), sem("head_summed")
        normed_ready = sem("normed_ready")
        keys_normed, scales_ready = sem("keys_normed"), sem("scales_ready")
        lam_products, lam_exps = sem("lam_products"), sem("lam_exps")
        gla_vec, gla_act = sem("gla_vec"), sem("gla_act")
        mix_ready = sem("mix_ready")
        bias_ready, probs_ready = sem("bias_ready"), sem("probs_ready")
        roped = sem("roped")
        relu_done, scored = sem("relu_done"), sem("scored")
        selected = sem("selected")
        tanh_done = sem("tanh_done")
        router_step = sem("router_step")
        router_exp = sem("router_exp")
        after_experts, merged = sem("after_experts"), sem("merged")
        out_ready, out_stored = sem("out_ready"), sem("out_stored")
        dve_step, act_step, pool_step = sem("dve_step"), sem("act_step"), sem("pool_step")
        rows_switched = sem("rows_switched")

        main_s, more_s = ExpertSems(sem, "moe", 0), ExpertSems(sem, "more", 1)

        def in_bank(name):
            return bank[USE[name][0]]

        def wait_filled(eng, name):
            b, k = USE[name]
            eng.wait_ge(filled[b], k + 1)
            return bank[b]

        def wait_drained(eng, name):
            b, k = USE[name]
            eng.wait_ge(drained[b], k + 1)

        def wait_free(name):
            b, k = USE[name]
            if k:
                nc.tensor.wait_ge(drained[b], k)
            return bank[b]

        def done(name, ins):
            ins.then_inc(drained[USE[name][0]], 1)

        def full(name, ins):
            ins.then_inc(filled[USE[name][0]], 1)

        def chain(eng, signal):
            count = [0]

            def link(ins):
                count[0] += 1
                ins.then_inc(signal, 1)
                eng.wait_ge(signal, count[0])
            return link

        def in_order(eng, signal, names, name):
            eng.wait_ge(signal, names.index(name) + 1)

        def column(name, c=0):
            at = COLS[name][0] + c
            return cols[:, at:at + 1]

        def stat(tile, name):
            _, lo, hi = NORM_AT[name]
            return tile[:, lo:hi]

        def wait_rstd(eng, name):
            eng.wait_ge(rstd_ready, NORM_AT[name][0] + 1)

        def slot(j, chunks=KC):
            return ring[:, j * SLOT:(j + 1) * SLOT].rearrange("p (k n) -> p k n", k=chunks)

        def raw_half(name, h):
            at = (2 * DENSE_BLOCKS.index(name) + h) % RAW_HALVES * HALF
            return ring[:, at:at + HALF]

        def hi_half(h):
            return ring[:, 2 * SLOT + h * HALF:2 * SLOT + (h + 1) * HALF]

        def wait_raw(eng, name, h):
            n = DENSE_BLOCKS.index(name)
            eng.wait_ge(raw_landed[(2 * n + h) % RAW_HALVES], 16 * (n // 2 + 1))

        def wait_used(eng, name, h):
            if h == 0:
                eng.wait_ge(half_used, DENSE_BLOCKS.index(name) + 1)
            else:
                wait_filled(eng, LAST_USE[name])

        def block_cols(w, lo, width=BLOCK_COLS):
            return w[0, :, lo:lo + width].rearrange("(k p) n -> p k n", p=P)

        W1, W2 = A["w_in"], A["w_in_2"]
        SOURCE = {"gqk": block_cols(W1, 1536), "gv": block_cols(W1, 2048), "dq": block_cols(W1, 0),
                  "dk": block_cols(W1, 512), "dv": block_cols(W1, 1024), "gg": block_cols(W1, 2560)}
        for j in range(2):
            SOURCE[f"ck{j}"] = block_cols(A["w_ckv"], 512 * j)
            SOURCE[f"cv{j}"] = block_cols(A["w_ckv"], D + 512 * j)
            SOURCE[f"wo{j}"] = block_cols(A["w_o"], 512 * j)
            SOURCE[f"cq{j}"] = block_cols(A["w_cq"], 512 * j)
            SOURCE[f"co{j}"] = block_cols(A["w_co"], 512 * j)
            SOURCE[f"out{j}"] = block_cols(A["w_out_2"], 512 * j)
        for n, b in enumerate(("mq", "mk", "mv", "mg", "dq2", "dk2", "dv2", "dg", "iq")):
            SOURCE[b] = block_cols(W2, 512 * n)
        IKW_AT = 9 * 512
        SOURCE["xq"] = block_cols(W2, IKW_AT + HD + H2)
        SOURCE["xg"] = block_cols(W2, IKW_AT + HD + H2 + 512)
        for n in range(6):
            SOURCE[f"gl{n}"] = block_cols(W2, IKW_AT + HD + H2 + 1024 + 512 * n)
        SOURCE["xk2"] = block_cols(A["w_mem_kv_2"], 0)
        SOURCE["xv2"] = block_cols(A["w_mem_kv_2"], 512)
        for n, w in enumerate(("w_up_moba_2", "w_up_dsa_2", "w_up_cross_2")):
            SOURCE[f"up{n}"] = A[w][0].rearrange("(k p) n -> p k n", p=P)

        def token_major(a):
            return a.rearrange("(t p) d -> p t d", p=P)

        def token_tiles(x):
            return x.rearrange("p (t d) -> p t d", t=TT)

        block = ctx.enter_context(nc.Block())

        @block.sync
        def _(sp):
            def load_dense(name):
                names = FIRST_BLOCKS if name in FIRST_BLOCKS else SECOND_BLOCKS
                at = names.index(name)
                src = SOURCE[name]
                chunks = src.shape[1] // 2
                for h in range(2):
                    if at >= RAW_HALVES // 2:
                        wait_used(sp, names[at - RAW_HALVES // 2], h)
                    dst = raw_half(name, h).rearrange("p (k n) -> p k n", k=chunks)
                    n = DENSE_BLOCKS.index(name)
                    sp.dma_start(dst, src[:, h * chunks:(h + 1) * chunks, :])\
                        .then_inc(raw_landed[(2 * n + h) % RAW_HALVES], 16)

            sp.dma_start(rows[0:N_COLS, :], A["rows"]).then_inc(rows_landed, 16)
            sp.wait_ge(x_landed, 16)
            for name in FIRST_BLOCKS[:2]:
                load_dense(name)
            sp.dma_start(token_tiles(mix), token_major(A["mem"][0])).then_inc(mem_landed, 16)
            params = [(rope[:, :, :], token_major(A["rope"])),
                      (wide_gain[:, :], A["norm_ffn"].broadcast_to([P, D])),
                      (w_router[:, :, 0:N_GROUPS], A["w_group"][0].rearrange("(k p) n -> p k n", p=P)),
                      (w_router[:, :, N_GROUPS:], A["w_expert"][0].rearrange("(k p) n -> p k n", p=P)),
                      (b_router[:, 0:N_GROUPS], A["b_group"].broadcast_to([P, N_GROUPS])),
                      (b_router[:, N_GROUPS:], A["b_expert"].broadcast_to([P, N_EXPERTS])),
                      (w_ikw[:, :, :], block_cols(W2, IKW_AT, HD + H2))]
            assert len(params) == N_PARAMS
            for dst, src in params:
                sp.dma_start(dst, src).then_inc(params_landed, 16)
            for name in FIRST_BLOCKS[2:]:
                load_dense(name)

            gate_w_of = A["w_e_gate"][0].rearrange("e (k p) n -> e p k n", p=P)
            up_w_of = A["w_e_up"][0].rearrange("e (k p) n -> e p k n", p=P)
            down_w_of = A["w_e_down"][0].rearrange("e (k p) n -> e p k n", p=P)

            def load_two(first_slot, pair, w_of, signals):
                for n in range(2):
                    sp.dma_start(slot(first_slot + n), w_of[pair[n], :, :, :]).then_inc(signals[n], 16)

            def load_down(j, e, signal):
                sp.dma_start(slot(j, FC), down_w_of[e, :, :, :]).then_inc(signal, 16)

            wait_filled(sp, "co_3")
            load_two(4, (0, 1), gate_w_of, landed[4:6])
            for e, name in enumerate(("co1", "xv2")):
                wait_filled(sp, LAST_USE[name])
                sp.dma_start(slot(e), up_w_of[e, :, :, :]).then_inc(landed[e], 16)
            for e in range(2):
                load_down(2 + e, e, landed[2 + e])
            with sp.Fori(1, PAIRS) as i:
                e0 = sp.snap(i * 2)
                e1 = sp.snap(i * 2 + 1)
                gates_used = sp.snap(i * 2 - 1)
                all_used = sp.snap(i * 2)
                sp.wait_ge(main_s.hidden_psum, gates_used)
                load_two(4, (e0, e1), gate_w_of, landed[4:6])
                sp.wait_ge(main_s.hidden_psum, all_used)
                load_two(0, (e0, e1), up_w_of, landed[0:2])
                sp.wait_ge(main_s.down_done, all_used)
                load_down(2, e0, landed[2])
                load_down(3, e1, landed[3])
            sp.wait_ge(main_s.down_done, N_EXPERTS)

            sp.wait_ge(router_step, 2)
            over = sp.value_load(over_flag[0:1, 0:1], min_val=0, max_val=1)
            with sp.If(over):
                sp.sem_inc(more_s.down_done, 1)
                with sp.Fori(0, MORE_ROUNDS) as r:
                    with sp.Fori(0, PAIRS) as i:
                        e0 = sp.snap(i * 2)
                        e1 = sp.snap(i * 2 + 1)
                        used = sp.snap(r * N_EXPERTS + i * 2 + 1)
                        sp.wait_ge(more_s.down_done, used)
                        load_two(4, (e0, e1), gate_w_of, [more_s.weights] * 2)
                        load_two(0, (e0, e1), up_w_of, [more_s.weights] * 2)
                        load_down(2, e0, more_s.weights)
                        load_down(3, e1, more_s.weights)
                sp.wait_ge(more_s.down_done, 1 + MORE_ROUNDS * N_EXPERTS)
            for name in SECOND_BLOCKS:
                load_dense(name)

            for t in range(TT):
                sp.wait_ge(out_ready, 1 + t)
                sp.dma_start(token_major(out[0])[:, t, :], normed[:, t, :]).then_inc(out_stored, 16)
            sp.wait_ge(out_stored, 16 * TT)

        @block.gpsimd
        def _(pool):
            g = nc.gpsimd
            link = chain(pool, pool_step)
            link(g.memset(ident[:, :], 0.0))
            g.affine_select(out=ident[:, :], in_=ident[:, :], compare_op=ALU.not_equal, fill=1.0, base=0,
                            pattern=[[-1, P]], channel_multiplier=1).then_inc(consts_made, 1)
            g.memset(minus_half[:, :], -0.5).then_inc(consts_made, 1)
            g.memset(ones[:, :], 1.0).then_inc(consts_made, 1)
            g.iota(slot_i[:, :], pattern=[[1, CAP]], base=1, channel_multiplier=0).then_inc(consts_made, 1)
            g.iota(expert_i[:, :], pattern=[[1, N_EXPERTS]], base=0, channel_multiplier=0)\
                .then_inc(consts_made, 1)
            pool.wait_ge(consts_made, 5)
            g.affine_select(out=earlier[:, :], in_=ones[:, :], compare_op=ALU.is_gt, fill=0.0, base=0,
                            pattern=[[1, P]], channel_multiplier=-1).then_inc(consts_made, 1)

            def rsqrt(name):
                n, lo, hi = NORM_AT[name]
                pool.wait_ge(means_ready, n + 1)
                g.tensor_tensor(out=rstd[:, lo:hi], in0=mean_sq[:, lo:hi], in1=minus_half[:, 0:hi - lo],
                                op=ALU.pow).then_inc(rstd_ready, 1)

            def mask(made, steps):
                if made:
                    pool.wait_ge(masks_cast, made)
                for step in steps[:-1]:
                    link(step())
                steps[-1]().then_inc(consts_made, 1)

            def fill(value, rows_=slice(0, P), cols_=slice(0, P)):
                return lambda: g.memset(build_m[rows_, cols_], value)

            def keep(op, pattern, mult, value):
                return lambda: g.affine_select(out=build_m[:, :], in_=build_m[:, :], compare_op=op,
                                               fill=value, base=0, pattern=[[pattern, P]],
                                               channel_multiplier=mult)

            low, high = slice(0, GLA_CHUNK), slice(GLA_CHUNK, P)
            rsqrt("x")
            mask(0, [fill(1.0), keep(ALU.is_ge, 1, -1, 0.0), fill(0.0, low, high)])
            mask(1, [fill(1.0), keep(ALU.is_gt, -1, 1, 0.0), fill(0.0, high, low)])
            mask(2, [fill(0.0), fill(NEG, low, high)])
            mask(3, [fill(0.0), keep(ALU.is_ge, -1, 1, NEG)])
            for name, _ in NORMS[1:]:
                rsqrt(name)

        @block.scalar
        def _(act):
            a = nc.scalar
            link = chain(act, act_step)
            act.dma_start(h[:, :, :], token_major(A["x"][0])).then_inc(x_landed, 16)
            act.dma_start(w_gr.rearrange("p (k n) -> p k n", k=KC), block_cols(W1, 3072, 16)).then_inc(gates_landed, 16)
            act.dma_start(gate_w[:, :], A["gla_gate_w"][0]).then_inc(gates_landed, 16)
            for n, name in enumerate(("lambda_q1", "lambda_k1", "lambda_q2", "lambda_k2")):
                act.dma_start(lam_in[:, n * DA_D:(n + 1) * DA_D], A[name].broadcast_to([P, DA_D]))\
                    .then_inc(lambdas_landed, 16)

            def copy(name, dst, width=512, rows_=P, scale=1.0):
                src = wait_filled(act, name)[0:rows_, 0:width]
                done(name, a.activation(dst, src, ACT.Copy, scale=scale))

            def square_rows(name, src, junk, complete=None):
                _, lo, _ = NORM_AT[name]
                for t in range(TT):
                    if complete:
                        wait_drained(act, f"{complete}0_{t}")
                        wait_drained(act, f"{complete}1_{t}")
                    last = a.activation(junk[:, t, :], src[:, t, :], ACT.Square,
                                        accum_out=mean_sq[:, lo + t:lo + t + 1])
                last.then_inc(row_squared, 1)

            def square_heads(name, bank_name):
                n = HEAD_SQUARES.index(name)
                if n >= 2:
                    act.wait_ge(head_summed, n - 1)
                a.activation(squares[:, n % 2 * 512:n % 2 * 512 + 512], wait_filled(act, bank_name)[:, :],
                             ACT.Square).then_inc(head_squared, 1)

            def gained(name, dst, gains):
                src = wait_filled(act, name)
                for n, gain in enumerate(gains):
                    last = a.activation(dst[:, n * T:(n + 1) * T], src[:, n * T:(n + 1) * T], ACT.Copy,
                                        scale=gain)
                done(name, last)

            uT_flat = uT[:, :, :].rearrange("p c t -> p (c t)")

            def uT_chunks(c2):
                return uT[:, 2 * c2:2 * c2 + 2, :].rearrange("p c t -> p (c t)")

            def hi_of(name, dst, gains=(1.0, 1.0)):
                src = wait_filled(act, name)
                for n, gain in enumerate(gains):
                    at = slice(n * T, (n + 1) * T)
                    last = a.activation(rounded(dst[:, at]), src[:, at], ACT.Copy, scale=gain)
                last.then_inc(hi_moved, 1)

            def norm_T(prefix, dst, gain):
                for c2 in range(4):
                    hi_of(f"{prefix}T{c2}", dst[:, c2 * 512:c2 * 512 + 512],
                          [column(gain, 2 * c2 + n) for n in range(2)])

            def split_hi(name, halves=range(2)):
                n = DENSE_BLOCKS.index(name)
                for h in halves:
                    wait_raw(act, name, h)
                    if n:
                        wait_used(act, DENSE_BLOCKS[n - 1], h)
                    a.activation(rounded(hi_half(h)), raw_half(name, h), ACT.Copy).then_inc(hi_made, 1)

            def exps(name, n, parts, probs_free=None):
                place = SOFTMAXES.index(name)
                act.wait_ge(bias_ready, place + 1)
                if probs_free:
                    wait_filled(act, probs_free)
                at = place % 2 * 4
                for i, (src, dst, col, scale, ends) in enumerate(parts):
                    ins = a.activation(dst, src, ACT.Exp, bias=bias[:, at + col:at + col + 1], scale=scale,
                                       accum_out=expsum[:, at + col:at + col + 1])
                    if ends:
                        done(ends, ins)

            def tiles(x):
                return x.rearrange("p (t d) -> p t d", t=TT)

            act.wait_ge(x_landed, 16)
            square_rows("x", h, normed)
            copy("cols", cols[:, :], N_COLS)
            wait_drained(act, "cols")
            norm_T("x", uT_flat, "norm_mix")
            split_hi("gqk")

            copy("grT", grT[:, :], T, 16)
            split_hi("gv")
            copy("gqk0", gq, scale=DA_D ** -0.5)
            copy("gqk1", gk)
            act.wait_ge(mem_landed, 16)
            square_rows("mem", mix.rearrange("p (t d) -> p t d", t=TT),
                        memT.rearrange("p (t d) -> p t d", t=TT))
            act.wait_ge(lam_products, 1)
            a.activation(lam_s[:, 2:4], lam_s[:, 0:2], ACT.Exp).then_inc(lam_exps, 1)
            act.wait_ge(gla_vec, 1)
            link(a.activation(k_dec, k_dec, ACT.Exp))
            a.activation(k_dec, k_dec, ACT.Ln, bias=1.0).then_inc(gla_act, 1)
            split_hi("dq")
            for t in range(TT):
                copy(f"gv_{t}", gv[:, t * 512:t * 512 + 512])
            act.wait_ge(gla_vec, 2)
            tau = 1.0 / GLA_TAU
            a.activation(e_pos, la, ACT.Exp, scale=tau)
            a.activation(q_L, L, ACT.Exp, scale=tau)
            a.activation(decay[:, :], L.rearrange("p (c t) -> p c t", t=GLA_CHUNK)[:, :, GLA_CHUNK - 1],
                         ACT.Exp, scale=tau)
            a.activation(k_dec, k_dec, ACT.Exp, scale=tau)
            a.activation(la, la, ACT.Exp, scale=-tau).then_inc(gla_act, 1)
            for name, following, dst in (("dq", "dk", dq_tok), ("dk", "ck0", dk_tok)):
                split_hi(following)
                for t in range(TT):
                    square_heads(f"{name}{t}", f"{name}_{t}")
                    copy(f"{name}_{t}", dst[:, t * 512:t * 512 + 512])
            norm_T("mem", memT, "norm_mem")
            copy("kdT", k_decT)
            for j in range(2):
                split_hi(("ck1", "cv0")[j])
                for t in range(TT):
                    square_heads(f"ck{2 * j + t}", f"ck{j}_{t}")
                    if j + t == 0:
                        wait_filled(act, "xT3")
                    copy(f"ck{j}_{t}", ck_tok[:, t * D + j * 512:t * D + j * 512 + 512])
            for t in range(TT):
                square_heads(f"og{t}", f"og{t}")
                if t == 0:
                    wait_filled(act, "memT3")
                copy(f"og{t}", mix[:, t * D + 512:(t + 1) * D])
            for half in range(2):
                copy(f"dkT{half}", dkT[:, half * 512:half * 512 + 512])
            split_hi("cv1")
            split_hi("dv")
            for c2 in (0, 2):
                copy(f"ckT{c2}", ckT[:, c2 * 512:c2 * 512 + 512])
            split_hi("gg")
            for t in range(TT):
                copy(f"dv_{t}", dv[:, t * 512:t * 512 + 512])

            def d_exps(hh):
                s0 = wait_filled(act, f"ds0_{hh}")
                s1 = wait_filled(act, f"ds1_{hh}")
                parts = []
                for t in range(TT):
                    for s in range(2):
                        lo = s * P if t == 0 else s * T
                        src = (s0, s1)[t][:, lo:lo + (t + 1) * P]
                        dst = d_prob[hh % 2][:, s * 384 + t * P:s * 384 + t * P + (t + 1) * P]
                        at = t * 8 + hh * 2 + s
                        ends = f"ds{t}_{hh}" if s else None
                        parts.append((src, dst, t * 2 + s, q_scale[:, 0, at:at + 1], ends))
                exps(f"d{hh}", hh, parts, f"dpT{hh - 2}" if hh >= 2 else None)

            def d_pT_out(hh):
                if hh:
                    wait_filled(act, f"do{hh - 1}")
                copy(f"dpT{hh}", d_pT, 384)

            def d_out(hh):
                src = wait_filled(act, f"do{hh}")
                _, lo, _ = NORM_AT["da"]
                for t in range(TT):
                    junk = squares[:, (t * 4 + hh) * P:(t * 4 + hh + 1) * P]
                    a.activation(junk, src[:, t * P:(t + 1) * P], ACT.Square,
                                 accum_out=mean_sq[:, lo + t * 4 + hh:lo + t * 4 + hh + 1])
                dst = mix.rearrange("p (t d) -> p t d", t=TT)[:, :, hh * P:(hh + 1) * P]
                done(f"do{hh}", a.activation(dst, src[:, 0:2 * P].rearrange("p (t d) -> p t d", t=TT),
                                             ACT.Copy))

            def gate_tanh(name):
                n = TANHS.index(name)
                if n >= 2:
                    wait_drained(act, TANHS[n - 2])
                a.activation(tanh_b[:, n % 2 * 512:n % 2 * 512 + 512], wait_filled(act, name)[:, :],
                             ACT.Tanh, scale=0.5).then_inc(tanh_done, 1)

            d_exps(0)
            d_exps(1)
            act.wait_ge(head_summed, len(HEAD_SQUARES[:10]))
            for t in range(TT):
                gate_tanh(f"gg_{t}")
            d_pT_out(0)
            wait_drained(act, "gg_1")
            d_out(0)
            d_exps(2)
            d_pT_out(1)
            d_out(1)
            d_exps(3)
            split_hi("wo0")
            for hh in (2, 3):
                d_pT_out(hh)
                d_out(hh)
            wait_filled(act, "do3")
            act.dma_start(tiles(mem2_tok), token_major(A["mem_2"][0])).then_inc(mem2_landed, 16)
            act.wait_ge(mix_ready, 1)
            da_gain, gla_gain = qk_gain[:, 1:2], column("gla_out_norm")
            for c2 in range(4):
                hi_of(f"mixT{c2}", mixT[:, c2 * 512:c2 * 512 + 512], [(da_gain, gla_gain)[c2 // 2]] * 2)
            split_hi("wo1")
            split_hi("cq0", [0])

            square_rows("h1", h, normed, "wo")
            split_hi("cq0", [1])
            norm_T("h1", uT_flat, "norm_cross")
            act.wait_ge(mem2_landed, 16)
            square_rows("mem2", tiles(mem2_tok), tiles(mem2T))
            for j in range(2):
                split_hi(("cq1", "xk2")[j], range(2 - j))
                for t in range(TT):
                    square_heads(f"cq{2 * j + t}", f"cq{j}_{t}")
                    copy(f"cq{j}_{t}", cq_tok[:, t * D + j * 512:t * D + j * 512 + 512])
            split_hi("xk2", [1])
            for c2 in (0, 2):
                gained(f"cqT{c2}", cqT[:, c2 * 512:c2 * 512 + 512], [qk_gain[:, 2 + n:3 + n] for n in range(2)])

            norm_T("mem2", mem2T, "g_mem_2")

            def pair_exps(kind, t, hp, dsts, scale):
                name = f"{kind}s{t}_{hp}"
                src = wait_filled(act, name)
                parts = [(src[:, n * T:(n + 1) * T], dsts[t + 2 * hp][:, n * T:(n + 1) * T], n,
                          scale(t, 2 * hp + n), name if n else None) for n in range(2)]
                exps(f"{kind}{t + 2 * hp}", t + 2 * hp, parts)

            at = NORM_AT["dq"][2] - NORM_AT["dq"][1]
            for hp in range(2):
                for t in range(TT):
                    pair_exps("c", t, hp, c_prob,
                              lambda t, hh: q_scale[:, 0, at + t * 4 + hh:at + t * 4 + hh + 1])
            split_hi("co0")
            for half in range(2):
                copy(f"xk2_{half}", xkT[:, half * 512:half * 512 + 512])
            for hh in range(4):
                if hh >= 2:
                    wait_filled(act, f"co_{hh - 2}")
                copy(f"cpT{hh}", c_pT[hh % 2])
                if hh:
                    hi_of(f"co_{hh - 1}", coT[:, (hh - 1) * 512:hh * 512])
            hi_of("co_3", coT[:, 3 * 512:4 * 512])
            split_hi("co1")
            split_hi("xv2", [0])
            square_rows("h2", h, normed, "co")
            split_hi("xv2", [1])
            for c2 in (0, 2):
                copy(f"h2T{c2}", uT_chunks(c2))
            act.wait_ge(normed_ready, 10)
            act.dma_start(wide_gain[:, :], A["g_final_2"].broadcast_to([P, D])).then_inc(final_gain_landed, 16)
            act.wait_ge(router_step, 1)
            a.activation(rt_exp[:, :, :], rt_exp[:, :, :], ACT.Exp).then_inc(router_exp, 1)

            def expert_gates(S, n):
                act.wait_ge(S.gate_psum, n + 1)
                a.activation(gate_mat, bank[4][:, 0:T], ACT.Copy).then_inc(S.gate_ready, 1)

            def expert_tanh(S, n):
                act.wait_ge(S.hidden_psum, n * 2 + 1)
                a.activation(tanh_g, bank[2][:, :], ACT.Tanh, scale=0.5).then_inc(S.tanh_ready, 1)

            def turned_hidden(S, n):
                act.wait_ge(S.hidden_turned, n + 1)
                a.activation(hidT, bank[0][:, :], ACT.Copy).then_inc(S.hidT_ready, 1)

            def expert_out(S, n):
                for half in range(2):
                    act.wait_ge(S.down_done, n * 2 + 1 + half + S.first_down)
                    last = a.activation(y_slots[:, half * 512:half * 512 + 512], bank[4 + half][:, :], ACT.Copy)
                last.then_inc(S.y_ready, 1)

            def gathered_low(S, n):
                act.wait_ge(S.gathered, n + 1)
                a.activation(xgT[:, 0:512], bank[0][:, :], ACT.Copy).then_inc(S.lo_drained, 1)

            a.activation(act_junk[:, :], bias[:, 0:1], ACT.Copy).then_inc(main_s.y_ready, 1)
            gathered_low(main_s, 0)
            with act.Fori(0, PAIRS - 1) as i:
                expert_gates(main_s, i)
                expert_tanh(main_s, i)
                turned_hidden(main_s, i)
                expert_out(main_s, i)
                gathered_low(main_s, i + 1)
            expert_gates(main_s, PAIRS - 1)
            expert_tanh(main_s, PAIRS - 1)
            turned_hidden(main_s, PAIRS - 1)
            expert_out(main_s, PAIRS - 1)
            act.wait_ge(router_step, 2)
            over = act.value_load(over_flag[0:1, 0:1], min_val=0, max_val=1)
            with act.If(over):
                a.activation(act_junk[:, :], bias[:, 0:1], ACT.Copy).then_inc(more_s.y_ready, 1)
                with act.Fori(0, MORE_ROUNDS * PAIRS) as n:
                    gathered_low(more_s, n)
                    expert_gates(more_s, n)
                    expert_tanh(more_s, n)
                    turned_hidden(more_s, n)
                    expert_out(more_s, n)

            act.wait_ge(after_experts, 1)
            square_rows("h3", h, normed)
            split_hi("iq")
            norm_T("h3", uT_flat, "g_in_2")
            for name in ("dq2", "dk2", "dv2"):
                split_hi(name)
            for half in range(2):
                copy(f"iqT{half}", iqT[:, half * 512:half * 512 + 512])
            copy("ikT", ikT, T)
            split_hi("mq")
            for t in range(TT):
                copy(f"dv2_{t}", dv2[:, t * 512:t * 512 + 512])

            def relu_bank(name):
                n = RELUS.index(name)
                if n >= 2:
                    act.wait_ge(scored, n - 1)
                done(name, a.activation(relu[:, n % 2 * 512:n % 2 * 512 + 512], wait_filled(act, name)[:, :],
                                        ACT.Relu, scale=HD ** -0.5))

            for name in RELUS:
                if name == "il1_0":
                    split_hi("mk")
                if name == "il1_2":
                    split_hi("mv")
                relu_bank(name)
            split_hi("mg")
            for t in range(TT):
                copy(f"mv_{t}", mv[:, t * 512:t * 512 + 512])
            for name, dst in (("dqT2", dq2T), ("dkT2", dk2T)):
                for half in range(2):
                    copy(f"{name}_{half}", dst[:, half * 512:half * 512 + 512])
            for name, dst in (("mqT", mqT), ("mkT", mkT)):
                for half in range(2):
                    copy(f"{name}{half}", dst[:, half * 512:half * 512 + 512])

            def branch_tanh(n, half):
                name = f"gl{n}_{half}"
                src = wait_filled(act, name)
                for c in range(2):
                    chunk = 4 * n + 2 * half + c
                    last = a.activation(branch_gate[:, chunk * T:(chunk + 1) * T], src[:, c * T:(c + 1) * T],
                                        ACT.Tanh, scale=0.5, bias=half_bias[:, chunk:chunk + 1])
                done(name, last)

            def filler(b):
                split_hi(DENSE_BLOCKS[DENSE_BLOCKS.index(b) + 1])
                for half in range(2):
                    if b == "xq":
                        copy(f"xq_{half}", xqT[:, half * 512:half * 512 + 512])
                    elif b.startswith("gl"):
                        branch_tanh(int(b[2:]), half)
                    else:
                        gate_tanh(f"{b}_{half}")

            def pair8_exps(kind, pair):
                s0 = wait_filled(act, f"{kind}s0_{pair}")
                s1 = wait_filled(act, f"{kind}s1_{pair}")
                parts = []
                for t in range(TT):
                    for n in range(2):
                        lo = n * P if t == 0 else n * T
                        src = (s0, s1)[t][:, lo:lo + (t + 1) * P]
                        dst = probs[:, n * 384 + t * P:n * 384 + t * P + (t + 1) * P]
                        ends = f"{kind}s{t}_{pair}" if n else None
                        parts.append((src, dst, t * 2 + n, HD ** -0.5, ends))
                exps(f"{kind}{pair}", pair, parts, f"{kind}pT{2 * pair - 1}" if pair else None)

            def pair8(kind, pair):
                for n in range(2):
                    if kind + str(pair) == "m0" and n == 0:
                        act.wait_ge(selected, 2)
                    if pair and n == 0:
                        wait_filled(act, f"{kind}o{pair - 1}")
                    copy(f"{kind}pT{2 * pair + n}", probT[:, n * 384:n * 384 + 384], 384)
                if pair < 3:
                    pair8_exps(kind, pair + 1)
                for b in attention_fillers(kind)[pair]:
                    filler(b)

            for kind in "ms":
                pair8_exps(kind, 0)
                for pair in range(4):
                    pair8(kind, pair)
            for hp in range(2):
                for t in range(TT):
                    pair_exps("x", t, hp, x_prob, lambda t, hh: X2_D ** -0.5)
            for hp in range(2):
                for hh in (2 * hp, 2 * hp + 1):
                    if hp:
                        wait_filled(act, f"xo_{hh - 2}")
                    copy(f"xpT{hh}", x_pT[hh % 2])
                filler(f"gl{4 + hp}")
            for name in ("up1", "up2", "out0", "out1"):
                split_hi(name)
            square_rows("final", h, normed, "out")

        @block.vector
        def _(dve):
            v = nc.vector
            link = chain(dve, dve_step)

            def mean(name, width):
                st = stat(mean_sq, name)
                v.tensor_scalar(st, st, 1.0 / width, EPS, ALU.mult, ALU.add).then_inc(means_ready, 1)

            def scale_rows(name, src, dst):
                in_order(dve, row_squared, ROW_NORMS, name)
                mean(name, D)
                wait_rstd(dve, name)
                _, lo, _ = NORM_AT[name]
                for t in range(TT):
                    v.tensor_scalar(dst[:, t, :], src[:, t, :], rstd[:, lo + t:lo + t + 1], None, ALU.mult)\
                        .then_inc(normed_ready, 1)

            def head_sums(name, dst, heads):
                n = HEAD_SQUARES.index(name)
                dve.wait_ge(head_squared, n + 1)
                src = squares[:, n % 2 * 512:n % 2 * 512 + 512].rearrange("p (h d) -> p h d", h=heads)
                v.tensor_reduce(dst, src, axis=X, op=ALU.add).then_inc(head_summed, 1)

            def copy(name, dst, width=512):
                done(name, v.tensor_copy(dst, wait_filled(dve, name)[:, 0:width]))

            def gained(name, dst, gains):
                src = wait_filled(dve, name)
                for n, gain in enumerate(gains):
                    last = v.tensor_scalar(dst[:, n * T:(n + 1) * T], src[:, n * T:(n + 1) * T], gain, None,
                                           ALU.mult)
                done(name, last)

            uT_flat = uT[:, :, :].rearrange("p c t -> p (c t)")

            def uT_chunks(c2):
                return uT[:, 2 * c2:2 * c2 + 2, :].rearrange("p c t -> p (c t)")

            def lo_of(name, lo, hi, gains=None):
                in_order(dve, hi_moved, HI_BANKS, name)
                src = in_bank(name)
                if gains is None:
                    last = v.tensor_tensor(rounded(lo), src[:, :], as_f32(hi), ALU.subtract)
                else:
                    for n, gain in enumerate(gains):
                        at = slice(n * T, (n + 1) * T)
                        last = v.scalar_tensor_tensor(rounded(lo[:, at]), src[:, at], gain, as_f32(hi[:, at]),
                                                      ALU.mult, ALU.subtract)
                done(name, last)

            def norm_T(prefix, lo, hi, gain):
                for c2 in range(4):
                    at = slice(c2 * 512, c2 * 512 + 512)
                    lo_of(f"{prefix}T{c2}", lo[:, at], hi[:, at], [column(gain, 2 * c2 + n) for n in range(2)])

            def split_lo(name, halves=range(2)):
                for h in halves:
                    dve.wait_ge(hi_made, 2 * DENSE_BLOCKS.index(name) + h + 1)
                    raw = raw_half(name, h)
                    v.tensor_tensor(rounded(raw), raw, as_f32(hi_half(h)), ALU.subtract).then_inc(split_made, 1)

            def split_in_place(x, hi, signal):
                link(v.tensor_copy(rounded(hi), x))
                v.tensor_tensor(rounded(x), x, as_f32(hi), ALU.subtract).then_inc(signal, 1)

            def tiles(x):
                return x.rearrange("p (t d) -> p t d", t=TT)

            marks_made = [0]

            def mark(signal, by):
                n = marks_made[0]
                marks_made[0] += 1
                v.tensor_copy(marks[:, n:n + 1], ones[:, 0:1]).then_inc(signal, by)

            v.memset(aT, 0.0)
            link(v.memset(chunk_start[:, :], 1.0))
            link(v.memset(chunk_start[:, :].rearrange("p (c t) -> p c t", t=GLA_CHUNK)[:, :, 0:1], 0.0))
            scale_rows("x", h, normed)
            dve.wait_ge(gates_landed, 16 * 2)
            split_in_place(w_gr, w_gr_hi, gates_split)
            wait_drained(dve, "cols")
            v.tensor_scalar(half_bias[:, :], cols[:, COLS["b_merge_2"][0]:COLS["b_merge_2"][0] + 24], 0.5,
                            None, ALU.mult)
            v.tensor_tensor(qk_gain[:, 0:1], column("da_q_norm"), column("da_k_norm"), ALU.mult)
            v.tensor_scalar(qk_gain[:, 1:2], column("da_out_norm"), 1.0 - LAM_INIT, None, ALU.mult)
            q0, k0 = COLS["cross_q_norm"][0], COLS["cross_k_norm"][0]
            link(v.tensor_tensor(qk_gain[:, 2:4], cols[:, q0:q0 + 2], cols[:, k0:k0 + 2], ALU.mult))
            norm_T("x", lo_a, uT_flat, "norm_mix")
            split_lo("gqk")
            dve.wait_ge(consts_made, 6)
            v.tensor_copy(ident_b[:, :], ident[:, :])
            v.tensor_copy(slot_no[:, :], slot_i[:, :])
            v.tensor_copy(expert_no[:, :], expert_i[:, :])
            for n, dst in enumerate((past_m, future_m, chunks_b, causal_b)):
                dve.wait_ge(consts_made, 7 + n)
                v.tensor_copy(dst[:, :], build_m[:, :]).then_inc(masks_cast, 1)
            split_lo("gv")
            dve.wait_ge(lambdas_landed, 16 * 4)
            pr = lam_in[:, :].rearrange("p (q k d) -> p q k d", q=2, k=2)
            link(v.tensor_tensor(pr[:, :, 0, :], pr[:, :, 0, :], pr[:, :, 1, :], ALU.mult))
            v.tensor_reduce(lam_s[:, 0:2], pr[:, :, 0, :], axis=X, op=ALU.add).then_inc(lam_products, 1)

            z = wait_filled(dve, "z")
            for pair in range(2):
                last = v.tensor_scalar(la[:, pair * T:(pair + 1) * T], z[:, pair * T:(pair + 1) * T],
                                       column("gla_gate_b", pair), None, ALU.add)
            done("z", last)
            wait_drained(dve, "z")
            v.scalar_tensor_tensor(k_dec, la, -1.0, la, ALU.mult, ALU.min).then_inc(gla_vec, 1)
            link(v.tensor_scalar(la, la, 0.0, None, ALU.min))
            dve.wait_ge(lam_exps, 1)
            link(v.tensor_tensor(neg_lam[:, :], lam_s[:, 3:4], lam_s[:, 2:3], ALU.subtract))
            link(v.tensor_scalar(neg_lam[:, :], neg_lam[:, :], -LAM_INIT, None, ALU.add))
            dve.wait_ge(gla_act, 1)
            link(v.tensor_tensor(la, la, k_dec, ALU.subtract))
            for pair in range(2):
                at = slice(pair * T, (pair + 1) * T)
                scan = v.tensor_tensor_scan(L[:, at], chunk_start[:, :], la[:, at], 0.0, ALU.mult, ALU.add)
            link(scan)
            Lr = L.rearrange("p (c t) -> p c t", t=GLA_CHUNK)

            def from_L(dst, at, first_is_L):
                ref = Lr[:, :, at:at + 1].broadcast_to([P, 2 * T // GLA_CHUNK, GLA_CHUNK])
                d = dst.rearrange("p (c t) -> p c t", t=GLA_CHUNK)
                pair = (Lr, ref) if first_is_L else (ref, Lr)
                return v.tensor_tensor(d, pair[0], pair[1], ALU.subtract)

            split_lo("dq")
            from_L(la, GLA_CHUNK // 2 - 1, True)
            from_L(k_dec, GLA_CHUNK - 1, False).then_inc(gla_vec, 1)
            scale_rows("mem", tiles(mix), tiles(mix))
            dve.wait_ge(gla_act, 2)
            wait_drained(dve, "gqk1")
            v.tensor_tensor(q_pos, gq, e_pos, ALU.mult)
            v.tensor_tensor(k_neg, gk, la, ALU.mult)
            v.tensor_tensor(q_neg, gq, la, ALU.mult)
            v.tensor_tensor(k_pos, gk, e_pos, ALU.mult)
            v.tensor_tensor(k_dec, gk, k_dec, ALU.mult).then_inc(gla_vec, 1)
            v.tensor_tensor(q_L, gq, q_L, ALU.mult).then_inc(gla_vec, 1)
            for name, at in (("dq", NORM_AT["dq"][1]), ("dk", NORM_AT["dk"][1])):
                split_lo("dk" if name == "dq" else "ck0")
                for t in range(TT):
                    head_sums(f"{name}{t}", mean_sq[:, at + 8 * t:at + 8 * t + 8], 8)
                dve.wait_ge(head_summed, 2 if name == "dq" else 4)
                mean(name, DA_D)
            norm_T("mem", lo_b, memT, "norm_mem")
            wait_rstd(dve, "dk")
            _, lo, hi = NORM_AT["dk"]
            kk = dk_tok.rearrange("p (j d) -> p j d", d=DA_D)
            wait_drained(dve, "dk_1")
            v.tensor_tensor(kk, kk, rstd[:, lo:hi].rearrange("p (j o) -> p j o", o=1)
                            .broadcast_to([P, 16, DA_D]), ALU.mult).then_inc(keys_normed, 1)

            def q_scales(name, at, scale):
                st = stat(rstd, name)
                n = st.shape[1]
                v.tensor_scalar(q_scale[:, 0, at:at + n], st, scale, None, ALU.mult)
                v.tensor_scalar(q_scale[:, 1, at:at + n], st, -scale, None, ALU.mult)\
                    .then_inc(scales_ready, 1)

            q_scales("dq", 0, DA_D ** -0.5)
            dve.wait_ge(scales_ready, 1)
            for t in range(TT):
                for name, m in (("past", past_m), ("fut", future_m)):
                    src = wait_filled(dve, f"{name}{t}")
                    dst = aT[:, t * 512:t * 512 + 512].rearrange("p (h i) -> p h i", h=H1)
                    mask3 = m[:, :].rearrange("p (o i) -> p o i", o=1).broadcast_to([P, H1, P])
                    done(f"{name}{t}", v.copy_predicated(dst, mask3, src[:, :].rearrange("p (h i) -> p h i", h=H1)))
                    wait_drained(dve, f"{name}{t}")
            u01 = wait_filled(dve, "u01")
            u2 = wait_filled(dve, "u2")
            link(v.tensor_copy(states[:, 0:256], u01[:, 0:256]))
            for ch in (1, 2):
                src = (u01[:, 256:512], u2[:, 0:256])[ch - 1]
                for pair in range(2):
                    lo = pair * P
                    last = v.scalar_tensor_tensor(states[:, ch * 256 + lo:ch * 256 + lo + P],
                                                  states[:, (ch - 1) * 256 + lo:(ch - 1) * 256 + lo + P],
                                                  decay[:, pair * 4 + ch:pair * 4 + ch + 1],
                                                  src[:, lo:lo + P], ALU.mult, ALU.add)
                done(("u01", "u2")[ch - 1], last)
                wait_drained(dve, ("u01", "u2")[ch - 1])
            _, lo, hi = NORM_AT["ck"]
            for j in range(2):
                split_lo(("ck1", "cv0")[j])
                for t in range(TT):
                    head_sums(f"ck{2 * j + t}", mean_sq[:, lo + 4 * t + 2 * j:lo + 4 * t + 2 * j + 2], 2)
            dve.wait_ge(head_summed, 8)
            mean("ck", CROSS_D)
            _, glo, _ = NORM_AT["gla"]
            for t in range(TT):
                head_sums(f"og{t}", mean_sq[:, glo + 4 * t:glo + 4 * t + 4], H1)
            dve.wait_ge(head_summed, 10)
            mean("gla", DV)
            wait_rstd(dve, "ck")
            wait_drained(dve, "ck1_1")
            kk = ck_tok.rearrange("p (j d) -> p j d", d=CROSS_D)
            v.tensor_tensor(kk, kk, rstd[:, lo:hi].rearrange("p (j o) -> p j o", o=1)
                            .broadcast_to([P, 8, CROSS_D]), ALU.mult).then_inc(keys_normed, 1)
            for half in range(2):
                gained(f"dqT{half}", dqT[:, half * 512:half * 512 + 512], [qk_gain[:, 0:1]] * 2)
            for j in range(2):
                split_lo(("cv1", "dv")[j])
                for t in range(TT):
                    copy(f"cv{j}_{t}", cv[:, t * D + j * 512:t * D + j * 512 + 512])
            for c2 in (1, 3):
                copy(f"ckT{c2}", ckT[:, c2 * 512:c2 * 512 + 512])
            split_lo("gg")

            def soft_bias(name, parts, out_view, scale_view):
                place = SOFTMAXES.index(name)
                at = place % 2 * 4
                for src, lo, n in parts:
                    last = v.tensor_reduce(maxes[:, at + lo:at + lo + n], src, axis=X, op=ALU.max)
                link(last)
                b, m = out_view(bias[:, at:at + 4]), out_view(maxes[:, at:at + 4])
                if isinstance(scale_view, float):
                    v.tensor_scalar(b, m, scale_view, None, ALU.mult).then_inc(bias_ready, 1)
                else:
                    v.tensor_tensor(b, m, scale_view, ALU.mult).then_inc(bias_ready, 1)

            def soft_inverse(name, n, last_bank):
                at = SOFTMAXES.index(name) % 2 * 4
                wait_drained(dve, last_bank)
                link(v.reciprocal(inv[:, at:at + n], expsum[:, at:at + n]))
                return at

            def d_bias(hh):
                s0 = wait_filled(dve, f"ds0_{hh}")[:, 0:2 * P]
                s1 = wait_filled(dve, f"ds1_{hh}")
                neg = q_scale[:, 1, 0:16].rearrange("p (t j) -> p t j", t=TT)[:, :, 2 * hh:2 * hh + 2]
                soft_bias(f"d{hh}", [(s0.rearrange("p (s k) -> p s k", s=2), 0, 2),
                                     (s1[:, :].rearrange("p (s k) -> p s k", s=2), 2, 2)],
                          lambda x: x.rearrange("p (t s) -> p t s", t=2), neg)

            def d_weights(hh):
                at = soft_inverse(f"d{hh}", 4, f"ds1_{hh}")
                iv = inv[:, at:at + 4].rearrange("p (t s) -> p t s", t=2)
                cf = coef[:, at:at + 4].rearrange("p (t s) -> p t s", t=2)
                link(v.tensor_scalar(cf[:, :, 1], iv[:, :, 1], neg_lam[:, 0:1], None, ALU.mult))
                pr = d_prob[hh % 2]
                for t in range(TT):
                    lo, w = t * P, (t + 1) * P
                    last = v.tensor_scalar(pr[:, lo:lo + w], pr[:, lo:lo + w],
                                           inv[:, at + 2 * t:at + 2 * t + 1], None, ALU.mult)
                link(last)
                for t in range(TT):
                    lo, w = t * P, (t + 1) * P
                    last = v.scalar_tensor_tensor(pr[:, lo:lo + w], pr[:, 384 + lo:384 + lo + w],
                                                  coef[:, at + 2 * t + 1:at + 2 * t + 2], pr[:, lo:lo + w],
                                                  ALU.mult, ALU.add)
                last.then_inc(probs_ready, 1)

            def silu_gate(name, dst):
                n = TANHS.index(name)
                dve.wait_ge(tanh_done, n + 1)
                src = wait_filled(dve, name)
                done(name, v.scalar_tensor_tensor(dst, tanh_b[:, n % 2 * 512:n % 2 * 512 + 512], 1.0,
                                                  src[:, :], ALU.add, ALU.mult))

            d_bias(0)
            d_bias(1)
            d_weights(0)
            d_weights(1)
            d_bias(2)
            for t in range(TT):
                silu_gate(f"gg_{t}", gg[:, t * 512:t * 512 + 512])
            wait_drained(dve, "gg_1")
            wait_rstd(dve, "gla")
            wait_drained(dve, "og1")
            mg3 = tiles(mix)[:, :, 512:1024]
            for t in range(TT):
                m4 = mix[:, t * D + 512:(t + 1) * D].rearrange("p (h d) -> p h d", h=H1)
                st = rstd[:, glo + 4 * t:glo + 4 * t + 4].rearrange("p (h o) -> p h o", o=1)
                last = v.tensor_tensor(m4, m4, st.broadcast_to([P, H1, DV]), ALU.mult)
            link(last)
            v.scalar_tensor_tensor(mg3, mg3, 0.5, gg.rearrange("p (t d) -> p t d", t=TT), ALU.mult, ALU.mult)\
                .then_inc(mix_ready, 1)
            d_bias(3)
            d_weights(2)
            d_weights(3)
            split_lo("wo0")
            wait_drained(dve, "do3")
            mean("da", DV)
            wait_rstd(dve, "da")
            _, lo, _ = NORM_AT["da"]
            for t in range(TT):
                m4 = mix[:, t * D:t * D + 512].rearrange("p (h d) -> p h d", h=H1)
                st = rstd[:, lo + 4 * t:lo + 4 * t + 4].rearrange("p (h o) -> p h o", o=1)
                last = v.tensor_tensor(m4, m4, st.broadcast_to([P, H1, DV]), ALU.mult)
            last.then_inc(mix_ready, 1)
            for c2 in range(4):
                at = slice(c2 * 512, c2 * 512 + 512)
                lo_of(f"mixT{c2}", lo_b[:, at], mixT[:, at], [(qk_gain[:, 1:2], column("gla_out_norm"))[c2 // 2]] * 2)
            split_lo("wo1")

            def add_to_h(prefix, scale=None, following=(None, None)):
                for j in range(2):
                    if following[j]:
                        split_lo(following[j], [0] if j else range(2))
                    for t in range(TT):
                        name = f"{prefix}{j}_{t}"
                        src = wait_filled(dve, name)
                        hs = h[:, t, j * 512:(j + 1) * 512]
                        if scale:
                            done(name, v.scalar_tensor_tensor(hs, src[:, :], scale, hs, ALU.mult, ALU.add))
                        else:
                            done(name, v.tensor_tensor(hs, src[:, :], hs, ALU.add))
                for j in range(2):
                    for t in range(TT):
                        wait_drained(dve, f"{prefix}{j}_{t}")

            add_to_h("wo", following=(None, "cq0"))
            scale_rows("h1", h, normed)
            split_lo("cq0", [1])
            norm_T("h1", lo_a, uT_flat, "norm_cross")
            scale_rows("mem2", tiles(mem2_tok), tiles(mem2_tok))
            _, lo, _ = NORM_AT["cq"]
            for j in range(2):
                split_lo(("cq1", "xk2")[j], range(2 - j))
                for t in range(TT):
                    head_sums(f"cq{2 * j + t}", mean_sq[:, lo + 4 * t + 2 * j:lo + 4 * t + 2 * j + 2], 2)
            dve.wait_ge(head_summed, 14)
            mean("cq", CROSS_D)
            split_lo("xk2", [1])
            wait_rstd(dve, "cq")
            q_scales("cq", 16, CROSS_D ** -0.5)
            dve.wait_ge(scales_ready, 2)
            for c2 in (1, 3):
                gained(f"cqT{c2}", cqT[:, c2 * 512:c2 * 512 + 512], [qk_gain[:, 2 + n:3 + n] for n in range(2)])

            norm_T("mem2", lo_b, mem2T, "g_mem_2")

            def pair_bias(kind, n, scale_view):
                t, hp = n % 2, n // 2
                src = wait_filled(dve, f"{kind}s{t}_{hp}")
                soft_bias(f"{kind}{n}", [(src[:, :].rearrange("p (h k) -> p h k", h=2), 0, 2)],
                          lambda x: x[:, 0:2], scale_view)

            def pair_weights(kind, n, buffers):
                at = soft_inverse(f"{kind}{n}", 2, f"{kind}s{n % 2}_{n // 2}")
                for i in range(2):
                    pr = buffers[n][:, i * T:(i + 1) * T]
                    last = v.tensor_scalar(pr, pr, inv[:, at + i:at + i + 1], None, ALU.mult)
                last.then_inc(probs_ready, 1)

            def four(bias_, weights_):
                bias_(0)
                bias_(1)
                weights_(0)
                bias_(2)
                weights_(1)
                bias_(3)
                weights_(2)
                weights_(3)

            def c_neg(n):
                at = 16 + n % 2 * 4 + n // 2 * 2
                return q_scale[:, 1, at:at + 2]

            four(lambda n: pair_bias("c", n, c_neg(n)), lambda n: pair_weights("c", n, c_prob))
            split_lo("co0")
            for hh in range(4):
                at = slice(hh * 512, hh * 512 + 512)
                lo_of(f"co_{hh}", lo_a[:, at], coT[:, at])
            add_to_h("co", following=("co1", "xv2"))

            dve.wait_ge(params_landed, 16 * N_PARAMS)
            in_order(dve, row_squared, ROW_NORMS, "h2")
            mean("h2", D)
            wait_rstd(dve, "h2")
            _, lo, _ = NORM_AT["h2"]
            for t in range(TT):
                v.scalar_tensor_tensor(normed[:, t, :], h[:, t, :], rstd[:, lo + t:lo + t + 1],
                                       wide_gain[:, :], ALU.mult, ALU.mult).then_inc(normed_ready, 1)
            split_lo("xv2", [1])
            for c2 in (1, 3):
                copy(f"h2T{c2}", uT_chunks(c2))

            NG, NE = N_GROUPS, N_EXPERTS
            lg_b = wait_filled(dve, "logits")[:, 0:TT * (NG + NE)].rearrange("p (t e) -> p t e", t=TT)
            rc = Carver(rt, 0, 512)

            def small(w):
                return rc.take(TT * w).rearrange("p (t e) -> p t e", t=TT)

            def wide(x, w):
                return x.broadcast_to([P, TT, w])

            def all_tiles(x):
                return x.rearrange("p (o e) -> p o e", o=1).broadcast_to([P, TT, x.shape[1]])

            lg = small(NG + NE)
            done("logits", v.tensor_tensor(lg, lg_b, all_tiles(b_router[:, :]), ALU.add))
            wait_drained(dve, "logits")

            def one_hot_max(values, numbers, w, out_max, out_hot, tmp):
                link(v.tensor_reduce(out_max, values, axis=X, op=ALU.max))
                link(v.tensor_tensor(tmp, values, wide(out_max, w), ALU.is_lt))
                link(v.scalar_tensor_tensor(tmp, tmp, 1000.0, all_tiles(numbers), ALU.mult, ALU.add))
                link(v.tensor_reduce(first, tmp, axis=X, op=ALU.min))
                link(v.tensor_tensor(out_hot, all_tiles(numbers), wide(first, w), ALU.is_equal))

            first = small(1)
            g_max, g_hot, g_tmp = small(1), small(NG), small(NG)
            one_hot_max(lg[:, :, 0:NG], expert_no[:, 0:NG], NG, g_max, g_hot, g_tmp)
            e_val, e_tmp = small(NE), small(NE)
            hot1, hot2 = small(NE), small(NE)
            for t in range(TT):
                gh = g_hot[:, t, :].rearrange("p (g o) -> p g o", o=1).broadcast_to([P, NG, PER_GROUP])
                ev = e_val[:, t, :].rearrange("p (g e) -> p g e", g=NG)
                et = e_tmp[:, t, :].rearrange("p (g e) -> p g e", g=NG)
                v.tensor_scalar(et, gh, BIG, -BIG, ALU.mult, ALU.add)
                last = v.tensor_tensor(ev, lg[:, t, NG:].rearrange("p (g e) -> p g e", g=NG), gh, ALU.mult)
            link(last)
            link(v.tensor_tensor(e_val, e_val, e_tmp, ALU.add))
            m1, m2 = small(1), small(1)
            one_hot_max(e_val, expert_no[:, :], NE, m1, hot1, e_tmp)
            link(v.scalar_tensor_tensor(e_val, hot1, -3.0 * BIG, e_val, ALU.mult, ALU.add))
            one_hot_max(e_val, expert_no[:, :], NE, m2, hot2, e_tmp)
            v.tensor_tensor(rt_exp[:, :, 0:NG], lg[:, :, 0:NG], wide(g_max, NG), ALU.subtract)
            link(v.tensor_tensor(rt_exp[:, :, NG:NG + 1], m2, m1, ALU.subtract))
            v.tensor_tensor(assigned[:, :, :], hot1, hot2, ALU.add).then_inc(router_step, 1)
            for t in range(TT):
                copy(f"xv2_{t}", xv2[:, t * 512:t * 512 + 512])
            dve.wait_ge(router_exp, 1)
            g_sum, w_sum = small(1), small(1)
            v.tensor_reduce(g_sum, rt_exp[:, :, 0:NG], axis=X, op=ALU.add)
            link(v.tensor_scalar(w_sum, rt_exp[:, :, NG:NG + 1], 1.0, None, ALU.add))
            link(v.tensor_tensor(g_sum, g_sum, w_sum, ALU.mult))
            link(v.reciprocal(g_sum, g_sum))
            link(v.tensor_tensor(w_sum, g_sum, rt_exp[:, :, NG:NG + 1], ALU.mult))
            v.tensor_tensor(hot1, hot1, wide(g_sum, NE), ALU.mult)
            link(v.tensor_tensor(hot2, hot2, wide(w_sum, NE), ALU.mult))
            link(v.tensor_tensor(gates[:, :, :], hot1, hot2, ALU.add))
            rk = wait_filled(dve, "rank")
            link(v.scalar_tensor_tensor(rank1[:, :, :], rk[:, 0:TT * NE].rearrange("p (t e) -> p t e", t=TT),
                                        1.0, assigned[:, :, :], ALU.add, ALU.mult))
            link(v.tensor_reduce(most[:, :], rk[:, TT * NE:(TT + 1) * NE], axis=X, op=ALU.max))
            done("rank", v.tensor_scalar(over_flag[:, :], most[:, :], float(CAP), None, ALU.is_gt))
            wait_drained(dve, "rank")
            mark(router_step, 1)

            rank_flat = rank1[:, :, :].rearrange("p t e -> p (t e)")
            gate_flat = gates[:, :, :].rearrange("p t e -> p (t e)")

            def select_slots(S, i):
                for t in range(TT):
                    for e in range(2):
                        lo = (2 * t + e) * CAP
                        col = bass.ds(i * 2 + (t * N_EXPERTS + e), 1)
                        last = v.tensor_scalar(select[:, lo:lo + CAP], slot_no[:, :], rank_flat[:, col], None,
                                               ALU.is_equal)
                last.then_inc(S.select_ready, 1)

            def select_gates(S, i):
                for t in range(TT):
                    for e in range(2):
                        lo = (2 * t + e) * CAP
                        col = bass.ds(i * 2 + (t * N_EXPERTS + e), 1)
                        last = v.tensor_scalar(select_g[:, lo:lo + CAP], slot_no[:, :], rank_flat[:, col],
                                               gate_flat[:, col], ALU.is_equal, ALU.mult)
                last.then_inc(S.gates_ready, 1)

            def hidden(S, n):
                dve.wait_ge(S.tanh_ready, n + 1)
                v.scalar_tensor_tensor(half_h, tanh_g, 1.0, bank[2][:, :], ALU.add, ALU.mult)\
                    .then_inc(S.half_ready, 1)
                dve.wait_ge(S.half_ready, n + 1)
                dve.wait_ge(S.hidden_psum, n * 2 + 2)
                v.scalar_tensor_tensor(hid, half_h, 0.5, bank[3][:, :], ALU.mult, ALU.mult)\
                    .then_inc(S.hidden_ready, 1)

            def gathered_high(S, n):
                dve.wait_ge(S.gathered, n + 1)
                v.tensor_copy(xgT[:, 512:1024], bank[1][:, :]).then_inc(S.hi_drained, 1)

            def add_outputs(S, n):
                for t in range(TT):
                    for half in range(2):
                        dve.wait_ge(S.scattered, n * 4 + (2 * t + half + 1))
                        b = bank[(6, 2)[t] + half]
                        hs = h[:, t, half * 512:half * 512 + 512]
                        v.tensor_tensor(hs, b[:, :], hs, ALU.add).then_inc(S.added, 1)

            select_slots(main_s, 0)
            select_gates(main_s, 0)
            mark(main_s.added, 4)
            gathered_high(main_s, 0)
            with dve.Fori(0, PAIRS - 1) as i:
                dve.wait_ge(main_s.gathered, i + 1)
                select_slots(main_s, i + 1)
                dve.wait_ge(main_s.gate_psum, i + 1)
                select_gates(main_s, i + 1)
                hidden(main_s, i)
                gathered_high(main_s, i + 1)
                add_outputs(main_s, i)
            hidden(main_s, PAIRS - 1)
            add_outputs(main_s, PAIRS - 1)
            over = dve.value_load(over_flag[0:1, 0:1], min_val=0, max_val=1)
            with dve.If(over):
                mark(more_s.added, 4)
                with dve.Fori(0, MORE_ROUNDS) as r:
                    with dve.Fori(0, PAIRS) as i:
                        n = r * PAIRS + i
                        pair_ranks = rank1[:, :, bass.ds(i * 2, 2)]
                        v.tensor_scalar(pair_ranks, pair_ranks, -float(CAP), None, ALU.add)\
                            .then_inc(more_s.ranks_shifted, 1)
                        dve.wait_ge(more_s.ranks_shifted, n + 1)
                        select_slots(more_s, i)
                        select_gates(more_s, i)
                        gathered_high(more_s, n)
                        hidden(more_s, n)
                        add_outputs(more_s, n)
            mark(after_experts, 1)
            dve.wait_ge(main_s.added, 4 * PAIRS + 4)

            scale_rows("h3", h, normed)
            split_lo("iq", [0])
            norm_T("h3", lo_a, uT_flat, "g_in_2")
            split_lo("iq", [1])

            def rope_heads(src, dst, t, heads):
                s3 = src.rearrange("p (h d) -> p h d", d=HD)
                d3 = dst.rearrange("p (h d) -> p h d", d=HD)
                t3 = rope_t[:, 0:heads * HD].rearrange("p (h d) -> p h d", d=HD)
                half = HD // 2

                def table(lo, w):
                    return rope[:, t, lo:lo + w].rearrange("p (o d) -> p o d", o=1)\
                        .broadcast_to([P, heads, w])
                v.tensor_tensor(d3, s3, table(0, HD), ALU.mult)
                v.tensor_tensor(t3[:, :, 0:half], s3[:, :, half:HD], table(HD, half), ALU.mult)
                last = v.tensor_tensor(t3[:, :, half:HD], s3[:, :, 0:half], table(HD + half, half), ALU.mult)
                return last, lambda: v.tensor_tensor(d3, d3, t3, ALU.add)

            def rope_tensor(name, dst):
                for t in range(TT):
                    src = wait_filled(dve, f"{name}_{t}")
                    last, finish = rope_heads(src[:, :], dst[:, t * 512:t * 512 + 512], t, H2)
                    done(f"{name}_{t}", last)
                    wait_drained(dve, f"{name}_{t}")
                    if t == 0:
                        link(finish())
                    else:
                        finish().then_inc(roped, 1)
                        in_order(dve, roped, ROPED, name)

            split_lo("dq2")
            rope_tensor("iq", iq_tok)
            src = wait_filled(dve, "ikw")
            for t in range(TT):
                lo = t * (HD + H2)
                v.tensor_scalar(iw[:, t, :], src[:, lo + HD:lo + HD + H2], H2 ** -0.5, None, ALU.mult)
                last, finish = rope_heads(src[:, lo:lo + HD], ik_tok[:, t * P:t * P + HD], t, 1)
                if t:
                    done("ikw", last)
                    wait_drained(dve, "ikw")
                else:
                    link(last)
                link(finish())
            ik3 = ik_tok.rearrange("p (t two d) -> p t two d", t=TT, two=2)
            v.tensor_copy(ik3[:, :, 1, :], ik3[:, :, 0, :]).then_inc(roped, 1)
            split_lo("dk2")
            rope_tensor("dq2", dq2_tok)
            split_lo("dv2")
            rope_tensor("dk2", dk2_tok)
            split_lo("mq")

            def score_bank(name):
                n = RELUS.index(name)
                t, part = int(name[2]), int(name[4])
                w = (t + 1) * P
                heads = 512 // w
                wait_drained(dve, name)
                dst = score[:, t * P:t * P + w]
                for i in range(heads):
                    hh = part * heads + i
                    lo = n % 2 * 512 + i * w
                    wcol = iw[:, t, hh:hh + 1]
                    if hh == 0:
                        link(v.tensor_scalar(dst, relu[:, lo:lo + w], wcol, None, ALU.mult))
                    else:
                        ins = v.scalar_tensor_tensor(dst, relu[:, lo:lo + w], wcol, dst, ALU.mult, ALU.add)
                        if i == heads - 1:
                            ins.then_inc(scored, 1)
                            dve.wait_ge(scored, n + 1)
                        else:
                            link(ins)

            score_bank("il0_0")
            score_bank("il0_1")
            split_lo("mk")
            rope_tensor("mq", mq_tok)
            for name in RELUS[2:]:
                if name == "il1_2":
                    split_lo("mv")
                score_bank(name)
            rope_tensor("mk", mk_tok)
            split_lo("mg")

            def pick_keys(t):
                w = (t + 1) * P
                sc = score[:, t * P:t * P + w]
                wk = work[:, 0:w]
                link(v.tensor_tensor(sc[:, t * P:w], sc[:, t * P:w], causal_b[:, :], ALU.add))
                for step in range(DSA_TOPK // 8):
                    src = wk if step else sc
                    link(v.max(out=best8, in_=src))
                    link(v.match_replace(out=wk, in_to_replace=best8, in_values=src, imm_value=-3e38))
                link(v.tensor_tensor(wk, wk, sc, ALU.is_equal))
                dst = sel_b[:, t * P:t * P + w]
                if t:
                    v.tensor_scalar(dst[:, 0:P], wk[:, 0:P], NEG, None, ALU.mult)
                v.scalar_tensor_tensor(dst[:, t * P:w], wk[:, t * P:w], NEG, causal_b[:, :], ALU.mult,
                                       ALU.add).then_inc(selected, 1)
                dve.wait_ge(selected, t + 1)

            def head_bias(kind, pair):
                s0 = wait_filled(dve, f"{kind}s0_{pair}")[:, 0:2 * P]
                s1 = wait_filled(dve, f"{kind}s1_{pair}")
                soft_bias(f"{kind}{pair}", [(s0.rearrange("p (h k) -> p h k", h=2), 0, 2),
                                            (s1[:, :].rearrange("p (h k) -> p h k", h=2), 2, 2)],
                          lambda x: x, -(HD ** -0.5))

            def head_weights(kind, pair):
                at = soft_inverse(f"{kind}{pair}", 4, f"{kind}s1_{pair}")
                for n in range(2):
                    for t in range(TT):
                        lo, w = n * 384 + t * P, (t + 1) * P
                        pr = probs[:, lo:lo + w]
                        last = v.tensor_scalar(pr, pr, inv[:, at + 2 * t + n:at + 2 * t + n + 1], None,
                                               ALU.mult)
                last.then_inc(probs_ready, 1)

            def gated_out(name, dst, hi, gate):
                src = wait_filled(dve, name)
                done(name, v.scalar_tensor_tensor(dst, src[:, 0:T], 0.5, gate, ALU.mult, ALU.mult))
                wait_drained(dve, name)
                split_in_place(dst, hi, y_split)

            for t in range(TT):
                pick_keys(t)
            gate_of = {"mg": mgate, "dg": dgate, "xg": xgate}
            heads_of = {"m": (ya, ya_hi, mgate), "s": (yb, yb_hi, dgate)}

            def finish_pair(kind, pair):
                y, hi, gate = heads_of[kind]
                at = slice(pair * T, (pair + 1) * T)
                gated_out(f"{kind}o{pair}", y[:, at], hi[:, at], gate[:, at])

            for kind in "ms":
                head_bias(kind, 0)
                head_weights(kind, 0)
                for pair in range(4):
                    if pair < 3:
                        head_bias(kind, pair + 1)
                    for b in attention_fillers(kind)[pair]:
                        following = DENSE_BLOCKS[DENSE_BLOCKS.index(b) + 1]
                        split_lo(following, [0])
                        if pair < 3:
                            head_weights(kind, pair + 1)
                        split_lo(following, [1])
                        if b in gate_of:
                            for half in range(2):
                                silu_gate(f"{b}_{half}", gate_of[b][:, half * 512:half * 512 + 512])
                            wait_drained(dve, f"{b}_1")
                    finish_pair(kind, pair)
            four(lambda n: pair_bias("x", n, -(X2_D ** -0.5)), lambda n: pair_weights("x", n, x_prob))
            split_lo("gl5")
            for hh in range(4):
                if hh == 2:
                    split_lo("up0")
                at = slice(hh * T, (hh + 1) * T)
                gated_out(f"xo_{hh}", yc[:, at], yc_hi[:, at], xgate[:, at])

            for b in range(3):
                for c in range(4):
                    if c % 2 == 0:
                        split_lo(("up1", "up2", "out0")[b], [c // 2])
                    name = f"up{b}_{c}"
                    src = wait_filled(dve, name)
                    chunk = b * KC + 2 * c
                    gate = branch_gate[:, chunk * T:(chunk + 2) * T]
                    if b == 0:
                        if c == 0:
                            wait_drained(dve, "gl5_1")
                        done(name, v.scalar_tensor_tensor(uT_chunks(c), gate, 1.0, src[:, :], ALU.add,
                                                          ALU.mult))
                    else:
                        done(name, v.scalar_tensor_tensor(up_t, gate, 1.0, src[:, :], ALU.add, ALU.mult))
                        wait_drained(dve, name)
                        link(v.tensor_tensor(uT_chunks(c), uT_chunks(c), up_t, ALU.add))
                    if b == 2:
                        split_in_place(uT_chunks(c), lo_a[:, c * 512:c * 512 + 512], merged)
            add_to_h("out", 0.5, ("out1", None))
            in_order(dve, row_squared, ROW_NORMS, "final")
            mean("final", D)
            wait_rstd(dve, "final")
            dve.wait_ge(final_gain_landed, 16)
            _, lo, _ = NORM_AT["final"]
            for t in range(TT):
                v.scalar_tensor_tensor(normed[:, t, :], h[:, t, :], rstd[:, lo + t:lo + t + 1],
                                       wide_gain[:, :], ALU.mult, ALU.mult).then_inc(out_ready, 1)

        @block.tensor
        def _(pe):
            mm = nc.tensor.matmul
            then_upper = chain(pe, rows_switched)
            pe.wait_ge(consts_made, 6)
            pe.wait_ge(rows_landed, 16)

            def transpose(dst, src):
                k = src.shape[0]
                return nc.tensor.transpose(dst, src, ident[0:k, 0:k])

            def as_chunks(x):
                return x.rearrange("p (c t) -> p c t", t=T)

            def as_tiles(x):
                return x.rearrange("p (t d) -> p t d", t=TT)

            def turn(names, src):
                for c2, name in enumerate(names):
                    b = wait_free(name)
                    for c in range(2):
                        for t in range(TT):
                            last = transpose(b[:, c * T + t * P:c * T + t * P + P],
                                             src[:, t, (2 * c2 + c) * P:(2 * c2 + c + 1) * P])
                    full(name, last)

            def turn_normed(prefix, src):
                pe.wait_ge(normed_ready, 2 * ROW_NORMS.index(prefix) + 2)
                turn([f"{prefix}T{c}" for c in range(4)], src)

            def wait_turned(prefix, n=4):
                for c in range(n):
                    wait_drained(pe, f"{prefix}{c}")

            def parts(hi, lo):
                return as_chunks(rounded(hi)), as_chunks(rounded(lo))

            def dense(name, x, uses, weights_stand, before_half=None):
                n = DENSE_BLOCKS.index(name)
                chunks = SOURCE[name].shape[1] // 2
                banks = [wait_free(use) for use in uses]
                for h in range(2):
                    if before_half:
                        before_half(h)
                    pe.wait_ge(split_made, 2 * n + h + 1)
                    w = [rounded(y).rearrange("p (k n) -> p k n", k=chunks)
                         for y in (hi_half(h), raw_half(name, h))]
                    for i, use in enumerate(uses):
                        for c in range(2 if weights_stand else 1):
                            for k in range(chunks):
                                if weights_stand:
                                    dst, chunk = banks[i][:, c * T:(c + 1) * T], 2 * i + c
                                    left = [y[:, k, chunk * P:(chunk + 1) * P] for y in w]
                                    right = [y[:, h * chunks + k, :] for y in x]
                                else:
                                    dst = banks[i][:, :]
                                    left = [y[:, h * chunks + k, i * P:(i + 1) * P] for y in x]
                                    right = [y[:, k, :] for y in w]
                                first, last_one = h + c + k == 0, h == 1 and k == chunks - 1
                                mm(dst, left[0], right[0], start=first, stop=False, skip_group_check=True)
                                mm(dst, left[0], right[1], start=False, stop=False, skip_group_check=True)
                                last = mm(dst, left[1], right[0], start=False, stop=last_one,
                                          skip_group_check=True)
                        if h == 1:
                            full(use, last)
                    if h == 0:
                        last.then_inc(half_used, 1)

            def moving(name, x, before_half=None):
                dense(name, x, [f"{name}_{t}" for t in range(TT)], False, before_half)

            def standing(name, x, uses=None, before_half=None):
                dense(name, x, uses or [f"{name}_{half}" for half in range(2)], True, before_half)

            uT_flat = uT[:, :, :].rearrange("p c t -> p (c t)")
            stream = parts(uT_flat, lo_a)

            b = wait_free("cols")
            full("cols", transpose(b[:, 0:N_COLS], rows[0:N_COLS, :]))
            turn_normed("x", normed)
            wait_turned("xT")
            pe.wait_ge(gates_landed, 16 * 2)
            b = wait_free("grT")
            w_hi, w_lo = (rounded(w).rearrange("p (k n) -> p k n", k=KC) for w in (w_gr_hi, w_gr))
            x_hi, x_lo = stream
            pe.wait_ge(gates_split, 1)
            for k in range(KC):
                for part, (w, x) in enumerate(((w_hi, x_hi), (w_hi, x_lo), (w_lo, x_hi))):
                    last = mm(b[0:16, 0:T], w[:, k, :], x[:, k, :], start=k + part == 0,
                              stop=k == KC - 1 and part == 2)
            full("grT", last)
            standing("gqk", stream, ["gqk0", "gqk1"])
            wait_drained(pe, "grT")
            b = wait_free("z")
            for pair in range(2):
                last = mm(b[:, pair * T:(pair + 1) * T], gate_w[:, pair * P:(pair + 1) * P], grT[:, :],
                          start=True, stop=True)
            full("z", last)
            moving("gv", stream)
            moving("dq", stream)
            moving("dk", stream)
            turn_normed("mem", as_tiles(mix))
            gp, gn = as_chunks(q_pos), as_chunks(q_neg)
            kp, kn = as_chunks(k_pos), as_chunks(k_neg)
            pe.wait_ge(gla_vec, 4)
            b = wait_free("kdT")
            for t in range(TT):
                for pair in range(2):
                    lo = (2 * t + pair) * P
                    last = transpose(b[:, lo:lo + P], as_chunks(k_dec)[:, pair, t * P:(t + 1) * P])
            full("kdT", last)
            for t in range(TT):
                at = slice(t * P, (t + 1) * P)
                for name, k_, q_ in ((f"past{t}", kn, gp), (f"fut{t}", kp, gn)):
                    b = wait_free(name)
                    for hh in (0, 2, 1, 3):
                        on = slice(DA_D * (hh % 2), DA_D * (hh % 2) + DA_D)
                        last = mm(b[:, hh * P:(hh + 1) * P], k_[on, hh // 2, at], q_[on, hh // 2, at],
                                  start=True, stop=True)
                        if hh == 2:
                            then_upper(last)
                    full(name, last)
            wait_drained(pe, "kdT")
            for t in range(TT):
                wait_drained(pe, f"gv_{t}")
            kd4 = k_decT.rearrange("p (t r d) -> p t r d", t=TT, r=2)
            gv3 = as_tiles(gv)
            for name, chunks in (("u01", (0, 1)), ("u2", (2,))):
                b = wait_free(name)
                for ch in chunks:
                    on = slice(GLA_CHUNK * (ch % 2), GLA_CHUNK * (ch % 2) + GLA_CHUNK)
                    for hh in range(H1):
                        o = DA_D * (hh % 2)
                        lo = (ch % 2) * 256 * (name == "u01") + hh // 2 * P
                        last = mm(b[o:o + DA_D, lo:lo + P], kd4[on, ch // 2, hh // 2, o:o + DA_D],
                                  gv3[on, ch // 2, hh * DV:(hh + 1) * DV], start=True, stop=True)
                    if ch == 0:
                        then_upper(last)
                full(name, last)
            wait_turned("memT")
            memT3 = parts(memT, lo_b)
            moving("ck0", memT3)
            moving("ck1", memT3)
            for t in range(TT):
                wait_drained(pe, f"fut{t}")
            wait_drained(pe, "u2")
            st4 = states.rearrange("p (c r d) -> p c r d", c=3, r=2)
            qL = as_chunks(q_L)
            for t in range(TT):
                b = wait_free(f"og{t}")
                for hh in range(H1):
                    out_at = slice(hh * DV, (hh + 1) * DV)
                    mm(b[:, out_at], aT[:, t * 512 + hh * P:t * 512 + hh * P + P], gv3[:, t, out_at],
                       start=hh == 0, stop=True, skip_group_check=True)
                for hh in (0, 2, 1, 3):
                    out_at = slice(hh * DV, (hh + 1) * DV)
                    on = slice(DA_D * (hh % 2), DA_D * (hh % 2) + DA_D)
                    for half in range(2):
                        ch = 2 * t + half
                        if ch:
                            o = GLA_CHUNK * half
                            last = mm(b[o:o + GLA_CHUNK, out_at],
                                      qL[on, hh // 2, ch * GLA_CHUNK:(ch + 1) * GLA_CHUNK],
                                      st4[on, ch - 1, hh // 2, :], start=False, stop=True,
                                      skip_group_check=True)
                    if hh == 2:
                        then_upper(last)
                full(f"og{t}", last)
            pe.wait_ge(keys_normed, 1)
            wait_drained(pe, "dq_1")
            turn(["dqT0", "dqT1"], as_tiles(dq_tok))
            turn(["dkT0", "dkT1"], as_tiles(dk_tok))
            moving("cv0", memT3)
            moving("cv1", memT3)
            pe.wait_ge(keys_normed, 2)
            turn([f"ckT{c}" for c in range(4)], as_tiles(ck_tok))
            moving("dv", stream)
            wait_turned("dqT", 2)
            wait_turned("dkT", 2)
            q4, k4 = as_chunks(dqT), as_chunks(dkT)
            dv3 = as_tiles(dv)

            def mask_add(dst, m):
                return mm(dst, ident_b[:, :], m, start=False, stop=True, skip_group_check=True)

            def d_scores0(hh):
                b = wait_free(f"ds0_{hh}")
                for s in range(2):
                    on = slice(DA_D * s, DA_D * s + DA_D)
                    last = mm(b[:, s * P:(s + 1) * P], q4[on, hh, 0:P], k4[on, hh, 0:P], start=s == 0, stop=True,
                              skip_group_check=True)
                    if s == 0:
                        then_upper(last)
                for s in range(2):
                    last = mask_add(b[:, s * P:(s + 1) * P], chunks_b[:, :])
                full(f"ds0_{hh}", last)

            def d_scores1(hh):
                b = wait_free(f"ds1_{hh}")
                for s in range(2):
                    on = slice(DA_D * s, DA_D * s + DA_D)
                    last = mm(b[:, s * T:(s + 1) * T], q4[on, hh, P:T], k4[on, hh, :], start=s == 0, stop=True,
                              skip_group_check=True)
                    if s == 0:
                        then_upper(last)
                for s in range(2):
                    last = mask_add(b[:, s * T + P:(s + 1) * T], chunks_b[:, :])
                full(f"ds1_{hh}", last)

            def three_blocks(name, pr):
                b = wait_free(name)
                for n in range(3):
                    last = transpose(b[:, n * P:(n + 1) * P], pr[:, n * P:(n + 1) * P])
                full(name, last)

            def d_out(hh):
                in_order(pe, probs_ready, SOFTMAXES, f"d{hh}")
                three_blocks(f"dpT{hh}", d_prob[hh % 2])
                wait_drained(pe, f"dpT{hh}")
                b = wait_free(f"do{hh}")
                at = slice(hh * DV, (hh + 1) * DV)
                mm(b[:, 0:P], d_pT[:, 0:P], dv3[:, 0, at], start=True, stop=True)
                mm(b[:, P:2 * P], d_pT[:, P:2 * P], dv3[:, 0, at], start=True, stop=False)
                full(f"do{hh}", mm(b[:, P:2 * P], d_pT[:, 2 * P:3 * P], dv3[:, 1, at], start=False, stop=True))

            pe.wait_ge(masks_cast, 4)
            for hh in (0, 1):
                d_scores0(hh)
                d_scores1(hh)
            moving("gg", stream)
            d_scores0(2)
            d_scores1(2)
            for t in range(TT):
                wait_drained(pe, f"dv_{t}")
            d_out(0)
            d_scores0(3)
            d_scores1(3)
            for hh in (1, 2, 3):
                d_out(hh)
            pe.wait_ge(mix_ready, 2)
            turn([f"mixT{c}" for c in range(4)], as_tiles(mix))
            wait_turned("mixT")
            moving("wo0", parts(mixT, lo_b))
            moving("wo1", parts(mixT, lo_b))
            turn_normed("h1", normed)
            wait_turned("h1T")
            moving("cq0", stream)
            moving("cq1", stream)
            wait_drained(pe, "cq0_1")
            wait_drained(pe, "cq1_1")
            turn([f"cqT{c}" for c in range(4)], as_tiles(cq_tok))
            turn_normed("mem2", as_tiles(mem2_tok))
            wait_turned("cqT")
            wait_turned("ckT")
            cq3, ck3, cv3 = as_chunks(cqT), as_chunks(ckT), as_tiles(cv)
            for hp in range(2):
                for t in range(TT):
                    b = wait_free(f"cs{t}_{hp}")
                    for n in range(2):
                        for k in range(2):
                            c = 2 * (2 * hp + n) + k
                            last = mm(b[:, n * T:(n + 1) * T], cq3[:, c, t * P:(t + 1) * P], ck3[:, c, :],
                                      start=k == 0, stop=k == 1)
                    full(f"cs{t}_{hp}", last)
            wait_turned("mem2T")
            standing("xk2", parts(mem2T, lo_b))

            def four_blocks(name, buffers, hh):
                b = wait_free(name)
                for kt in range(TT):
                    for t in range(TT):
                        lo = hh % 2 * T + kt * P
                        last = transpose(b[:, kt * T + t * P:kt * T + t * P + P],
                                         buffers[t + hh // 2 * 2][:, lo:lo + P])
                full(name, last)

            def c_turn(hh):
                in_order(pe, probs_ready, SOFTMAXES, f"c{hh // 2 * 2 + 1}")
                four_blocks(f"cpT{hh}", c_prob, hh)

            c_turn(0)
            for hh in range(H1):
                if hh + 1 < H1:
                    c_turn(hh + 1)
                b = wait_free(f"co_{hh}")
                wait_drained(pe, f"cpT{hh}")
                for c in range(2):
                    for kt in range(TT):
                        lo = hh * CROSS_D + c * P
                        last = mm(b[:, c * T:(c + 1) * T], cv3[:, kt, lo:lo + P],
                                  c_pT[hh % 2][:, kt * T:(kt + 1) * T], start=kt == 0, stop=kt == 1)
                full(f"co_{hh}", last)
            for hh in range(H1):
                wait_drained(pe, f"co_{hh}")
            moving("co0", parts(coT, lo_a))
            moving("co1", parts(coT, lo_a))
            turn_normed("h2", normed)
            wait_turned("h2T")
            pe.wait_ge(params_landed, 16 * N_PARAMS)
            b = wait_free("logits")
            NE = N_EXPERTS
            w = N_GROUPS + NE
            for t in range(TT):
                for k in range(KC):
                    last = mm(b[:, t * w:(t + 1) * w], uT[:, k, t * P:(t + 1) * P], w_router[:, k, :],
                              start=k == 0, stop=k == KC - 1)
            full("logits", last)
            moving("xv2", parts(mem2T, lo_b))
            pe.wait_ge(router_step, 1)
            b = wait_free("rank")
            mm(b[:, 0:NE], earlier[:, :], assigned[:, 0, :], start=True, stop=True)
            mm(b[:, NE:2 * NE], ones[:, :], assigned[:, 0, :], start=True, stop=False)
            mm(b[:, NE:2 * NE], earlier[:, :], assigned[:, 1, :], start=False, stop=True)
            mm(b[:, 2 * NE:3 * NE], ones[:, :], assigned[:, 0, :], start=True, stop=False)
            full("rank", mm(b[:, 2 * NE:3 * NE], ones[:, :], assigned[:, 1, :], start=False, stop=True))
            for name in PSUM_PLAN[FIRST_USES - 8:FIRST_USES]:
                wait_drained(pe, name)

            sel3, selg3 = as_tiles(select), as_tiles(select_g)
            xg3 = xgT.rearrange("p (k s) -> p k s", k=KC)
            hidT3 = hidT.rearrange("p (c s) -> p c s", c=FC)

            def gather(S, n):
                pe.wait_ge(S.select_ready, n + 1)
                for k in range(KC):
                    dst = bank[k // 4][:, k % 4 * P:k % 4 * P + P]
                    for t in range(TT):
                        last = mm(dst, normed[:, t, k * P:(k + 1) * P], sel3[:, t, :], start=t == 0,
                                  stop=t == TT - 1)
                last.then_inc(S.gathered, 1)

            def experts(S, n, expert_landed):
                pe.wait_ge(S.gates_ready, n + 1)
                pe.wait_ge(S.y_ready, n + 1)
                for t in range(TT):
                    last = transpose(bank[4][:, t * P:(t + 1) * P], selg3[:, t, :])
                last.then_inc(S.gate_psum, 1)
                pe.wait_ge(S.lo_drained, n + 1)
                pe.wait_ge(S.hi_drained, n + 1)
                for part in range(2):
                    pe.wait_ge(S.added, n * 4 + (3 + part))
                    first_slot = (4, 0)[part]
                    expert_landed(first_slot)
                    expert_landed(first_slot + 1)
                    for k in range(KC):
                        for e in range(2):
                            on = slice(e * CAP, (e + 1) * CAP)
                            last = mm(bank[2 + part][on, :], xg3[:, k, on], slot(first_slot + e)[:, k, :],
                                      start=k == 0, stop=k == KC - 1)
                    last.then_inc(S.hidden_psum, 1)
                pe.wait_ge(S.hidden_ready, n + 1)
                for c in range(FC):
                    last = transpose(bank[0][:, c * P:(c + 1) * P], hid[:, c * P:(c + 1) * P])
                last.then_inc(S.hidden_turned, 1)
                pe.wait_ge(S.gate_ready, n + 1)
                pe.wait_ge(S.hidT_ready, n + 1)
                expert_landed(2)
                expert_landed(3)
                for half in range(2):
                    for c in range(FC):
                        for e in range(2):
                            on = slice(e * CAP, (e + 1) * CAP)
                            last = mm(bank[4 + half][on, :], hidT3[:, c, on],
                                      slot(2 + e, FC)[:, c, half * 512:half * 512 + 512],
                                      start=c == 0, stop=c == FC - 1)
                    last.then_inc(S.down_done, 1)

            def scatter(S, n):
                pe.wait_ge(S.y_ready, n + 2)
                for t in range(TT):
                    for half in range(2):
                        mm(bank[(6, 2)[t] + half][:, :], gate_mat[:, t * P:(t + 1) * P],
                           y_slots[:, half * 512:half * 512 + 512], start=True, stop=True)\
                            .then_inc(S.scattered, 1)

            def main_landed(i):
                def wait(j):
                    pe.wait_ge(landed[j], i * 16 + 16)
                return wait

            gather(main_s, 0)
            with pe.Fori(0, PAIRS - 1) as i:
                experts(main_s, i, main_landed(i))
                gather(main_s, i + 1)
                scatter(main_s, i)
            experts(main_s, PAIRS - 1, main_landed(PAIRS - 1))
            scatter(main_s, PAIRS - 1)
            pe.wait_ge(main_s.added, 4 * PAIRS + 4)
            pe.wait_ge(router_step, 2)
            over = pe.value_load(over_flag[0:1, 0:1], min_val=0, max_val=1)
            with pe.If(over):
                with pe.Fori(0, MORE_ROUNDS * PAIRS) as n:
                    gather(more_s, n)
                    experts(more_s, n, lambda j: pe.wait_ge(more_s.weights, n * 96 + 96))
                    scatter(more_s, n)
                pe.wait_ge(more_s.added, 4 * MORE_ROUNDS * PAIRS + 4)

            turn_normed("h3", normed)
            wait_turned("h3T")
            moving("iq", stream)
            b = wait_free("ikw")
            for t in range(TT):
                w = HD + H2
                for part, x in enumerate((as_chunks(as_f32(uT_flat)), as_chunks(as_f32(lo_a)))):
                    for k in range(KC):
                        last = mm(b[:, t * w:(t + 1) * w], x[:, k, t * P:(t + 1) * P], w_ikw[:, k, :],
                                  start=part + k == 0, stop=part == 1 and k == KC - 1)
            full("ikw", last)
            moving("dq2", stream)
            moving("dk2", stream)
            in_order(pe, roped, ROPED, "ik")
            turn(["iqT0", "iqT1"], as_tiles(iq_tok))
            b = wait_free("ikT")
            for t in range(TT):
                last = transpose(b[:, t * P:(t + 1) * P], ik_tok[:, t * P:(t + 1) * P])
            full("ikT", last)
            moving("dv2", stream)
            wait_turned("iqT", 2)
            wait_drained(pe, "ikT")
            iq3 = as_chunks(iqT)

            def index_scores(name):
                t, part = int(name[2]), int(name[4])
                w = (t + 1) * P
                heads = 512 // w
                b = wait_free(name)
                for i in [*range(0, heads, 2), *range(1, heads, 2)]:
                    hh = part * heads + i
                    on = slice(HD * (hh % 2), HD * (hh % 2) + HD)
                    last = mm(b[:, i * w:(i + 1) * w], iq3[on, hh // 2, t * P:(t + 1) * P], ikT[on, 0:w],
                              start=True, stop=True)
                    if i == heads - 2:
                        then_upper(last)
                full(name, last)

            index_scores("il0_0")
            index_scores("il0_1")
            moving("mq", stream)
            index_scores("il1_0")
            index_scores("il1_1")
            moving("mk", stream)
            index_scores("il1_2")
            index_scores("il1_3")
            moving("mv", stream)
            in_order(pe, roped, ROPED, "dk2")
            turn(["dqT2_0", "dqT2_1"], as_tiles(dq2_tok))
            turn(["dkT2_0", "dkT2_1"], as_tiles(dk2_tok))
            in_order(pe, roped, ROPED, "mk")
            turn(["mqT0", "mqT1"], as_tiles(mq_tok))
            turn(["mkT0", "mkT1"], as_tiles(mk_tok))

            def attention(kind, qT, kT, v3):
                q3, k3 = as_chunks(qT), as_chunks(kT)

                def scores0(pair):
                    b = wait_free(f"{kind}s0_{pair}")
                    for n in range(2):
                        on = slice(HD * n, HD * n + HD)
                        last = mm(b[:, n * P:(n + 1) * P], q3[on, pair, 0:P], k3[on, pair, 0:P],
                                  start=n == 0, stop=True, skip_group_check=True)
                        if n == 0:
                            then_upper(last)
                    for n in range(2):
                        last = mask_add(b[:, n * P:(n + 1) * P],
                                        causal_b[:, :] if kind == "m" else sel_b[:, 0:P])
                    full(f"{kind}s0_{pair}", last)

                def scores1(pair):
                    b = wait_free(f"{kind}s1_{pair}")
                    for n in range(2):
                        on = slice(HD * n, HD * n + HD)
                        last = mm(b[:, n * T:(n + 1) * T], q3[on, pair, P:T], k3[on, pair, :],
                                  start=n == 0, stop=True, skip_group_check=True)
                        if n == 0:
                            then_upper(last)
                    for n in range(2):
                        if kind == "m":
                            last = mask_add(b[:, n * T + P:(n + 1) * T], causal_b[:, :])
                        else:
                            last = mask_add(b[:, n * T:(n + 1) * T], sel_b[:, P:P + T])
                    full(f"{kind}s1_{pair}", last)

                scores0(0)
                scores1(0)
                for pair in range(4):
                    if pair < 3:
                        scores0(pair + 1)
                        scores1(pair + 1)

                    def turn_probs(h):
                        if h == 1:
                            in_order(pe, probs_ready, SOFTMAXES, f"{kind}{pair}")
                            for n in range(2):
                                three_blocks(f"{kind}pT{2 * pair + n}", probs[:, n * 384:n * 384 + 384])

                    for b in attention_fillers(kind)[pair]:
                        standing(b, stream, before_half=turn_probs)
                    b = wait_free(f"{kind}o{pair}")
                    for n in range(2):
                        wait_drained(pe, f"{kind}pT{2 * pair + n}")
                        o, lo, pT = HD * n, (2 * pair + n) * HD, n * 384
                        mm(b[o:o + HD, 0:T], v3[:, 0, lo:lo + HD], probT[:, pT:pT + T], start=True, stop=False)
                        last = mm(b[o:o + HD, P:T], v3[:, 1, lo:lo + HD], probT[:, pT + T:pT + T + P],
                                  start=False, stop=True)
                    full(f"{kind}o{pair}", last)

            for c in range(2):
                wait_drained(pe, f"mqT{c}")
                wait_drained(pe, f"mkT{c}")
            wait_drained(pe, "mv_1")
            attention("m", mqT, mkT, as_tiles(mv))
            for c in range(2):
                wait_drained(pe, f"dqT2_{c}")
                wait_drained(pe, f"dkT2_{c}")
            wait_drained(pe, "dv2_1")
            pe.wait_ge(selected, 2)
            attention("s", dq2T, dk2T, as_tiles(dv2))

            xq3, xk3, xv3 = as_chunks(xqT), as_chunks(xkT), as_tiles(xv2)
            for c in range(2):
                wait_drained(pe, f"xq_{c}")
                wait_drained(pe, f"xk2_{c}")
                wait_drained(pe, f"xv2_{c}")
            for hp in range(2):
                for t in range(TT):
                    b = wait_free(f"xs{t}_{hp}")
                    for n in range(2):
                        last = mm(b[:, n * T:(n + 1) * T], xq3[:, 2 * hp + n, t * P:(t + 1) * P],
                                  xk3[:, 2 * hp + n, :], start=True, stop=True)
                    full(f"xs{t}_{hp}", last)
            for hp, b in enumerate(("gl4", "gl5")):
                def turn_probs(h):
                    if h == 1:
                        in_order(pe, probs_ready, SOFTMAXES, f"x{2 * hp + 1}")
                        for hh in (2 * hp, 2 * hp + 1):
                            four_blocks(f"xpT{hh}", x_prob, hh)

                standing(b, stream, before_half=turn_probs)
                for hh in (2 * hp, 2 * hp + 1):
                    wait_drained(pe, f"xpT{hh}")
                    b = wait_free(f"xo_{hh}")
                    for kt in range(TT):
                        last = mm(b[:, 0:T], xv3[:, kt, hh * P:(hh + 1) * P],
                                  x_pT[hh % 2][:, kt * T:(kt + 1) * T], start=kt == 0, stop=kt == 1)
                    full(f"xo_{hh}", last)

            for n, (y, hi) in enumerate(((ya, ya_hi), (yb, yb_hi), (yc, yc_hi))):
                pe.wait_ge(y_split, 4 * (n + 1))
                dense(f"up{n}", parts(hi, y), [f"up{n}_{c2}" for c2 in range(4)], True)
            merged_parts = parts(lo_a, uT_flat)
            moving("out0", merged_parts, lambda h: pe.wait_ge(merged, 2 * h + 2))
            moving("out1", merged_parts)


NAMES = ["x", "mem", "norm_mix", "w_in", "da_q_norm", "da_k_norm", "lambda_q1", "lambda_k1", "lambda_q2",
         "lambda_k2", "da_out_norm", "gla_gate_w", "gla_gate_b", "gla_out_norm", "w_o", "norm_cross",
         "norm_mem", "w_cq", "w_ckv", "cross_q_norm", "cross_k_norm", "w_co", "norm_ffn", "w_group",
         "b_group", "w_expert", "b_expert", "w_e_gate", "w_e_up", "w_e_down", "mem_2", "g_in_2", "w_in_2",
         "b_merge_2", "g_mem_2", "w_mem_kv_2", "w_up_moba_2", "w_up_dsa_2", "w_up_cross_2", "w_out_2",
         "g_final_2"]


def rope_table():

    half = HD // 2
    inv = np.power(np.float32(10000.0), -np.arange(half, dtype=np.float32) * np.float32(2.0) / np.float32(HD))
    angle = np.arange(T, dtype=np.float32)[:, None] * inv[None, :].astype(np.float32)
    cos, sin = np.cos(angle), np.sin(angle)
    return np.concatenate([cos, cos, -sin, sin], axis=1).astype(np.float32)


def gain_rows(inputs):
    rows = []
    for name, (_, n) in COLS.items():
        vector = np.asarray(inputs[name]).reshape(-1)
        rows.append(np.concatenate([vector] * (n * P // vector.size)).reshape(n, P))
    return np.concatenate(rows)


def kernel(**inputs):
    import concourse.bacc as bacc
    from concourse.bass_utils import run_bass_kernel_spmd

    nc = bacc.Bacc("TRN2", target_bir_lowering=False, num_devices=1)
    arrays, aps = {}, {}
    for name in NAMES + ["rope", "rows"]:
        if name in COLS:
            continue
        made = {"rope": rope_table, "rows": lambda: gain_rows(inputs)}
        a = made[name]() if name in made else np.ascontiguousarray(inputs[name])
        if a.ndim == 1:
            a = a.reshape(1, -1)
        arrays[f"in_{name}"] = a
        aps[name] = nc.dram_tensor(f"in_{name}", a.shape, mybir.dt.from_np(a.dtype), kind="ExternalInput").ap()
    out = nc.dram_tensor("out_x", (1, T, D), F32, kind="ExternalOutput").ap()
    build(nc, aps, out)
    r = run_bass_kernel_spmd(nc, [arrays], core_ids=[0])
    return r.results[0]["out_x"]
```
